# Optimizing a Trainium2 kernel written in Bass

```python
import functools
import jax, jax.numpy as jnp
from jax import lax
import numpy as np

D_MODEL = 1024
BATCH = 1
SEQ = 512
DEPTH = 2
DEC_BATCH = 8
DEC_SEQ = 4
PAST_LEN = 4096
PAGE_SIZE = 128

N_EVEN = (DEPTH + 1) // 2
N_ODD = DEPTH // 2
ALPHA = (2 * DEPTH) ** 0.25
BETA = (8 * DEPTH) ** -0.25
LN_EPS = 1e-5
A_HEADS = 8
A_HD = 64
A_W = A_HEADS * A_HD
LORA_W = 64
LORA_A = 64
LORA_G = 128
RWKV_SIZES = (A_W, A_W, A_W, LORA_W, LORA_A, LORA_G)
RWKV_COLS = sum(RWKV_SIZES)
GN_EPS = 64e-5
B_HEADS = 8
QK_NOPE = 64
QK_ROPE = 32
V_HD = 64
Q_LORA = 384
KV_LORA = 256
MLA_SIZES = (Q_LORA, KV_LORA, QK_ROPE)
MLA_COLS = sum(MLA_SIZES)
IN_E = RWKV_COLS + MLA_COLS
MIX_E = A_W + B_HEADS * V_HD
SM_SCALE = (QK_NOPE + QK_ROPE) ** -0.5
ROPE_BASE = 10000.0
Q_BLOCK = 128
C_HEADS = 8
C_DK = 64
C_DV = 128
MIX_O = C_HEADS * C_DV
MLSTM_SIZES = (C_HEADS * C_DK, C_HEADS * C_DK, MIX_O, MIX_O, C_HEADS, C_HEADS)
IN_O = sum(MLSTM_SIZES)
MLSTM_CHUNK = 64
GATE_CAP = 15.0
N_KEYS = 128
N_EXPERTS = N_KEYS * N_KEYS
PEER_HEADS = 8
PEER_QDIM = 256
PEER_TOPK = 16
PEER_BLOCK = 128

kernel_name = 'rwkv7_mla_mlstm_peer_deepnorm_step'

def split_last(x, sizes):
    idx = [int(s) for s in np.cumsum(sizes)[:-1]]
    return jnp.split(x, idx, axis=-1)

def layer_norm(x, g, b, eps=LN_EPS):
    x32 = x.astype(jnp.float32)
    mu = x32.mean(-1, keepdims=True)
    var = jnp.square(x32 - mu).mean(-1, keepdims=True)
    return ((x32 - mu) * lax.rsqrt(var + eps) * g.astype(jnp.float32) + b.astype(jnp.float32)).astype(x.dtype)

def rms_norm(x, g, eps=1e-6):
    x32 = x.astype(jnp.float32)
    return (x32 * lax.rsqrt(jnp.mean(x32 * x32, -1, keepdims=True) + eps) * g.astype(jnp.float32)).astype(x.dtype)

def soft_cap(x):
    return GATE_CAP * jnp.tanh(x / GATE_CAP)

def rope_tables(pos):
    inv = ROPE_BASE ** (-jnp.arange(0, QK_ROPE, 2, dtype=jnp.float32) / QK_ROPE)
    ang = pos.astype(jnp.float32)[:, None] * inv[None, :]
    return jnp.cos(ang), jnp.sin(ang)

def apply_rope(x, cos, sin):
    x1, x2 = jnp.split(x.astype(jnp.float32), 2, axis=-1)
    return jnp.concatenate([x1 * cos - x2 * sin, x1 * sin + x2 * cos], -1).astype(x.dtype)

def wkv7_scan(r, w, k, v, kk, a, s0):
    def step(s, inp):
        r_t, w_t, k_t, v_t, kk_t, a_t = inp
        sa = jnp.einsum('bhij,bhj->bhi', s, -kk_t)
        s = (s * w_t[:, :, None, :] + sa[..., None] * (kk_t * a_t)[:, :, None, :]
             + v_t[..., None] * k_t[:, :, None, :])
        return s, jnp.einsum('bhij,bhj->bhi', s, r_t)
    xs = tuple(jnp.moveaxis(t, 1, 0) for t in (r, w, k, v, kk, a))
    s_final, y = lax.scan(step, s0, xs)
    return jnp.moveaxis(y, 0, 1), s_final

def mla_attend_prompt(q_lat, q_pe, c, kpe):
    bsz, t_len, n_h, n_c = q_lat.shape
    nb = t_len // Q_BLOCK
    k_pos = jnp.arange(t_len)

    def blk(args):
        ql, qp, i = args
        s = (jnp.einsum('bqhc,bkc->bhqk', ql, c) + jnp.einsum('bqhr,bkr->bhqk', qp, kpe)).astype(jnp.float32) * SM_SCALE
        q_pos = i * Q_BLOCK + jnp.arange(Q_BLOCK)
        s = jnp.where(k_pos[None, :] <= q_pos[:, None], s, -jnp.inf)
        p = jax.nn.softmax(s, axis=-1).astype(c.dtype)
        return jnp.einsum('bhqk,bkc->bqhc', p, c)

    qb = lambda t: jnp.moveaxis(t.reshape(bsz, nb, Q_BLOCK, *t.shape[2:]), 1, 0)
    o = lax.map(blk, (qb(q_lat), qb(q_pe), jnp.arange(nb)))
    return jnp.moveaxis(o, 0, 1).reshape(bsz, t_len, n_h, n_c)

def mla_attend_paged(q_lat, q_pe, c, kpe, ckv_pool, kpe_pool, page_table):
    s_new_len = q_lat.shape[1]
    causal = jnp.tril(jnp.ones((s_new_len, s_new_len), bool))

    def one(args):
        pt, ql, qp, cn, kn = args
        cp = ckv_pool[pt].reshape(-1, KV_LORA)
        kp = kpe_pool[pt].reshape(-1, QK_ROPE)
        s_past = (jnp.einsum('qhc,kc->hqk', ql, cp) + jnp.einsum('qhr,kr->hqk', qp, kp)).astype(jnp.float32) * SM_SCALE
        s_new = (jnp.einsum('qhc,kc->hqk', ql, cn) + jnp.einsum('qhr,kr->hqk', qp, kn)).astype(jnp.float32) * SM_SCALE
        s_new = jnp.where(causal, s_new, -jnp.inf)
        p = jax.nn.softmax(jnp.concatenate([s_past, s_new], -1), axis=-1).astype(cp.dtype)
        n_past = cp.shape[0]
        return (jnp.einsum('hqk,kc->qhc', p[..., :n_past], cp)
                + jnp.einsum('hqk,kc->qhc', p[..., n_past:], cn))

    return lax.map(one, (page_table, q_lat, q_pe, c, kpe))

def rwkv_mla_mixer(x, x_prev, wkv0, pos, attend, w_in, mu, w0, w2, a0, a2, g2, k_k, k_a, r_k,
                   lnx_w, lnx_b, q_norm, w_uq, kv_norm, w_uk, w_uv, w_out):
    f32 = jnp.float32
    bsz, t_len, _ = x.shape
    heads = lambda t: t.reshape(bsz, t_len, A_HEADS, A_HD)
    proj = x @ w_in
    p_rw, p_mla = proj[..., :RWKV_COLS], proj[..., RWKV_COLS:]
    prev = jnp.concatenate([(x_prev @ w_in[:, :RWKV_COLS])[:, None], p_rw[:, :-1]], axis=1)
    p_rw = p_rw + (prev - p_rw) * mu
    r, k, v, lw, la, lg = split_last(p_rw, RWKV_SIZES)
    w_log = -jax.nn.softplus(-(w0 + jnp.tanh(lw) @ w2).astype(f32)) - 0.5
    decay = heads(jnp.exp(-jnp.exp(w_log)))
    a = heads(jax.nn.sigmoid((a0 + la @ a2).astype(f32)))
    g = jax.nn.sigmoid(lg) @ g2
    r, k, v = heads(r.astype(f32)), heads(k.astype(f32)), heads(v.astype(f32))
    kk = k * k_k.reshape(A_HEADS, A_HD).astype(f32)
    kk = kk / jnp.maximum(jnp.linalg.norm(kk, axis=-1, keepdims=True), 1e-12)
    k = k * (1.0 + (a - 1.0) * k_a.reshape(A_HEADS, A_HD).astype(f32))
    y, wkv_new = wkv7_scan(r, decay, k, v, kk, a, wkv0.astype(f32))
    y_mu = y.mean(-1, keepdims=True)
    y_var = jnp.square(y - y_mu).mean(-1, keepdims=True)
    y = ((y - y_mu) * lax.rsqrt(y_var + GN_EPS) * lnx_w.reshape(A_HEADS, A_HD).astype(f32)
         + lnx_b.reshape(A_HEADS, A_HD).astype(f32))
    y = y + jnp.sum(r * k * r_k.astype(f32), axis=-1, keepdims=True) * v
    out_a = (y.reshape(bsz, t_len, A_W) * g).astype(x.dtype)
    cq, ckv, kpe = split_last(p_mla, MLA_SIZES)
    q = (rms_norm(cq, q_norm) @ w_uq).reshape(bsz, t_len, B_HEADS, QK_NOPE + QK_ROPE)
    q_nope, q_pe = q[..., :QK_NOPE], q[..., QK_NOPE:]
    cos, sin = rope_tables(pos)
    q_pe = apply_rope(q_pe, cos[:, None], sin[:, None])
    c = rms_norm(ckv, kv_norm)
    kpe = apply_rope(kpe, cos, sin)
    q_lat = jnp.einsum('bthn,chn->bthc', q_nope, w_uk)
    o_lat = attend(q_lat, q_pe, c, kpe)
    out_b = jnp.einsum('bthc,chv->bthv', o_lat, w_uv).reshape(bsz, t_len, B_HEADS * V_HD)
    out = jnp.concatenate([out_a, out_b], axis=-1) @ w_out
    return out, c, kpe, x[:, -1], wkv_new.astype(x.dtype)

def mlstm_chunkwise(q, k, v, ig, lf, c0, n0, m0, chunk):
    f32 = jnp.float32
    bsz, t_len, n_h, _ = q.shape
    nc = t_len // chunk

    def to_chunks(t):
        t = t.astype(f32).reshape(bsz, nc, chunk, n_h, *t.shape[3:])
        return jnp.moveaxis(jnp.moveaxis(t, 1, 0), 3, 2)

    causal = jnp.tril(jnp.ones((chunk, chunk), bool))

    def step(carry, inp):
        c, n, m = carry
        qc, kc, vc, ic, fc = inp
        b = jnp.cumsum(fc, axis=-1)
        d = jnp.where(causal, b[..., :, None] - b[..., None, :] + ic[..., None, :], -jnp.inf)
        g = b + m[..., None]
        mt = jnp.maximum(g, d.max(-1))
        w_inter = jnp.exp(g - mt)
        att = jnp.exp(d - mt[..., None]) * jnp.einsum('bhtd,bhjd->bhtj', qc, kc)
        num = w_inter[..., None] * jnp.einsum('bhvd,bhtd->bhtv', c, qc) + jnp.einsum('bhtj,bhjv->bhtv', att, vc)
        den = w_inter * jnp.einsum('bhd,bhtd->bht', n, qc) + att.sum(-1)
        h = num / jnp.maximum(jnp.abs(den), jnp.exp(-mt))[..., None]
        m_new = mt[..., -1]
        w_state = jnp.exp(b[..., -1:] - b + ic - m_new[..., None])
        dec = jnp.exp(b[..., -1] + m - m_new)
        c = dec[..., None, None] * c + jnp.einsum('bhj,bhjv,bhjd->bhvd', w_state, vc, kc)
        n = dec[..., None] * n + jnp.einsum('bhj,bhjd->bhd', w_state, kc)
        return (c, n, m_new), h

    (c, n, m), h = lax.scan(step, (c0.astype(f32), n0.astype(f32), m0.astype(f32)),
                            tuple(to_chunks(t) for t in (q, k, v, ig, lf)))
    h = jnp.moveaxis(jnp.moveaxis(h, 2, 3), 0, 1).reshape(bsz, t_len, n_h, -1)
    return h, c, n, m

def mlstm_mixer(x, c0, n0, m0, w_in, b_i, b_f, mh_norm, w_out):
    f32 = jnp.float32
    bsz, t_len, _ = x.shape
    q, k, v, o, i_pre, f_pre = split_last(x @ w_in, MLSTM_SIZES)
    q = q.reshape(bsz, t_len, C_HEADS, C_DK) * (C_DK ** -0.5)
    k = k.reshape(bsz, t_len, C_HEADS, C_DK)
    v = v.reshape(bsz, t_len, C_HEADS, C_DV)
    ig = soft_cap((i_pre + b_i).astype(f32))
    lf = jax.nn.log_sigmoid(soft_cap((f_pre + b_f).astype(f32)))
    chunk = MLSTM_CHUNK if t_len % MLSTM_CHUNK == 0 else t_len
    h, c_new, n_new, m_new = mlstm_chunkwise(q, k, v, ig, lf, c0, n0, m0, chunk)
    h = rms_norm(h.astype(x.dtype), mh_norm.reshape(C_HEADS, C_DV)).reshape(bsz, t_len, MIX_O)
    out = (h * jax.nn.sigmoid(o)) @ w_out
    return out, c_new.astype(x.dtype), n_new.astype(x.dtype), m_new.astype(x.dtype)

def peer(x, wq, k1, k2, u_tab, v_tab):
    shp = x.shape
    xt = x.reshape(-1, D_MODEL)
    n_tok = xt.shape[0]
    nb = -(-n_tok // PEER_BLOCK)
    xt = jnp.pad(xt, ((0, nb * PEER_BLOCK - n_tok), (0, 0))).reshape(nb, PEER_BLOCK, D_MODEL)
    half = PEER_QDIM // 2

    def blk(xb):
        q = (xb @ wq).reshape(PEER_BLOCK, PEER_HEADS, PEER_QDIM).astype(jnp.float32)
        s1 = jnp.einsum('bhd,nd->bhn', q[..., :half], k1.astype(jnp.float32))
        s2 = jnp.einsum('bhd,nd->bhn', q[..., half:], k2.astype(jnp.float32))
        t1, i1 = lax.top_k(s1, PEER_TOPK)
        t2, i2 = lax.top_k(s2, PEER_TOPK)
        cand = (t1[..., :, None] + t2[..., None, :]).reshape(PEER_BLOCK, PEER_HEADS, PEER_TOPK * PEER_TOPK)
        cidx = (i1[..., :, None] * N_KEYS + i2[..., None, :]).reshape(PEER_BLOCK, PEER_HEADS, PEER_TOPK * PEER_TOPK)
        top, sel = lax.top_k(cand, PEER_TOPK)
        idx = jnp.take_along_axis(cidx, sel, axis=-1)
        gate = jax.nn.softmax(top, axis=-1).astype(xb.dtype)
        act = jax.nn.gelu(jnp.einsum('bd,bhkd->bhk', xb, u_tab[idx]), approximate=False) * gate
        return jnp.einsum('bhk,bhkd->bd', act, v_tab[idx])

    y = lax.map(blk, xt).reshape(-1, D_MODEL)[:n_tok]
    return y.reshape(shp)

def setup_inputs(seed: int = 0) -> dict:
    key = jax.random.key(seed)
    ks = iter(jax.random.split(key, 64))
    f32 = jnp.float32

    def nrm(shape, scale=1.0):
        return jax.random.normal(next(ks), shape, f32) * scale

    def gain(shape):
        return 1.0 + nrm(shape, 0.02)

    n_pages = PAST_LEN // PAGE_SIZE
    n_used = DEC_BATCH * n_pages
    n_pool = n_used + max(1, n_used // 4)
    page_table = jax.random.permutation(next(ks), n_pool)[:n_used].reshape(DEC_BATCH, n_pages).astype(jnp.int32)
    d_in = D_MODEL ** -0.5
    return {
        'x_prompt': nrm((BATCH, SEQ, D_MODEL)),
        'x_sample': nrm((DEC_BATCH, DEC_SEQ, D_MODEL)),
        'cache_ckv': nrm((N_EVEN, n_pool, PAGE_SIZE, KV_LORA)),
        'cache_kpe': nrm((N_EVEN, n_pool, PAGE_SIZE, QK_ROPE)),
        'page_table': page_table,
        'state_shift': nrm((N_EVEN, DEC_BATCH, D_MODEL)),
        'state_wkv': nrm((N_EVEN, DEC_BATCH, A_HEADS, A_HD, A_HD), 0.3),
        'state_mlstm_c': nrm((N_ODD, DEC_BATCH, C_HEADS, C_DV, C_DK), 0.3),
        'state_mlstm_n': nrm((N_ODD, DEC_BATCH, C_HEADS, C_DK), 0.3),
        'state_mlstm_m': nrm((N_ODD, DEC_BATCH, C_HEADS), 0.5),
        'w_in_e': nrm((N_EVEN, D_MODEL, IN_E), d_in),
        'mu_e': jax.random.uniform(next(ks), (N_EVEN, RWKV_COLS), f32),
        'w0_e': jax.random.uniform(next(ks), (N_EVEN, A_W), f32, -6.0, 1.0),
        'w2_e': nrm((N_EVEN, LORA_W, A_W), 0.1 * LORA_W ** -0.5),
        'a0_e': nrm((N_EVEN, A_W), 0.5),
        'a2_e': nrm((N_EVEN, LORA_A, A_W), 0.5 * LORA_A ** -0.5),
        'g2_e': nrm((N_EVEN, LORA_G, A_W), LORA_G ** -0.5),
        'kk_e': 0.85 + nrm((N_EVEN, A_W), 0.05),
        'ka_e': 1.0 + nrm((N_EVEN, A_W), 0.05),
        'rk_e': nrm((N_EVEN, A_HEADS, A_HD), 0.1),
        'lnx_w_e': gain((N_EVEN, A_W)),
        'lnx_b_e': nrm((N_EVEN, A_W), 0.02),
        'q_norm_e': gain((N_EVEN, Q_LORA)),
        'w_uq_e': nrm((N_EVEN, Q_LORA, B_HEADS * (QK_NOPE + QK_ROPE)), Q_LORA ** -0.5),
        'kv_norm_e': gain((N_EVEN, KV_LORA)),
        'w_uk_e': nrm((N_EVEN, KV_LORA, B_HEADS, QK_NOPE), KV_LORA ** -0.5),
        'w_uv_e': nrm((N_EVEN, KV_LORA, B_HEADS, V_HD), KV_LORA ** -0.5),
        'w_out_e': nrm((N_EVEN, MIX_E, D_MODEL), BETA * MIX_E ** -0.5),
        'w_in_o': nrm((N_ODD, D_MODEL, IN_O), d_in),
        'b_i_o': nrm((N_ODD, C_HEADS), 0.5),
        'b_f_o': jnp.linspace(3.0, 6.0, C_HEADS, dtype=f32) + nrm((N_ODD, C_HEADS), 0.1),
        'mh_norm_o': gain((N_ODD, MIX_O)),
        'w_out_o': nrm((N_ODD, MIX_O, D_MODEL), BETA * MIX_O ** -0.5),
        'peer_wq': nrm((DEPTH, D_MODEL, PEER_HEADS * PEER_QDIM), d_in),
        'peer_k1': nrm((DEPTH, N_KEYS, PEER_QDIM // 2), (PEER_QDIM // 2) ** -0.5),
        'peer_k2': nrm((DEPTH, N_KEYS, PEER_QDIM // 2), (PEER_QDIM // 2) ** -0.5),
        'peer_u': nrm((DEPTH, N_EXPERTS, D_MODEL), d_in),
        'peer_v': nrm((DEPTH, N_EXPERTS, D_MODEL), BETA * 0.5),
        'ln1_g': gain((DEPTH, D_MODEL)),
        'ln1_b': nrm((DEPTH, D_MODEL), 0.02),
        'ln2_g': gain((DEPTH, D_MODEL)),
        'ln2_b': nrm((DEPTH, D_MODEL), 0.02),
    }

def reference(x_prompt, x_sample, cache_ckv, cache_kpe, page_table, state_shift, state_wkv,
              state_mlstm_c, state_mlstm_n, state_mlstm_m,
              w_in_e, mu_e, w0_e, w2_e, a0_e, a2_e, g2_e, kk_e, ka_e, rk_e, lnx_w_e, lnx_b_e,
              q_norm_e, w_uq_e, kv_norm_e, w_uk_e, w_uv_e, w_out_e,
              w_in_o, b_i_o, b_f_o, mh_norm_o, w_out_o,
              peer_wq, peer_k1, peer_k2, peer_u, peer_v,
              ln1_g, ln1_b, ln2_g, ln2_b):
    xp, xs = x_prompt, x_sample
    bp = xp.shape[0]
    past_len = page_table.shape[1] * PAGE_SIZE
    pos_p = jnp.arange(xp.shape[1])
    pos_s = past_len + jnp.arange(xs.shape[1])
    ckv_p, kpe_p, ckv_s, kpe_s, sh_p, sh_s, wkv_p, wkv_s = ([] for _ in range(8))
    mc_p, mc_s, mn_p, mn_s, mm_p, mm_s = ([] for _ in range(6))
    for l in range(DEPTH):
        if l % 2 == 0:
            e = l // 2
            wts = (w_in_e[e], mu_e[e], w0_e[e], w2_e[e], a0_e[e], a2_e[e], g2_e[e], kk_e[e], ka_e[e],
                   rk_e[e], lnx_w_e[e], lnx_b_e[e], q_norm_e[e], w_uq_e[e], kv_norm_e[e], w_uk_e[e],
                   w_uv_e[e], w_out_e[e])
            hp, c1, k1, last1, s1 = rwkv_mla_mixer(
                xp, jnp.zeros((bp, D_MODEL), xp.dtype), jnp.zeros((bp, A_HEADS, A_HD, A_HD), xp.dtype),
                pos_p, mla_attend_prompt, *wts)
            attend_s = functools.partial(mla_attend_paged, ckv_pool=cache_ckv[e], kpe_pool=cache_kpe[e],
                                         page_table=page_table)
            hs, c2, k2, last2, s2 = rwkv_mla_mixer(xs, state_shift[e], state_wkv[e], pos_s, attend_s, *wts)
            ckv_p.append(c1); kpe_p.append(k1); ckv_s.append(c2); kpe_s.append(k2)
            sh_p.append(last1); sh_s.append(last2); wkv_p.append(s1); wkv_s.append(s2)
        else:
            od = l // 2
            wts = (w_in_o[od], b_i_o[od], b_f_o[od], mh_norm_o[od], w_out_o[od])
            hp, cp1, np1, mp1 = mlstm_mixer(
                xp, jnp.zeros((bp, C_HEADS, C_DV, C_DK), xp.dtype), jnp.zeros((bp, C_HEADS, C_DK), xp.dtype),
                jnp.zeros((bp, C_HEADS), xp.dtype), *wts)
            hs, cs1, ns1, ms1 = mlstm_mixer(xs, state_mlstm_c[od], state_mlstm_n[od], state_mlstm_m[od], *wts)
            mc_p.append(cp1); mn_p.append(np1); mm_p.append(mp1)
            mc_s.append(cs1); mn_s.append(ns1); mm_s.append(ms1)
        xp = layer_norm(ALPHA * xp + hp, ln1_g[l], ln1_b[l])
        xs = layer_norm(ALPHA * xs + hs, ln1_g[l], ln1_b[l])
        pw = (peer_wq[l], peer_k1[l], peer_k2[l], peer_u[l], peer_v[l])
        xp = layer_norm(ALPHA * xp + peer(xp, *pw), ln2_g[l], ln2_b[l])
        xs = layer_norm(ALPHA * xs + peer(xs, *pw), ln2_g[l], ln2_b[l])
    y_prompt, y_sample = xp, xs
    new_ckv_prompt, new_kpe_prompt = jnp.stack(ckv_p), jnp.stack(kpe_p)
    new_ckv_sample, new_kpe_sample = jnp.stack(ckv_s), jnp.stack(kpe_s)
    new_shift_prompt, new_shift_sample = jnp.stack(sh_p), jnp.stack(sh_s)
    new_wkv_prompt, new_wkv_sample = jnp.stack(wkv_p), jnp.stack(wkv_s)
    new_c_prompt, new_c_sample = jnp.stack(mc_p), jnp.stack(mc_s)
    new_n_prompt, new_n_sample = jnp.stack(mn_p), jnp.stack(mn_s)
    new_m_prompt, new_m_sample = jnp.stack(mm_p), jnp.stack(mm_s)
    return (y_prompt, y_sample, new_ckv_prompt, new_kpe_prompt, new_ckv_sample, new_kpe_sample,
            new_shift_prompt, new_shift_sample, new_wkv_prompt, new_wkv_sample,
            new_c_prompt, new_c_sample, new_n_prompt, new_n_sample, new_m_prompt, new_m_sample)


_drawn_inputs = setup_inputs


def setup_inputs(seed=0):
    import zlib

    import numpy as np

    out = dict(_drawn_inputs(seed))
    spreads = {}
    factors = {'cache_ckv': 3.55,
     'cache_kpe': 5.297,
     'w2_e': 7.294,
     'lnx_w_e': 5.01,
     'lnx_b_e': 3.404,
     'q_norm_e': 8.0,
     'mh_norm_o': 20.068}
    for name, (base, spread) in spreads.items():
        noise = np.random.default_rng([zlib.crc32(name.encode()), seed]).standard_normal(out[name].shape)
        drawn = base * np.exp(spread * noise) if base else spread * noise
        out[name] = __import__('jax').numpy.asarray(drawn.astype(out[name].dtype))
    for name, factor in factors.items():
        out[name] = (out[name] * factor).astype(out[name].dtype)
    return out
```

```python
from contextlib import ExitStack

import numpy as np
import concourse.bass as bass
from concourse import mybir

ALU = mybir.AluOpType
ACT = mybir.ActivationFunctionType
F32 = mybir.dt.float32
U32 = mybir.dt.uint32
AX = mybir.AxisListType.X

P = 128
D = 1024
KD = D // P
SEQ = 512
NB = 8
NS = 4
TILES = SEQ // P + 1
SAMP = TILES - 1
SEG = 16
NSEG = P // SEG
TOK = SEQ + NB * NS
H = 8
HD = 64
AW = H * HD
PAIRS = H // 2
RW = 3 * AW + 64 + 64 + 128
QL, KV, RP = 384, 256, 32
INE = RW + QL + KV + RP
DV = 128
INO = 2 * AW + 2 * H * DV + 2 * H
NPAGE, PAGE = 32, 128
PAST = NPAGE * PAGE
ALPHA = 4.0 ** 0.25
SM = (64 + 32) ** -0.5
NEG = -1.0e30
NK = 128
PH, PK = 8, 16
HK = PH * PK
CAP = 15.0



def constants():
    r = np.arange(P)
    row, col = r[:, None], r[None, :]
    same = row // SEG == col // SEG
    real = (r % SEG >= 1) & (r % SEG <= NS)
    c = {}
    c["ident"] = row == col
    c["iota"] = np.broadcast_to(col, (P, P))
    c["upto16"] = same & (row <= col)
    c["before16"] = same & (row < col)
    c["after16"] = same & (row > col)
    c["upto"] = row <= col
    c["pair"] = row // HD == col // HD
    c["seg_of_row"] = row // SEG == np.arange(NSEG)[None, :]
    c["seg_of_col"] = np.broadcast_to((np.arange(NSEG)[:, None] == r[None, :] // SEG).reshape(1, -1), (P, NSEG * P))
    c["real"] = real[:, None]
    c["ones"] = np.ones((P, P))
    c["negc"] = np.full((P, 1), -np.exp(-0.5))
    c["negc_real"] = real[:, None] * -np.exp(-0.5)
    c["causal"] = np.where(col <= row, 0.0, NEG)
    c["causal_s"] = np.where(same & (col <= row) & real[None, :], 0.0, NEG)
    c["last"] = (row == P - 1) & (col >= 0)
    c["last_s"] = row == SEG * (col // SEG) + NS
    c["newest"] = (row == SEG * np.arange(NSEG)[None, :] + NS)
    pos = np.concatenate([np.arange(SEQ), PAST + np.arange(P) % SEG - 1.0])
    inv = (np.float32(10000.0) ** (-np.arange(0, RP, 2, dtype=np.float32) / np.float32(RP))).astype(np.float32)
    ang = pos.astype(np.float32)[:, None] * inv[None, :]
    lay = lambda a: a.reshape(TILES, P, RP // 2).transpose(1, 0, 2).reshape(P, -1)
    c["cos"], c["sin"] = lay(np.cos(ang)), lay(np.sin(ang))
    q = r % NS
    s = np.arange(SEG)
    c["newmask"] = np.where((s[None, :] >= 1) & (s[None, :] <= q[:, None] + 1), 0.0, NEG)
    return {k: np.ascontiguousarray(v, dtype=np.float32) for k, v in c.items()}


CONST_COLS = {k: v.shape[1] for k, v in constants().items()}
CONST_AT, _n = {}, 0
for _k, _w in CONST_COLS.items():
    CONST_AT[_k] = _n
    _n += _w
CONST_N = _n


class Stage:

    def __init__(self, nc, name):
        self.nc, self.name, self.ctx, self.sems = nc, name, ExitStack(), []

    def sb(self, name, shape, dt=F32):
        return self.ctx.enter_context(self.nc.sbuf_tensor(f"{self.name}_{name}", shape, dt))

    def banks(self, name, n=1):
        return self.ctx.enter_context(self.nc.psum_tensor(f"{self.name}_{name}", [P, n, 512], F32))

    def sem(self, name):
        s = self.nc.alloc_semaphore(f"{self.name}_{name}")
        self.sems.append(s)
        return s

    def __enter__(self):
        return self

    def __exit__(self, *exc):
        self.ctx.close()
        if exc[0] is None:
            self.nc.clear_and_free_semaphores(self.sems)
            self.nc.all_engine_barrier()
        return False


class Chain:

    def __init__(self, eng, sem):
        self.eng, self.sem, self.n = eng, sem, 0

    def __call__(self, ins):
        self.n += 1
        ins.then_inc(self.sem, 1)
        self.eng.wait_ge(self.sem, self.n)


def mid(ap, n):
    return ap.unsqueeze(1).to_broadcast([ap.shape[0], n, ap.shape[1]])


def last(ap, n):
    return ap.unsqueeze(2).to_broadcast([ap.shape[0], ap.shape[1], n])


def project(nc, name, w_dram, n_cols, xT, out):
    chunks = [(a, min(512, n_cols - a)) for a in range(0, n_cols, 512)]
    with Stage(nc, name) as st:
        w = st.sb("w", [P, 2, KD, 512])
        acc = st.banks("acc", 4)
        w_in = [st.sem(f"w_loaded{i}") for i in range(2)]
        tile_done = st.sem("tile_multiplied")
        kept = [st.sem("kept_by_vector"), st.sem("kept_by_scalar")]
        wv = w_dram.rearrange("(k p) n -> p k n", p=P)
        with nc.Block() as block:
            @block.sync
            def _(sp):
                for n, (a, m) in enumerate(chunks):
                    if n >= 2:
                        sp.wait_ge(tile_done, TILES * (n - 1))
                    sp.dma_start(w[:, n % 2, :, 0:m], wv[:, :, a:a + m]).then_inc(w_in[n % 2], 16)

            @block.tensor
            def _(pe):
                for n, (a, m) in enumerate(chunks):
                    pe.wait_ge(w_in[n % 2], 16 * (n // 2 + 1))
                    for t in range(TILES):
                        i = n * TILES + t
                        if i >= 4:
                            pe.wait_ge(kept[i % 2], (i - 4) // 2 + 1)
                        for k in range(KD):
                            mm = nc.tensor.matmul(acc[:, i % 4, 0:m], xT[:, k, t * P:(t + 1) * P],
                                                  w[:, n % 2, k, 0:m], start=k == 0, stop=k == KD - 1)
                        mm.then_inc(tile_done, 1)

            def keep(eng, copy, par):
                for n, (a, m) in enumerate(chunks):
                    for t in range(TILES):
                        i = n * TILES + t
                        if i % 2 == par:
                            eng.wait_ge(tile_done, i + 1)
                            copy(out[:, t, a:a + m], acc[:, i % 4, 0:m]).then_inc(kept[par], 1)

            @block.vector
            def _(dve):
                keep(dve, nc.vector.tensor_copy, 0)

            @block.scalar
            def _(act):
                keep(act, nc.scalar.copy, 1)


def rwkv(nc, C, A, proj, mix, O):
    with Stage(nc, "rwkv") as st:
        sb, sem = st.sb, st.sem
        names = ["mu", "w0", "a0", "kk", "ka", "rk", "lnw", "lnb"]
        width = {"mu": RW}
        row = {n: sb("row_" + n, [P, width.get(n, AW)]) for n in names}
        wa2 = sb("wa2", [P, AW])
        g2 = sb("g2", [P, AW])
        lwaT = sb("lwaT", [P, P])
        lgT = sb("lgT", [P, P])
        a_s = sb("a", [P, AW])
        z_s = sb("z", [P, AW])
        g_s = sb("g", [P, AW])
        logd = sb("logd", [P, AW])
        kk = sb("kk", [P, AW])
        kp = sb("kp", [P, AW])
        tmp = sb("tmp", [P, 2 * AW])
        nrm = sb("nrm", [P, 4, H])
        e_in, e_neg, e_ex, e_rev = (sb(n, [P, AW]) for n in ("e_in", "e_neg", "e_ex", "e_rev"))
        e_chunk = sb("e_chunk", [P, PAIRS * NSEG])
        at, bt, kt, rt = e_ex, e_neg, sb("kt", [P, AW]), e_in
        bend, kend = e_rev, sb("kend", [P, AW])
        atT, btT, ktT, rtT = (sb(n, [P, PAIRS, P]) for n in ("atT", "btT", "ktT", "rtT"))
        mats = sb("mats", [P, 8, PAIRS, P])
        M, MT, M2, M2T, KAT, RBT, RKT, R = (mats[:, i, :, :] for i in range(8))
        bexp, kexp = (mats[:, i:i + 2, :, :].rearrange("p a b c -> p (a b) c") for i in (0, 2))
        Wp, U0 = (sb(n, [P, PAIRS, 2, HD]) for n in ("Wp", "U0"))
        GT = sb("GT", [P, PAIRS, P])
        y0 = sb("y0", [P, H, HD])
        Pbd, Qbd = (sb(n, [P, PAIRS, NSEG, P]) for n in ("Pbd", "Qbd"))
        prev = Pbd[:, :, :, :].rearrange("p a b c -> p (a b c)")[:, 0:RW]
        S = sb("S", [P, NSEG + 1, PAIRS, P])
        bank = st.banks("bank", 8)

        rows_in, prev_in, s_in = sem("rows_loaded"), sem("previous_rows"), sem("sample_states_loaded")
        prev_zero, last_in = sem("previous_zeroed"), sem("last_rows_stored")
        mixed, lora_t, lora_in, lora_out = sem("tokens_shifted"), sem("lora_transposed"), sem("lora_inputs"), sem("lora_products")
        gates_z, gates = sem("gate_sums"), sem("gates_ready")
        sq_sum, root = sem("square_sums"), sem("key_norms")
        logd_ok, sums, exps = sem("log_decay"), sem("decay_sums"), sem("decay_exps")
        scaled, turned, turned_kept = sem("scaled"), sem("operands_turned"), sem("turned_kept")
        gram, gram_kept = sem("gram_products"), sem("gram_kept")
        step_pe, step_kept = sem("solve_products"), sem("solve_kept")
        yg, yg_kept = sem("chunk_outputs"), sem("chunk_outputs_kept")
        expd, pq, pq_kept = sem("keys_spread"), sem("transitions"), sem("transitions_kept")
        sc, sc_kept = sem("scan_product"), sem("scan_state")
        gexp, y1, var_ok, dev_ok, out_ok = sem("queries_spread"), sem("state_outputs"), sem("variances"), sem("deviations"), sem("tile_done")
        chain, pchain, out_s, s_used = sem("vector_chain"), sem("pool_chain"), sem("states_stored"), sem("state_seeded")

        with nc.Block() as block:
            @block.sync
            def _(sp):
                for n, src in (("mu", A["mu_e"]), ("w0", A["w0_e"]), ("a0", A["a0_e"]), ("kk", A["kk_e"]),
                               ("ka", A["ka_e"]), ("rk", A["rk_e"]), ("lnw", A["lnx_w_e"]), ("lnb", A["lnx_b_e"])):
                    sp.dma_start(row[n][:, :], src.partition_broadcast(P)).then_inc(rows_in, 16)
                sp.dma_start(wa2[0:64, :], A["w2_e"]).then_inc(rows_in, 16)
                sp.dma_start(wa2[64:128, :], A["a2_e"]).then_inc(rows_in, 16)
                sp.dma_start(g2[:, :], A["g2_e"]).then_inc(rows_in, 16)
                sp.dma_start(A["last_rows"], proj[P - 1:P, 0:SAMP, 0:RW]).then_inc(last_in, 16)
                sp.wait_ge(last_in, 16)
                sp.wait_ge(prev_zero, 1)
                for t in range(TILES):
                    if t:
                        sp.wait_ge(out_ok, t)
                    sp.dma_start(prev[1:P, :], proj[0:P - 1, t, 0:RW]).then_inc(prev_in, 16)
                    if t:
                        sp.dma_start(prev[0:1, :], A["last_rows"][:, t - 1, :]).then_inc(prev_in, 16)
                sp.wait_ge(out_ok, SAMP)
                sp.dma_start(O["wkv_p"].rearrange("q p i -> p q i"), S[:, NSEG, :, :]).then_inc(out_s, 16)
                sp.wait_ge(out_s, 16)
                sp.dma_start(S[:, 0:NSEG, :, :], A["wkv_s"].rearrange("b q p i -> p b q i")).then_inc(s_in, 16)
                sp.wait_ge(out_ok, TILES)
                sp.dma_start(O["wkv_s"].rearrange("q b p i -> p q b i"), Pbd[:, :, :, :]).then_inc(out_s, 16)
                sp.wait_ge(out_s, 32)

            @block.tensor
            def _(pe):
                mmul = nc.tensor.matmul
                pe.wait_ge(rows_in, 16 * 11)
                for t in range(TILES):
                    v = proj[:, t, 2 * AW:3 * AW]
                    pe.wait_ge(mixed, t + 1)
                    if t:
                        pe.wait_ge(out_ok, t)
                    nc.tensor.transpose(bank[:, 0, 0:P], proj[:, t, 3 * AW:3 * AW + P], C["ident"])
                    nc.tensor.transpose(bank[:, 0, P:2 * P], proj[:, t, 3 * AW + P:RW], C["ident"]).then_inc(lora_t, 1)
                    pe.wait_ge(lora_in, 3 * (t + 1))
                    mmul(bank[:, 1, :], lwaT[0:64, :], wa2[0:64, :], start=True, stop=True)
                    mmul(bank[:, 2, :], lwaT[64:P, :], wa2[64:P, :], start=True, stop=True)
                    mmul(bank[:, 3, :], lgT[:, :], g2[:, :], start=True, stop=True).then_inc(lora_out, 1)
                    pe.wait_ge(logd_ok, t + 1)
                    mmul(bank[:, 4, :], C["upto16"], logd[:, :], start=True, stop=True)
                    mmul(bank[:, 5, :], C["before16"], logd[:, :], start=True, stop=True)
                    mmul(bank[:, 6, :], C["after16"], logd[:, :], start=True, stop=True)
                    for q in range(PAIRS):
                        mm = mmul(bank[:, 7, q * NSEG:(q + 1) * NSEG], logd[:, q * P:(q + 1) * P], C["seg_of_row"],
                                  start=True, stop=True)
                    mm.then_inc(sums, 1)
                    pe.wait_ge(scaled, t + 1)
                    pe.wait_ge(gates, 3 * (t + 1))
                    for i, x in enumerate((at, bt, kt, rt)):
                        for q in range(PAIRS):
                            mm = nc.tensor.transpose(bank[:, i, q * P:(q + 1) * P], x[:, q * P:(q + 1) * P], C["ident"])
                    mm.then_inc(turned, 1)
                    for g in range(2):
                        n = 2 * t + g
                        half = slice(g * HD, (g + 1) * HD)
                        pe.wait_ge(turned_kept, 4 * (t + 1))
                        if g:
                            pe.wait_ge(yg_kept, 2 * n)
                        for i, (x, y) in enumerate(((atT, btT), (btT, atT), (ktT, atT), (btT, rtT), (ktT, rtT))):
                            for q in range(PAIRS):
                                mm = mmul(bank[:, i, q * P:(q + 1) * P], x[half, q, :], y[half, q, :], start=True, stop=True)
                            mm.then_inc(gram, 1)
                        hd = lambda x, q: x[:, (2 * q + g) * HD:(2 * q + g + 1) * HD]
                        pe.wait_ge(gram_kept, 6 * n + 4)
                        for q in range(PAIRS):
                            mm = mmul(bank[:, 5, q * HD:(q + 1) * HD], KAT[:, q, :], hd(v, q), start=True, stop=True)
                        mm.then_inc(step_pe, 1)
                        pe.wait_ge(step_kept, 6 * n + 1)
                        seq = ((MT, M, M2, M2T), (M2T, M2, M, MT), (MT, M, M2, M2T))
                        for s, (xT, x, nx, nxT) in enumerate(seq):
                            for q in range(PAIRS if s < 2 else 0):
                                mmul(bank[:, 0, q * P:(q + 1) * P], xT[:, q, :], x[:, q, :], start=True, stop=True)
                            for q in range(PAIRS):
                                mmul(bank[:, 1, q * P:(q + 1) * P], x[:, q, :], xT[:, q, :], start=True, stop=True)
                            for q in range(PAIRS):
                                mm = mmul(bank[:, 2, q * P:(q + 1) * P], xT[:, q, :], R[:, q, :], start=True, stop=True)
                            mm.then_inc(step_pe, 1)
                            pe.wait_ge(step_kept, 6 * n + 2 + s)
                        for q in range(PAIRS):
                            mm = mmul(bank[:, 3, q * P:(q + 1) * P], M2T[:, q, :], R[:, q, :], start=True, stop=True)
                        mm.then_inc(step_pe, 1)
                        pe.wait_ge(step_kept, 6 * n + 6)
                        for q in range(PAIRS):
                            mmul(bank[half, 4, q * P:(q + 1) * P], Wp[:, q, g, :], RBT[:, q, :], start=True, stop=True)
                        for q in range(PAIRS):
                            mmul(bank[:, 5, q * HD:(q + 1) * HD], RBT[:, q, :], U0[:, q, g, :], start=True, stop=False)
                            mm = mmul(bank[:, 5, q * HD:(q + 1) * HD], RKT[:, q, :], hd(v, q), start=False, stop=True)
                        mm.then_inc(yg, 1)
                    for q in range(PAIRS):
                        n = PAIRS * t + q
                        pe.wait_ge(expd, 2 * (n + 1))
                        pe.wait_ge(pq_kept, 4 * n) if n else None
                        pe.wait_ge(yg_kept, 4 * (t + 1))
                        wq = Wp[:, q, :, :].rearrange("p a b -> p (a b)")
                        uq = U0[:, q, :, :].rearrange("p a b -> p (a b)")
                        for i in range(2):
                            mm = mmul(bank[:, i, :], wq, bexp[:, 4 * i:4 * i + 4, :].rearrange("p a b -> p (a b)"), start=True, stop=True)
                        for c in range(NSEG):
                            o = bank[:, 2 + c // 4, (c % 4) * P:(c % 4 + 1) * P]
                            mmul(o, bexp[:, c, :], uq, start=True, stop=False)
                            mm = mmul(o, kexp[:, c, :], v[:, q * P:(q + 1) * P], start=False, stop=True)
                        mm.then_inc(pq, 1)
                    for c in range(NSEG):
                        n = NSEG * t + c
                        pe.wait_ge(pq_kept, 4 * PAIRS * (t + 1))
                        if n:
                            pe.wait_ge(sc_kept, n)
                        if c == 0 and t < SAMP:
                            pe.wait_ge(s_used, t + 1)
                        elif c == 0:
                            pe.wait_ge(s_in, 16)
                        for q in range(PAIRS):
                            mm = mmul(bank[:, 4 + c % 2, q * P:(q + 1) * P], Pbd[:, q, c, :], S[:, c, q, :], start=True, stop=True)
                        mm.then_inc(sc, 1)
                    for q in range(PAIRS):
                        n = PAIRS * t + q
                        pe.wait_ge(gexp, n + 1)
                        for c in range(NSEG):
                            mm = mmul(bank[:, 6, q * P:(q + 1) * P], (bexp if q % 2 == 0 else kexp)[:, c, :], S[:, c, q, :],
                                      start=c == 0, stop=c == NSEG - 1)
                        mm.then_inc(y1, 1)

            @block.scalar
            def _(act):
                a_ = nc.scalar.activation
                for t in range(TILES):
                    act.wait_ge(lora_t, t + 1)
                    a_(lwaT[0:64, :], bank[0:64, 0, 0:P], ACT.Tanh).then_inc(lora_in, 1)
                    nc.scalar.copy(lwaT[64:P, :], bank[64:P, 0, 0:P]).then_inc(lora_in, 1)
                    a_(lgT[:, :], bank[:, 0, P:2 * P], ACT.Sigmoid).then_inc(lora_in, 1)
                    act.wait_ge(lora_out, t + 1)
                    nc.scalar.copy(g_s[:, :], bank[:, 3, :]).then_inc(gates, 1)
                    act.wait_ge(gates_z, 2 * (t + 1))
                    a_(z_s[:, :], z_s[:, :], ACT.Sigmoid).then_inc(gates, 1)
                    a_(a_s[:, :], a_s[:, :], ACT.Sigmoid).then_inc(gates, 1)
                    act.wait_ge(sq_sum, t + 1)
                    a_(nrm[:, 1, :], nrm[:, 0, :], ACT.Sqrt).then_inc(root, 1)
                    act.wait_ge(sums, t + 1)
                    a_(e_in[:, :], bank[:, 4, :], ACT.Exp).then_inc(exps, 1)
                    a_(e_neg[:, :], bank[:, 4, :], ACT.Exp, scale=-1.0).then_inc(exps, 1)
                    a_(e_ex[:, :], bank[:, 5, :], ACT.Exp).then_inc(exps, 1)
                    a_(e_rev[:, :], bank[:, 6, :], ACT.Exp).then_inc(exps, 1)
                    a_(e_chunk[:, :], bank[:, 7, 0:PAIRS * NSEG], ACT.Exp).then_inc(exps, 1)
                    act.wait_ge(turned, t + 1)
                    for i, x in enumerate((atT, btT, ktT, rtT)):
                        nc.scalar.copy(x[:, :, :].rearrange("p a b -> p (a b)"), bank[:, i, :]).then_inc(turned_kept, 1)
                    act.wait_ge(var_ok, t + 1)
                    a_(nrm[:, 1, :], nrm[:, 0, :], ACT.Sqrt).then_inc(dev_ok, 1)

            @block.gpsimd
            def _(pool):
                nc.gpsimd.memset(prev[0:1, :], 0.0).then_inc(prev_zero, 1)

            @block.vector
            def _(dve):
                V = nc.vector
                ch = Chain(dve, chain)
                tt, stt, tsc = V.tensor_tensor, V.scalar_tensor_tensor, V.tensor_scalar
                flat = lambda x: x[:, :, :].rearrange("p a b -> p (a b)")
                h3 = lambda x: x.rearrange("p (h d) -> p h d", h=H)
                dve.wait_ge(rows_in, 16 * 11)
                for t in range(TILES):
                    r, k, v = (proj[:, t, i * AW:(i + 1) * AW] for i in range(3))
                    rw = proj[:, t, 0:RW]
                    if t == 0:
                        dve.wait_ge(prev_zero, 1)
                    dve.wait_ge(last_in, 16)
                    dve.wait_ge(prev_in, 16 * (2 * t + 1))
                    ch(tt(prev[:, :], prev[:, :], rw, ALU.subtract))
                    ch(tt(prev[:, :], prev[:, :], row["mu"][:, :], ALU.mult))
                    tt(rw, rw, prev[:, :], ALU.add).then_inc(mixed, 1)
                    dve.wait_ge(mixed, t + 1)
                    dve.wait_ge(lora_out, t + 1)
                    tt(z_s[:, :], bank[:, 1, :], row["w0"][:, :], ALU.add).then_inc(gates_z, 1)
                    tt(a_s[:, :], bank[:, 2, :], row["a0"][:, :], ALU.add).then_inc(gates_z, 1)
                    ch(tt(kk[:, :], k, row["kk"][:, :], ALU.mult))
                    ch(tt(tmp[:, 0:AW], kk[:, :], kk[:, :], ALU.mult))
                    V.tensor_reduce(nrm[:, 0, :], h3(tmp[:, 0:AW]), AX, ALU.add).then_inc(sq_sum, 1)
                    dve.wait_ge(gates, 3 * (t + 1))
                    real = "negc" if t < SAMP else "negc_real"
                    tsc(logd[:, :], z_s[:, :], C[real], None, ALU.mult).then_inc(logd_ok, 1)
                    dve.wait_ge(root, t + 1)
                    ch(tsc(nrm[:, 2, :], nrm[:, 1, :], 1e-12, None, ALU.max))
                    ch(V.reciprocal(nrm[:, 1, :], nrm[:, 2, :]))
                    if t == SAMP:
                        ch(tsc(nrm[:, 1, :], nrm[:, 1, :], C["real"], None, ALU.mult))
                    ch(tt(h3(kk[:, :]), h3(kk[:, :]), last(nrm[:, 1, :], HD), ALU.mult))
                    ch(stt(tmp[:, 0:AW], a_s[:, :], -1.0, row["ka"][:, :], ALU.add, ALU.mult))
                    ch(stt(kp[:, :], tmp[:, 0:AW], 1.0, k, ALU.add, ALU.mult))
                    if t == SAMP:
                        ch(tsc(kp[:, :], kp[:, :], C["real"], None, ALU.mult))
                    ch(tt(a_s[:, :], a_s[:, :], kk[:, :], ALU.mult))
                    ch(tt(tmp[:, 0:AW], r, kp[:, :], ALU.mult))
                    ch(tt(tmp[:, 0:AW], tmp[:, 0:AW], row["rk"][:, :], ALU.mult))
                    ch(V.tensor_reduce(nrm[:, 3, :], h3(tmp[:, 0:AW]), AX, ALU.add))
                    dve.wait_ge(exps, 5 * (t + 1))
                    stt(at[:, :], e_ex[:, :], -1.0, kk[:, :], ALU.mult, ALU.mult)
                    tt(kt[:, :], e_neg[:, :], kp[:, :], ALU.mult)
                    tt(bt[:, :], e_neg[:, :], a_s[:, :], ALU.mult)
                    ch(tt(rt[:, :], e_in[:, :], r, ALU.mult))
                    tt(kend[:, :], e_rev[:, :], kp[:, :], ALU.mult).then_inc(scaled, 1)
                    dve.wait_ge(scaled, t + 1)
                    ch(tt(bend[:, :], e_rev[:, :], a_s[:, :], ALU.mult))
                    for g in range(2):
                        n = 2 * t + g
                        half = slice(g * HD, (g + 1) * HD)
                        masks = ("after16", "before16", "before16", "upto16", "upto16")
                        for i, (x, m) in enumerate(zip((M, MT, KAT, RBT, RKT), masks)):
                            dve.wait_ge(gram, 5 * n + i + 1)
                            tt(x[:, :, :], bank[:, i, :].rearrange("p (a b) -> p a b", b=P), mid(C[m], PAIRS), ALU.mult).then_inc(gram_kept, 1)
                            if i == 2:
                                V.tensor_copy(R[:, :, 0:HD], at[:, :].rearrange("p (q g d) -> p q g d", g=2, d=HD)[:, :, g, :]).then_inc(gram_kept, 1)
                        dve.wait_ge(step_pe, 5 * n + 1)
                        V.tensor_copy(R[:, :, HD:P], bank[:, 5, 0:PAIRS * HD].rearrange("p (q d) -> p q d", d=HD)).then_inc(step_kept, 1)
                        for s, (nx, nxT) in enumerate(((M2, M2T), (M, MT), (M2, M2T))):
                            dve.wait_ge(step_pe, 5 * n + 2 + s)
                            if s < 2:
                                V.tensor_copy(flat(nx), bank[:, 0, :])
                            ch(V.tensor_copy(flat(nxT), bank[:, 1, :]))
                            tt(flat(R), flat(R), bank[:, 2, :], ALU.add).then_inc(step_kept, 1)
                            dve.wait_ge(step_kept, 6 * n + 2 + s)
                        dve.wait_ge(step_pe, 5 * n + 5)
                        b3 = bank[:, 3, :].rearrange("p (q x) -> p q x", x=P)
                        tt(Wp[:, :, g, :], R[:, :, 0:HD], b3[:, :, 0:HD], ALU.add).then_inc(step_kept, 1)
                        tt(U0[:, :, g, :], R[:, :, HD:P], b3[:, :, HD:P], ALU.add).then_inc(step_kept, 1)
                        dve.wait_ge(yg, n + 1)
                        tt(GT[half, :, :], bank[half, 4, :].rearrange("p (q x) -> p q x", x=P), rtT[half, :, :], ALU.add).then_inc(yg_kept, 1)
                        V.tensor_copy(y0[:, :, :].rearrange("p (q g) d -> p q g d", g=2)[:, :, g, :],
                                      bank[:, 5, 0:PAIRS * HD].rearrange("p (q d) -> p q d", d=HD)).then_inc(yg_kept, 1)
                    for q in range(PAIRS):
                        n = PAIRS * t + q
                        if q:
                            dve.wait_ge(pq, n)
                        for x, y in ((bexp, bend), (kexp, kend)):
                            tt(x[:, :, :], mid(y[:, q * P:(q + 1) * P], NSEG), last(C["seg_of_row"], P), ALU.mult).then_inc(expd, 1)
                        dve.wait_ge(pq, n + 1)
                        tt(Qbd[:, q, :, :], bank[:, 2:4, :].rearrange("p a (c x) -> p (a c) x", x=P), mid(C["pair"], NSEG), ALU.mult).then_inc(pq_kept, 1)
                        tt(Pbd[:, q, :, :], bank[:, 0:2, :].rearrange("p a (c x) -> p (a c) x", x=P), mid(C["pair"], NSEG), ALU.mult).then_inc(pq_kept, 1)
                        d3 = tmp[:, 0:NSEG * P].rearrange("p (c x) -> p c x", x=P)
                        tt(d3, mid(C["ident"], NSEG), last(e_chunk[:, q * NSEG:(q + 1) * NSEG], P), ALU.mult).then_inc(pq_kept, 1)
                        dve.wait_ge(pq_kept, 4 * n + 3)
                        tt(Pbd[:, q, :, :], Pbd[:, q, :, :], d3, ALU.add).then_inc(pq_kept, 1)
                        dve.wait_ge(pq_kept, 4 * n + 4)
                    sflat = lambda c: S[:, c, :, :]
                    if t == 0:
                        V.memset(sflat(0), 0.0).then_inc(s_used, 1)
                    elif t < SAMP:
                        V.tensor_copy(sflat(0), sflat(NSEG)).then_inc(s_used, 1)
                    if t < SAMP:
                        dve.wait_ge(s_used, t + 1)
                    for c in range(NSEG):
                        n = NSEG * t + c
                        dve.wait_ge(sc, n + 1)
                        b = bank[:, 4 + c % 2, :].rearrange("p (q x) -> p q x", x=P)
                        o = S[:, c + 1, :, :] if t < SAMP else Pbd[:, :, c, :]
                        tt(o, b, Qbd[:, :, c, :], ALU.add).then_inc(sc_kept, 1)
                    for q in range(PAIRS):
                        n = PAIRS * t + q
                        if q == 0:
                            dve.wait_ge(pq, PAIRS * (t + 1))
                        if q >= 2:
                            dve.wait_ge(y1, n - 1)
                        tt((bexp if q % 2 == 0 else kexp)[:, :, :], mid(GT[:, q, :], NSEG),
                           C["seg_of_col"].rearrange("p (c x) -> p c x", x=P), ALU.mult).then_inc(gexp, 1)
                    dve.wait_ge(y1, PAIRS * (t + 1))
                    y = tmp[:, 0:AW]
                    y2 = tmp[:, AW:2 * AW]
                    dve.wait_ge(yg_kept, 4 * (t + 1))
                    ch(tt(h3(y), bank[:, 6, :].rearrange("p (h d) -> p h d", h=H), y0[:, :, :], ALU.add))
                    ch(V.tensor_reduce(nrm[:, 0, :], h3(y), AX, ALU.add))
                    ch(tsc(nrm[:, 0, :], nrm[:, 0, :], 1.0 / HD, None, ALU.mult))
                    ch(tt(h3(y), h3(y), last(nrm[:, 0, :], HD), ALU.subtract))
                    ch(tt(y2, y, y, ALU.mult))
                    ch(V.tensor_reduce(nrm[:, 2, :], h3(y2), AX, ALU.add))
                    tsc(nrm[:, 0, :], nrm[:, 2, :], 1.0 / HD, 64e-5, ALU.mult, ALU.add).then_inc(var_ok, 1)
                    dve.wait_ge(dev_ok, t + 1)
                    ch(V.reciprocal(nrm[:, 2, :], nrm[:, 1, :]))
                    ch(tt(h3(y), h3(y), last(nrm[:, 2, :], HD), ALU.mult))
                    ch(tt(y, y, row["lnw"][:, :], ALU.mult))
                    ch(tt(y, y, row["lnb"][:, :], ALU.add))
                    ch(tt(h3(y2), h3(v), last(nrm[:, 3, :], HD), ALU.mult))
                    ch(tt(y, y, y2, ALU.add))
                    tt(mix[:, t, 0:AW], y, g_s[:, :], ALU.mult).then_inc(out_ok, 1)
                    dve.wait_ge(out_ok, t + 1)


def mla(nc, C, A, proj, mix, O):
    QH = 64 + RP
    ROWS = H * NS
    GB = P // ROWS
    JP = 4
    with Stage(nc, "mla") as st:
        sb, sem = st.sb, st.sem
        wuq = sb("wuq", [P, 3, H * QH])
        wuk = sb("wuk", [P, 2, H * 64])
        wuv = sb("wuv", [P, 2, H * 64])
        wukT = sb("wukT", [64, H, KV])
        qnorm, kvnorm = sb("qnorm", [P, QL]), sb("kvnorm", [P, KV])
        pages = sb("pages", [1, NB * NPAGE], mybir.dt.int32)
        cn = sb("cn", [P, TILES, KV])
        kr = sb("kr", [P, TILES, RP])
        kpad = sb("kpad", [P, QH])
        cqn, sq = sb("cqn", [P, QL]), sb("sq", [P, QL])
        ms = sb("ms", [P, 6])
        q_s = sb("q", [P, H * QH])
        rt1, rt2 = sb("rt1", [P, H, RP // 2]), sb("rt2", [P, H, RP // 2])
        cqT, cT = sb("cqT", [P, 3, P]), sb("cT", [P, 2, P])
        kpT = sb("kpT", [QH, P])
        Vs = sb("Vs", [P, SAMP, H * 64])
        qT = sb("qT", [QH, H, P])
        mx, neg, tot, inv = (sb(n, [P, H]) for n in ("mx", "neg", "tot", "inv"))
        prob, probT = sb("prob", [P, 2, SEQ]), sb("probT", [P, 2, SEQ])
        qlT = sb("qlT", [P, 2, NB * ROWS])
        qpT = sb("qpT", [QH, NB * ROWS])
        keys = sb("keys", [P, 4, JP, 2 * PAGE])
        kpes = sb("kpes", [QH, 4, JP, PAGE])
        vals = sb("vals", [P, 4, JP, KV])
        vnew = sb("vnew", [SEG, NB, KV])
        W = PAST + SEG
        S = sb("S", [P, W])
        KT = S[0:QH, 0:H * SEQ].rearrange("p (h x) -> p h x", h=H)
        ST = sb("ST", [P, NPAGE + 1, P])
        o_s = sb("o", [P, KV])
        oT = sb("oT", [P, 2, H, NB * SEG])
        gm = sb("gm", [P, 4])
        bank = st.banks("bank", 8)

        here, pad0 = sem("weights_loaded"), sem("pads_zeroed")
        sq_in, rt_in = sem("mean_squares"), sem("roots")
        norm, flipped, flip_kept = sem("rows_normed"), sem("rows_turned"), sem("turned_kept")
        q_ok, q_kept, roped = sem("queries"), sem("queries_kept"), sem("queries_rotated")
        qt, qt_kept = sem("queries_turned"), sem("turned_queries_kept")
        kv, kv_kept = sem("keys_and_values"), sem("keys_and_values_kept")
        sc, sm, ex = sem("scores"), sem("score_maxima"), sem("exps")
        pt, pt_kept, pv, tile_ok = sem("probs_turned"), sem("turned_probs_kept"), sem("head_outputs"), sem("tile_done")
        chain = sem("vector_chain")
        ql, ql_kept = sem("latent_queries"), sem("latent_queries_kept")
        new_out, new_in, stores = sem("new_rows_stored"), sem("new_rows_loaded"), sem("outputs_stored")
        kin = [sem(f"keys_loaded{i}") for i in range(4)]
        vin = [sem(f"values_loaded{i}") for i in range(4)]
        pin = sem("page_table_loaded")
        ps, ps_kept = sem("page_scores"), [sem("scores_kept_v"), sem("scores_kept_s")]
        ns, ns_kept, gmax, gexp = sem("new_scores"), sem("new_scores_kept"), sem("group_maxima"), sem("group_exps")
        gt, gt_kept, gv, go = sem("group_turned"), sem("group_turned_kept"), sem("page_values"), sem("group_normed")
        gl, gl_kept, fin = sem("group_latents_turned"), sem("group_latents_kept"), sem("sample_outputs")
        JB = NPAGE // JP
        NCH = JB * GB

        with nc.Block() as block:
            @block.sync
            def _(sp):
                for dst, src in ((wuq[:, :, :], A["w_uq_e"].rearrange("(k p) n -> p k n", p=P)),
                                 (wuk[:, :, :], A["w_uk_e"].rearrange("(k p) n -> p k n", p=P)),
                                 (wuv[:, :, :], A["w_uv_e"].rearrange("(k p) n -> p k n", p=P)),
                                 (wukT[:, :, :], A["w_ukT_e"]),
                                 (qnorm[:, :], A["q_norm_e"].partition_broadcast(P)),
                                 (kvnorm[:, :], A["kv_norm_e"].partition_broadcast(P))):
                    sp.dma_start(dst, src).then_inc(here, 16)
                sp.dma_start(pages[:, :], A["page_table"]).then_inc(pin, 16)
                sp.wait_ge(pin, 16)
                for n in range(2 * NCH):
                    g, j, b = n // NCH, n % NCH // GB, n % GB
                    if n >= 4:
                        sp.wait_ge(ps, n - 3)
                    for i in range(JP):
                        at = (GB * g + b) * NPAGE + JP * j + i
                        pg = sp.value_load(pages[0:1, at:at + 1], min_val=0, max_val=A["keysT"].shape[0] - 1)
                        sp.dma_start(keys[:, n % 4, i, :], A["keysT"][bass.ds(pg, 1), :, :].rearrange("a p x -> p (a x)")).then_inc(kin[n % 4], 16)
                        sp.dma_start(kpes[64:QH, n % 4, i, :], A["kpesT"][bass.ds(pg, 1), :, :].rearrange("a p x -> p (a x)")).then_inc(kin[n % 4], 16)

            @block.gpsimd
            def _(pool):
                nc.gpsimd.memset(kpad[:, :], 0.0).then_inc(pad0, 1)
                nc.gpsimd.memset(oT[:, :, :, :], 0.0).then_inc(pad0, 1)
                pool.wait_ge(norm, TILES)
                pool.dma_start(A["new_rows"], cn[:, SAMP, :]).then_inc(new_out, 16)
                pool.wait_ge(new_out, 16)
                pool.dma_start(vnew[:, :, :], A["new_rows"].rearrange("(b s) c -> s b c", s=SEG)).then_inc(new_in, 16)
                pool.wait_ge(pin, 16)
                for n in range(2 * NCH):
                    g, j, b = n // NCH, n % NCH // GB, n % GB
                    if n >= 4:
                        pool.wait_ge(gv, n - 3)
                    for i in range(JP):
                        at = (GB * g + b) * NPAGE + JP * j + i
                        pg = pool.value_load(pages[0:1, at:at + 1], min_val=0, max_val=A["keysT"].shape[0] - 1)
                        pool.dma_start(vals[:, n % 4, i, :], A["cache_ckv"][bass.ds(pg, 1), :, :].rearrange("a p x -> p (a x)")).then_inc(vin[n % 4], 16)

            @block.tensor
            def _(pe):
                mmul, turn = nc.tensor.matmul, nc.tensor.transpose
                pe.wait_ge(here, 16 * 6)
                for t in range(TILES):
                    pe.wait_ge(norm, t + 1)
                    if t:
                        pe.wait_ge(tile_ok, t)
                    for i in range(3):
                        turn(bank[:, 0, i * P:(i + 1) * P], cqn[:, i * P:(i + 1) * P], C["ident"])
                    for i in range(2):
                        turn(bank[:, 1, i * P:(i + 1) * P], cn[:, t, i * P:(i + 1) * P], C["ident"])
                    turn(bank[0:QH, 3, 0:P], kpad[:, :], C["ident"]).then_inc(flipped, 1)
                    pe.wait_ge(flip_kept, 3 * (t + 1))
                    for x in range(2):
                        for k in range(3):
                            mm = mmul(bank[:, 2 + x, 0:384], cqT[:, k, :], wuq[:, k, x * 384:(x + 1) * 384], start=k == 0, stop=k == 2)
                    mm.then_inc(q_ok, 1)
                    if t < SAMP:
                        for h in range(H):
                            for k in range(2):
                                mmul(bank[0:64, 6 + h // 4, h % 4 * P:(h % 4 + 1) * P], wuk[:, k, h * 64:(h + 1) * 64], cT[:, k, :],
                                     start=k == 0, stop=k == 1)
                        for k in range(2):
                            mm = mmul(bank[:, 0, :], cT[:, k, :], wuv[:, k, :], start=k == 0, stop=k == 1)
                        mm.then_inc(kv, 1)
                    pe.wait_ge(roped, t + 1)
                    for h in range(H):
                        mm = turn(bank[0:QH, 4 + h // 4, h % 4 * P:(h % 4 + 1) * P], q_s[:, h * QH:(h + 1) * QH], C["ident"])
                    mm.then_inc(qt, 1)
                    pe.wait_ge(qt_kept, 2 * (t + 1))
                    if t < SAMP:
                        pe.wait_ge(kv_kept, 3 * (t + 1))
                        n_k = (t + 1) * P
                        for i in range(H + 2):
                            if i < H:
                                n = H * t + i
                                if i >= 2:
                                    pe.wait_ge(ex, n - 1)
                                mmul(bank[:, 2 + i % 2, 0:n_k], qT[:, i, :], KT[:, i, 0:n_k], start=True, stop=True).then_inc(sc, 1)
                            if 1 <= i <= H:
                                n = H * t + i - 1
                                pe.wait_ge(ex, n + 1)
                                if i >= 3:
                                    pe.wait_ge(pt_kept, n - 1)
                                for k in range(t + 1):
                                    mm = turn(bank[:, 4 + (i - 1) % 2, k * P:(k + 1) * P], prob[:, (i - 1) % 2, k * P:(k + 1) * P], C["ident"])
                                mm.then_inc(pt, 1)
                            if i >= 2:
                                h, n = i - 2, H * t + i - 2
                                pe.wait_ge(pt_kept, n + 1)
                                for k in range(t + 1):
                                    mm = mmul(bank[:, 1, h * 64:(h + 1) * 64], probT[:, h % 2, k * P:(k + 1) * P], Vs[:, k, h * 64:(h + 1) * 64],
                                              start=k == 0, stop=k == t)
                                mm.then_inc(pv, 1)
                for k in range(2):
                    for h in range(H):
                        mm = mmul(bank[:, 2 * k + 2 + h // 4, h % 4 * P:(h % 4 + 1) * P] if k == 0 else bank[:, 6 + h // 4, h % 4 * P:(h % 4 + 1) * P],
                                  wukT[:, h, k * P:(k + 1) * P], qT[0:64, h, :], start=True, stop=True)
                mm.then_inc(ql, 1)
                pe.wait_ge(ql_kept, 5)
                for g in range(2):
                    for n in range(NCH):
                        j, b = n // GB, n % GB
                        m = g * NCH + n
                        jj = g * JB + j
                        if b == 0 and jj >= 2:
                            pe.wait_ge(ps_kept[jj % 2], jj // 2)
                        pe.wait_ge(kin[m % 4], 16 * 2 * JP * (m // 4 + 1))
                        cols = slice((GB * g + b) * ROWS, (GB * g + b + 1) * ROWS)
                        o = bank[b * ROWS:(b + 1) * ROWS, 2 + jj % 2, :].rearrange("p (i x) -> p i x", i=JP)
                        for k in range(2):
                            mmul(o, qlT[:, k, cols], keys[:, m % 4, :, k * PAGE:(k + 1) * PAGE], start=k == 0, stop=False)
                        mmul(o, qpT[64:QH, cols], kpes[64:QH, m % 4, :, :], start=False, stop=True).then_inc(ps, 1)
                    if g:
                        pe.wait_ge(ns_kept, 1)
                    for b in range(GB):
                        s = GB * g + b
                        o = bank[b * ROWS:(b + 1) * ROWS, 4, 0:SEG]
                        cols = slice(s * ROWS, (s + 1) * ROWS)
                        for k in range(2):
                            mmul(o, qlT[:, k, cols], cT[:, k, s * SEG:(s + 1) * SEG], start=k == 0, stop=False)
                        mm = mmul(o, qpT[64:QH, cols], kpT[64:QH, s * SEG:(s + 1) * SEG], start=False, stop=True)
                    mm.then_inc(ns, 1)
                    pe.wait_ge(gexp, g + 1)
                    for k in range(NPAGE + 1):
                        i = k // 4
                        if k % 4 == 0 and i >= 2:
                            pe.wait_ge(gt_kept, (NPAGE // 4 + 1) * g + i - 1)
                        w = PAGE if k < NPAGE else SEG
                        mm = turn(bank[0:w, 6 + i % 2, k % 4 * P:(k % 4 + 1) * P], S[:, k * PAGE:k * PAGE + w], C["ident"])
                        if k % 4 == 3 or k == NPAGE:
                            mm.then_inc(gt, 1)
                    pe.wait_ge(gt_kept, (NPAGE // 4 + 1) * (g + 1))
                    if g == 0:
                        pe.wait_ge(new_in, 16)
                    else:
                        pe.wait_ge(go, 1)
                    for n in range(NCH):
                        j, b = n // GB, n % GB
                        m = g * NCH + n
                        pe.wait_ge(vin[m % 4], 16 * JP * (m // 4 + 1))
                        o = bank[b * ROWS:(b + 1) * ROWS, 5, 0:KV]
                        for i in range(JP):
                            k = JP * j + i
                            mm = mmul(o, ST[:, k, b * ROWS:(b + 1) * ROWS], vals[:, m % 4, i, :], start=k == 0, stop=False)
                        mm.then_inc(gv, 1)
                    for b in range(GB):
                        mm = mmul(bank[b * ROWS:(b + 1) * ROWS, 5, 0:KV], ST[0:SEG, NPAGE, b * ROWS:(b + 1) * ROWS], vnew[:, GB * g + b, :],
                                  start=False, stop=True)
                    mm.then_inc(fin, 1)
                    pe.wait_ge(go, g + 1)
                    for k in range(2):
                        mm = turn(bank[:, 6, k * P:(k + 1) * P], o_s[:, k * P:(k + 1) * P], C["ident"])
                    mm.then_inc(gl, 1)
                    pe.wait_ge(gl_kept, 2 * (g + 1))
                for h in range(H):
                    for k in range(2):
                        mm = mmul(bank[:, 0, h * 64:(h + 1) * 64], oT[:, k, h, :], wuv[:, k, h * 64:(h + 1) * 64], start=k == 0, stop=k == 1)
                mm.then_inc(fin, 1)

            @block.scalar
            def _(act):
                a_, cp = nc.scalar.activation, nc.scalar.copy
                for t in range(TILES):
                    act.wait_ge(sq_in, t + 1)
                    a_(ms[:, 2:4], ms[:, 0:2], ACT.Sqrt).then_inc(rt_in, 1)
                    act.wait_ge(flipped, t + 1)
                    cp(cqT[:, :, :].rearrange("p a b -> p (a b)"), bank[:, 0, 0:3 * P]).then_inc(flip_kept, 1)
                    cp(cT[:, :, :].rearrange("p a b -> p (a b)"), bank[:, 1, 0:2 * P]).then_inc(flip_kept, 1)
                    if t < SAMP:
                        act.wait_ge(kv, t + 1)
                        for i in range(2):
                            cp(KT[0:64, 4 * i:4 * i + 4, t * P:(t + 1) * P], bank[0:64, 6 + i, :].rearrange("p (h x) -> p h x", h=4)).then_inc(kv_kept, 1)
                        cp(Vs[:, t, :], bank[:, 0, :]).then_inc(kv_kept, 1)
                    act.wait_ge(qt, t + 1)
                    for i in range(2):
                        cp(qT[:, 4 * i:4 * i + 4, :].rearrange("p a b -> p (a b)"), bank[0:QH, 4 + i, :]).then_inc(qt_kept, 1)
                    if t == SAMP:
                        break
                    n_k = (t + 1) * P
                    for i in range(H + 1):
                        if i < H:
                            n = H * t + i
                            act.wait_ge(sm, n + 1)
                            if i >= 2:
                                act.wait_ge(pt, n - 1)
                            a_(prob[:, i % 2, 0:n_k], bank[:, 2 + i % 2, 0:n_k], ACT.Exp, bias=neg[:, i:i + 1], scale=SM,
                               accum_out=tot[:, i:i + 1]).then_inc(ex, 1)
                        if i >= 1:
                            n = H * t + i - 1
                            act.wait_ge(pt, n + 1)
                            if i >= 3:
                                act.wait_ge(pv, n - 1)
                            cp(probT[:, (i - 1) % 2, 0:n_k], bank[:, 4 + (i - 1) % 2, 0:n_k]).then_inc(pt_kept, 1)
                act.wait_ge(ql, 1)
                for k in range(2):
                    for i in range(2):
                        src = bank[:, (2 if k == 0 else 6) + i, :].rearrange("p (h b s) -> p h b s", h=4, s=SEG)[:, :, :, 1:1 + NS]
                        dst = qlT[:, k, :].rearrange("p (b h q) -> p h b q", h=H, q=NS)[:, 4 * i:4 * i + 4, :, :]
                        cp(dst, src).then_inc(ql_kept, 1)
                cp(qpT[64:QH, :].rearrange("p (b h q) -> p h b q", h=H, q=NS),
                   qT[64:QH, :, :].rearrange("p h (b s) -> p h b s", s=SEG)[:, :, :, 1:1 + NS]).then_inc(ql_kept, 1)
                for g in range(2):
                    for j in range(1, JB, 2):
                        act.wait_ge(ps, NCH * g + GB * (j + 1))
                        if g and j == 1:
                            act.wait_ge(gt, 9)
                        cp(S[:, j * 512:(j + 1) * 512], bank[:, 3, :]).then_inc(ps_kept[1], 1)
                    act.wait_ge(gmax, g + 1)
                    a_(S[:, :], S[:, :], ACT.Exp, bias=gm[:, 1:2], scale=SM, accum_out=gm[:, 2:3]).then_inc(gexp, 1)
                    for i in range(9):
                        act.wait_ge(gt, 9 * g + i + 1)
                        if g and i == 0:
                            act.wait_ge(fin, 1)
                        if i < 8:
                            cp(ST[:, 4 * i:4 * i + 4, :].rearrange("p a b -> p (a b)"), bank[:, 6 + i % 2, :]).then_inc(gt_kept, 1)
                        else:
                            cp(ST[0:SEG, NPAGE, :], bank[0:SEG, 6, 0:P]).then_inc(gt_kept, 1)
                act.wait_ge(norm, TILES)
                act.dma_start(O["ckv"].rearrange("(t p) c -> p t c", p=P), cn[:, :, :]).then_inc(stores, 16)
                act.dma_start(O["kpe"].rearrange("(t p) c -> p t c", p=P), kr[:, :, :]).then_inc(stores, 16)
                act.wait_ge(stores, 32)

            @block.vector
            def _(dve):
                V = nc.vector
                ch = Chain(dve, chain)
                tt, tsc = V.tensor_tensor, V.tensor_scalar
                dve.wait_ge(here, 16 * 6)
                dve.wait_ge(pad0, 2)
                for t in range(TILES):
                    cq = proj[:, t, 0:QL]
                    ckv = proj[:, t, QL:QL + KV]
                    kpe = proj[:, t, QL + KV:QL + KV + RP]
                    ch(tt(sq[:, :], cq, cq, ALU.mult))
                    ch(V.tensor_reduce(ms[:, 4:5], sq[:, :], AX, ALU.add))
                    ch(tt(sq[:, 0:KV], ckv, ckv, ALU.mult))
                    ch(V.tensor_reduce(ms[:, 5:6], sq[:, 0:KV], AX, ALU.add))
                    ch(tsc(ms[:, 0:1], ms[:, 4:5], 1.0 / QL, 1e-6, ALU.mult, ALU.add))
                    tsc(ms[:, 1:2], ms[:, 5:6], 1.0 / KV, 1e-6, ALU.mult, ALU.add).then_inc(sq_in, 1)
                    dve.wait_ge(rt_in, t + 1)
                    ch(V.reciprocal(ms[:, 4:6], ms[:, 2:4]))
                    ch(tsc(cqn[:, :], cq, ms[:, 4:5], None, ALU.mult))
                    tt(cqn[:, :], cqn[:, :], qnorm[:, :], ALU.mult)
                    ch(tsc(cn[:, t, :], ckv, ms[:, 5:6], None, ALU.mult))
                    ch(tt(cn[:, t, :], cn[:, t, :], kvnorm[:, :], ALU.mult))
                    cos, sin = (C[n][:, t * 16:(t + 1) * 16] for n in ("cos", "sin"))

                    def rotate(x1, x2, cs, sn, y1, y2, a, b):
                        tt(a, x1, cs, ALU.mult)
                        ch(tt(b, x2, sn, ALU.mult))
                        ch(tt(b, a, b, ALU.subtract))
                        ch(tt(a, x1, sn, ALU.mult))
                        ch(V.tensor_copy(y1, b))
                        ch(tt(b, x2, cs, ALU.mult))
                        ch(tt(y2, a, b, ALU.add))

                    rotate(kpe[:, 0:16], kpe[:, 16:32], cos, sin, kr[:, t, 0:16], kr[:, t, 16:32], rt1[:, 0, :], rt2[:, 0, :])
                    V.tensor_copy(kpad[:, 64:QH], kr[:, t, :]).then_inc(norm, 1)
                    dve.wait_ge(flipped, t + 1)
                    if t < SAMP:
                        V.tensor_copy(KT[64:QH, :, t * P:(t + 1) * P], mid(bank[64:QH, 3, 0:P], H)).then_inc(flip_kept, 1)
                    else:
                        V.tensor_copy(kpT[64:QH, :], bank[64:QH, 3, 0:P]).then_inc(flip_kept, 1)
                    dve.wait_ge(q_ok, t + 1)
                    ch(V.tensor_copy(q_s[:, :].rearrange("p (a x) -> p a x", a=2), bank[:, 2:4, 0:384]))
                    q3 = q_s[:, :].rearrange("p (h x) -> p h x", h=H)
                    x1, x2 = q3[:, :, 64:80], q3[:, :, 80:96]
                    rotate(x1, x2, mid(cos, H), mid(sin, H), x1, x2, rt1[:, :, :], rt2[:, :, :])
                    V.tensor_copy(rt1[:, 0, 0:1], rt2[:, 0, 0:1]).then_inc(roped, 1)
                    if t == SAMP:
                        V.tensor_copy(rt1[:, 0, 1:2], rt2[:, 0, 1:2]).then_inc(tile_ok, 1)
                        break
                    for h in range(H):
                        n = H * t + h
                        dve.wait_ge(sc, n + 1)
                        b = bank[:, 2 + h % 2, :]
                        ch(tt(b[:, t * P:(t + 1) * P], b[:, t * P:(t + 1) * P], C["causal"], ALU.add))
                        ch(V.tensor_reduce(mx[:, h:h + 1], b[:, 0:(t + 1) * P], AX, ALU.max))
                        tsc(neg[:, h:h + 1], mx[:, h:h + 1], -SM, None, ALU.mult).then_inc(sm, 1)
                    dve.wait_ge(ex, H * (t + 1))
                    ch(V.reciprocal(inv[:, :], tot[:, :]))
                    dve.wait_ge(pv, H * (t + 1))
                    tt(mix[:, t, :].rearrange("p (h d) -> p h d", h=H), bank[:, 1, :].rearrange("p (h d) -> p h d", h=H),
                       last(inv[:, :], 64), ALU.mult).then_inc(tile_ok, 1)
                for g in range(2):
                    for j in range(0, JB, 2):
                        dve.wait_ge(ps, NCH * g + GB * (j + 1))
                        if g and j == 0:
                            dve.wait_ge(gt, 9)
                        V.tensor_copy(S[:, j * 512:(j + 1) * 512], bank[:, 2, :]).then_inc(ps_kept[0], 1)
                    dve.wait_ge(ns, g + 1)
                    tt(S[:, PAST:W], bank[:, 4, 0:SEG], C["newmask"], ALU.add).then_inc(ns_kept, 1)
                    dve.wait_ge(ns_kept, g + 1)
                    dve.wait_ge(ps_kept[1], JB // 2 * (g + 1))
                    ch(V.tensor_reduce(gm[:, 0:1], S[:, :], AX, ALU.max))
                    tsc(gm[:, 1:2], gm[:, 0:1], -SM, None, ALU.mult).then_inc(gmax, 1)
                    dve.wait_ge(gexp, g + 1)
                    ch(V.reciprocal(gm[:, 3:4], gm[:, 2:3]))
                    dve.wait_ge(fin, g + 1)
                    tsc(o_s[:, :], bank[:, 5, 0:KV], gm[:, 3:4], None, ALU.mult).then_inc(go, 1)
                    dve.wait_ge(gl, g + 1)
                    for k in range(2):
                        for b in range(GB):
                            s = GB * g + b
                            ins = V.tensor_copy(oT[:, k, :, s * SEG + 1:s * SEG + 1 + NS],
                                                bank[:, 6, k * P + b * ROWS:k * P + (b + 1) * ROWS].rearrange("p (h q) -> p h q", h=H))
                        ins.then_inc(gl_kept, 1)
                dve.wait_ge(fin, 3)
                ch(V.tensor_copy(mix[:, SAMP, :], bank[:, 0, :]))


def turn(nc, name, C, x, xT, compact):
    with Stage(nc, name) as st:
        bank = st.banks("bank", 4)
        turned, kept = st.sem("rows_turned"), st.sem("columns_kept")
        with nc.Block() as block:
            @block.tensor
            def _(pe):
                for t in range(TILES):
                    for i in range(2):
                        n = 2 * t + i
                        if n >= 4:
                            pe.wait_ge(kept, n - 3)
                        for k in range(4):
                            mm = nc.tensor.transpose(bank[:, n % 4, k * P:(k + 1) * P], x[:, t, (4 * i + k) * P:(4 * i + k + 1) * P], C["ident"])
                        mm.then_inc(turned, 1)

            @block.vector
            def _(dve):
                for t in range(TILES):
                    for i in range(2):
                        n = 2 * t + i
                        dve.wait_ge(turned, n + 1)
                        src = bank[:, n % 4, :].rearrange("p (k x) -> p k x", k=4)
                        dst = xT[:, 4 * i:4 * i + 4, :]
                        if t < SAMP or not compact:
                            nc.vector.tensor_copy(dst[:, :, t * P:(t + 1) * P], src).then_inc(kept, 1)
                        else:
                            nc.vector.tensor_copy(dst[:, :, SEQ:TOK].rearrange("p k (b s) -> p k b s", s=NS),
                                                  src.rearrange("p k (b s) -> p k b s", s=SEG)[:, :, :, 1:1 + NS]).then_inc(kept, 1)


def layer_norm_vector(nc, dve, ch, x, t, sem_sum, sem_root, sem_norm, stats, mv, gain, shift):
    V = nc.vector
    V.bn_stats(stats[:, 0, :], x[:, t, 0:512])
    ch(V.bn_stats(stats[:, 1, :], x[:, t, 512:D]))
    ch(V.bn_aggr(mv[:, 0:2], stats[:, :, :]))
    V.tensor_scalar(mv[:, 2:3], mv[:, 1:2], 1e-5, None, ALU.add).then_inc(sem_sum, 1)
    dve.wait_ge(sem_root, t + 1)
    ch(V.reciprocal(mv[:, 4:5], mv[:, 3:4]))
    V.scalar_tensor_tensor(out=mv[:, 5:6], in0=mv[:, 0:1], scalar=-1.0, in1=mv[:, 4:5], op0=ALU.mult, op1=ALU.mult).then_inc(sem_sum, 1)
    dve.wait_ge(sem_norm, t + 1)
    ch(V.tensor_tensor(x[:, t, :], x[:, t, :], gain, ALU.mult))
    ch(V.tensor_tensor(x[:, t, :], x[:, t, :], shift, ALU.add))


def layer_norm_scalar(nc, act, x, t, sem_sum, sem_root, sem_norm, mv):
    act.wait_ge(sem_sum, 2 * t + 1)
    nc.scalar.activation(mv[:, 3:4], mv[:, 2:3], ACT.Sqrt).then_inc(sem_root, 1)
    act.wait_ge(sem_sum, 2 * t + 2)
    nc.scalar.activation(x[:, t, :], x[:, t, :], ACT.Identity, bias=mv[:, 5:6], scale=mv[:, 4:5]).then_inc(sem_norm, 1)


def out_project(nc, name, C, mixed, w_dram, gain_dram, shift_dram, x):
    with Stage(nc, name) as st:
        w = st.sb("w", [P, KD, D])
        gain, shift = st.sb("gain", [P, D]), st.sb("shift", [P, D])
        mT = st.sb("mT", [P, 2, KD, P])
        stats, mv = st.sb("stats", [P, 2, 6]), st.sb("mv", [P, 6])
        bank = st.banks("bank", 8)
        here = st.sem("weights_loaded")
        turned, kept, done, added = st.sem("turned"), st.sem("turned_kept"), st.sem("products"), st.sem("residual_added")
        s_sum, s_root, s_norm, chain = st.sem("statistics"), st.sem("deviation"), st.sem("normed"), st.sem("vector_chain")
        with nc.Block() as block:
            @block.sync
            def _(sp):
                sp.dma_start(w[:, :, :], w_dram.rearrange("(k p) n -> p k n", p=P)).then_inc(here, 16)
                sp.dma_start(gain[:, :], gain_dram.partition_broadcast(P)).then_inc(here, 16)
                sp.dma_start(shift[:, :], shift_dram.partition_broadcast(P)).then_inc(here, 16)

            @block.tensor
            def _(pe):
                def turns(t):
                    for i in range(2):
                        n = 2 * t + i
                        if n >= 4:
                            pe.wait_ge(kept, n - 3)
                        for k in range(4):
                            mm = nc.tensor.transpose(bank[:, n % 4, k * P:(k + 1) * P], mixed(t, 4 * i + k), C["ident"])
                        mm.then_inc(turned, 1)

                turns(0)
                pe.wait_ge(here, 48)
                for t in range(TILES):
                    if t + 1 < TILES:
                        turns(t + 1)
                    pe.wait_ge(kept, 2 * (t + 1))
                    if t >= 2:
                        pe.wait_ge(added, t - 1)
                    for i in range(2):
                        for k in range(KD):
                            mm = nc.tensor.matmul(bank[:, 4 + 2 * (t % 2) + i, :], mT[:, t % 2, k, :], w[:, k, i * 512:(i + 1) * 512],
                                                  start=k == 0, stop=k == KD - 1)
                    mm.then_inc(done, 1)

            @block.scalar
            def _(act):
                def keep(t):
                    if t >= 2:
                        act.wait_ge(done, t - 1)
                    for i in range(2):
                        act.wait_ge(turned, 2 * t + i + 1)
                        nc.scalar.copy(mT[:, t % 2, 4 * i:4 * i + 4, :].rearrange("p a b -> p (a b)"), bank[:, (2 * t + i) % 4, :]).then_inc(kept, 1)

                keep(0)
                for t in range(TILES):
                    if t + 1 < TILES:
                        keep(t + 1)
                    layer_norm_scalar(nc, act, x, t, s_sum, s_root, s_norm, mv)

            @block.vector
            def _(dve):
                ch = Chain(dve, chain)
                dve.wait_ge(here, 48)
                for t in range(TILES):
                    dve.wait_ge(done, t + 1)
                    nc.vector.scalar_tensor_tensor(out=x[:, t, :], in0=x[:, t, :], scalar=ALPHA,
                                                   in1=bank[:, 4 + 2 * (t % 2):6 + 2 * (t % 2), :].rearrange("p a b -> p (a b)"),
                                                   op0=ALU.mult, op1=ALU.add).then_inc(added, 1)
                    dve.wait_ge(added, t + 1)
                    layer_norm_vector(nc, dve, ch, x, t, s_sum, s_root, s_norm, stats, mv, gain[:, :], shift[:, :])


def peer_select(nc, name, C, xT, wq_dram, k1T_dram, k2T_dram, picks):
    T4 = SEQ // P
    rows = [P] * T4 + [TOK - SEQ]
    HALF = TOK // 2
    with Stage(nc, name) as st:
        sb, sem = st.sb, st.sem
        wq = sb("wq", [P, 2, KD, 512])
        kT = sb("kT", [P, 2, NK])
        qT = sb("qT", [P, 2, TOK])
        s = sb("scores", [P, 2, TILES, NK])
        s2 = sb("scores_rest", [P, TILES, NK])
        val = sb("val", [P, TILES, PH, 2, PK])
        idx = sb("idx", [P, TILES, PH, 2, PK], U32)
        idxf = sb("idxf", [P, PH, 2, PK])
        cand, cand2 = sb("cand", [P, PH, PK * PK]), sb("cand_rest", [P, PH, PK * PK])
        top, sel = sb("top", [P, PH, PK]), sb("sel", [P, PH, PK], U32)
        ab, abf = sb("ab", [P, 2, HK], U32), sb("abf", [P, 2, HK])
        out = sb("out", [P, 3, HK])
        eg, zg = sb("eg", [P, PH, PK]), sb("zg", [P, 2, PH])
        bank = st.banks("bank", 8)
        w_in, k_in = [sem("wq_loaded0"), sem("wq_loaded1")], sem("sub_keys_loaded")
        q_ok, q_kept, s_ok, s_kept, s_used = sem("queries"), sem("queries_kept"), sem("scores"), sem("scores_kept"), sem("scores_ranked")
        chain, diff, expd = sem("vector_chain"), sem("gate_logits"), sem("gate_exps")
        out_ok, turned, kept = sem("picks_ready"), sem("picks_turned"), sem("picks_kept")
        NC_ = 2 * PH
        with nc.Block() as block:
            @block.sync
            def _(sp):
                sp.dma_start(kT[:, 0, :], k1T_dram).then_inc(k_in, 16)
                sp.dma_start(kT[:, 1, :], k2T_dram).then_inc(k_in, 16)
                wv = wq_dram.rearrange("(k p) n -> p k n", p=P)
                for n in range(4):
                    if n >= 2:
                        sp.wait_ge(q_ok, 4 * (n - 1))
                    sp.dma_start(wq[:, n % 2, :, :], wv[:, :, n * 512:(n + 1) * 512]).then_inc(w_in[n % 2], 16)

            @block.tensor
            def _(pe):
                pe.wait_ge(k_in, 32)
                for c in range(NC_ + 1):
                    if c < NC_:
                        n = c // 4
                        pe.wait_ge(w_in[n % 2], 16 * (n // 2 + 1))
                        if c >= 2:
                            pe.wait_ge(q_kept, c - 1)
                        for i in range(2):
                            for k in range(KD):
                                mm = nc.tensor.matmul(bank[:, 2 * (c % 2) + i, 0:HALF], wq[:, n % 2, k, c % 4 * P:(c % 4 + 1) * P],
                                                      xT[:, k, i * HALF:(i + 1) * HALF], start=k == 0, stop=k == KD - 1)
                        mm.then_inc(q_ok, 1)
                    if c:
                        d = c - 1
                        pe.wait_ge(q_kept, d + 1)
                        if d >= 2:
                            pe.wait_ge(s_kept, 2 * (d - 1))
                        for t in range(TILES):
                            o = bank[0:rows[t], 4 + 2 * (d % 2) + t // T4, t % T4 * P:(t % T4 + 1) * P]
                            mm = nc.tensor.matmul(o, qT[:, d % 2, t * P:t * P + rows[t]], kT[:, d % 2, :], start=True, stop=True)
                        mm.then_inc(s_ok, 1)
                pe.wait_ge(s_kept, 2 * NC_)
                for t in range(TILES):
                    r = rows[t]
                    pe.wait_ge(out_ok, t + 1)
                    if t >= 2:
                        pe.wait_ge(kept, t - 1)
                    for i in range(3):
                        mm = nc.tensor.transpose(bank[:, t % 2, i * P:i * P + r], out[0:r, i, :], C["ident"][0:r, 0:r])
                    mm.then_inc(turned, 1)

            @block.scalar
            def _(act):
                for c in range(NC_ + 1):
                    if c < NC_:
                        act.wait_ge(q_ok, c + 1)
                        if c >= 2:
                            act.wait_ge(s_ok, c - 1)
                        nc.scalar.copy(qT[:, c % 2, :].rearrange("p (a x) -> p a x", a=2), bank[:, 2 * (c % 2):2 * (c % 2) + 2, 0:HALF]).then_inc(q_kept, 1)
                    if c:
                        d = c - 1
                        act.wait_ge(s_ok, d + 1)
                        if d >= 2:
                            act.wait_ge(s_used, d - 1)
                        nc.scalar.copy(s[:, d % 2, 0:T4, :].rearrange("p a b -> p (a b)"), bank[:, 4 + 2 * (d % 2), :]).then_inc(s_kept, 1)
                        nc.scalar.copy(s[0:rows[T4], d % 2, T4, :], bank[0:rows[T4], 5 + 2 * (d % 2), 0:P]).then_inc(s_kept, 1)
                for t in range(TILES):
                    act.wait_ge(diff, t + 1)
                    nc.scalar.activation(eg[0:rows[t], :, :], eg[0:rows[t], :, :], ACT.Exp).then_inc(expd, 1)
                    act.wait_ge(turned, t + 1)
                    src = bank[:, t % 2, 0:3 * P].rearrange("p (i x) -> p i x", i=3)[:, :, 0:rows[t]]
                    nc.scalar.copy(picks[:, :, t * P:t * P + rows[t]], src).then_inc(kept, 1)

            @block.vector
            def _(dve):
                V = nc.vector
                ch = Chain(dve, chain)
                tt = V.tensor_tensor

                def best16(items):
                    for n, step in enumerate((
                            lambda a, r, v, i: V.max(v[:, 0:8], a),
                            lambda a, r, v, i: V.max_index(i[:, 0:8], v[:, 0:8], a),
                            lambda a, r, v, i: V.match_replace(r, v[:, 0:8], a, NEG),
                            lambda a, r, v, i: V.max(v[:, 8:16], r),
                            lambda a, r, v, i: V.max_index(i[:, 8:16], v[:, 8:16], r))):
                        for item in items:
                            ins = step(*item)
                        ch(ins)

                for c in range(NC_):
                    h, half = c // 2, c % 2
                    dve.wait_ge(s_kept, 2 * (c + 1))
                    best16([(s[0:rows[t], c % 2, t, :], s2[0:rows[t], t, :], val[0:rows[t], t, h, half, :], idx[0:rows[t], t, h, half, :])
                            for t in range(TILES)])
                    V.tensor_copy(zg[0:1, 0, 0:1], val[0:1, 0, h, half, 0:1]).then_inc(s_used, 1)
                for t in range(TILES):
                    r = slice(0, rows[t])
                    c4 = cand[r].rearrange("p h (a b) -> p h a b", b=PK)
                    v1 = val[r, t, :, 0, :].unsqueeze(3).to_broadcast([rows[t], PH, PK, PK])
                    v2 = val[r, t, :, 1, :].unsqueeze(2).to_broadcast([rows[t], PH, PK, PK])
                    V.tensor_copy(idxf[r], idx[r, t])
                    ch(tt(c4, v1, v2, ALU.add))
                    best16([(cand[r, h, :], cand2[r, h, :], top[r, h, :], sel[r, h, :]) for h in range(PH)])
                    flat = sel[r].rearrange("p h k -> p (h k)")
                    V.tensor_scalar(ab[r, 0, :], flat, 4, None, ALU.logical_shift_right)
                    V.tensor_scalar(ab[r, 1, :], flat, PK - 1, None, ALU.bitwise_and)
                    ch(tt(eg[r], top[r], top[r, :, 0:1].to_broadcast([rows[t], PH, PK]), ALU.subtract))
                    V.tensor_copy(abf[r], ab[r]).then_inc(diff, 1)
                    dve.wait_ge(diff, t + 1)
                    if t:
                        dve.wait_ge(turned, t)
                    for i in range(2):
                        e = cand[r].rearrange("p h x -> p (h x)")
                        e3 = e.rearrange("p (n a) -> p n a", a=PK)
                        ch(tt(e3, last(abf[r, i, :], PK), mid(C["iota"][r, 0:PK], HK), ALU.is_equal))
                        e4 = e.rearrange("p (h k a) -> p h k a", h=PH, a=PK)
                        ch(tt(e4, e4, idxf[r, :, i, :].unsqueeze(2).to_broadcast([rows[t], PH, PK, PK]), ALU.mult))
                        ch(V.tensor_reduce(out[r, i, :], e3, AX, ALU.add))
                    dve.wait_ge(expd, t + 1)
                    ch(V.tensor_reduce(zg[r, 0, :], eg[r], AX, ALU.add))
                    ch(V.reciprocal(zg[r, 1, :], zg[r, 0, :]))
                    tt(out[r, 2, :].rearrange("p (h k) -> p h k", h=PH), eg[r], last(zg[r, 1, :], PK), ALU.mult).then_inc(out_ok, 1)
                    dve.wait_ge(out_ok, t + 1)


BLK = 32
NBLK = TOK // BLK


def peer_spread(nc, name, C, picks, grids):
    G4 = BLK // 4
    with Stage(nc, name) as st:
        sb, sem = st.sb, st.sem
        rowhot, colhot = sb("rowhot", [P, 4, 4, NK]), sb("colhot", [P, 4, 4, NK])
        grid = sb("grid", [P, 2, NK, BLK])
        bank = st.banks("bank", 4)
        marked, kept, free = sem("picks_marked"), sem("grids_kept"), sem("marks_used")
        sent = [sem("grid_sent0"), sem("grid_sent1")]
        TWO = NBLK // 2

        def block_steps(work, eng):
            with eng.Fori(0, TWO) as m:
                for u in range(2):
                    work(m * 2 + u, u, m)
            work(NBLK - 1, (NBLK - 1) % 2, TWO)

        with nc.Block() as block:
            @block.vector
            def _(dve):
                def work(b, u, m):
                    for j in range(G4):
                        dve.wait_ge(free, b * G4 + j + 1)
                        nc.vector.tensor_tensor(colhot[:, j % 4, :, :], mid(C["iota"], 4), last(picks[:, 1, bass.ds(b * BLK + 4 * j, 4)], NK), ALU.is_equal)
                        for i in range(4):
                            tok = b * BLK + (4 * j + i)
                            ins = nc.vector.tensor_scalar(rowhot[:, j % 4, i, :], C["iota"], picks[:, 0, bass.ds(tok, 1)],
                                                          picks[:, 2, bass.ds(tok, 1)], ALU.is_equal, ALU.mult)
                        ins.then_inc(marked, 1)
                block_steps(work, dve)

            @block.tensor
            def _(pe):
                pe.sem_inc(free, 4)
                def work(b, u, m):
                    for j in range(G4):
                        pe.wait_ge(marked, b * G4 + j + 1)
                        pe.wait_ge(kept, b * G4 + j + 1)
                        for i in range(4):
                            mm = nc.tensor.matmul(bank[:, j % 4, i * NK:(i + 1) * NK], rowhot[:, j % 4, i, :], colhot[:, j % 4, i, :], start=True, stop=True)
                        mm.then_inc(free, 1)
                block_steps(work, pe)

            @block.scalar
            def _(act):
                act.sem_inc(kept, 4)
                def work(b, u, m):
                    act.wait_ge(sent[u], m * 16 + 16)
                    for j in range(G4):
                        act.wait_ge(free, b * G4 + j + 5)
                        nc.scalar.copy(grid[:, u, :, 4 * j:4 * j + 4], bank[:, j % 4, :].rearrange("p (t x) -> p x t", t=4)).then_inc(kept, 1)
                block_steps(work, act)

            @block.sync
            def _(sp):
                for u in range(2):
                    sp.sem_inc(sent[u], 16)
                def work(b, u, m):
                    sp.wait_ge(kept, b * G4 + G4 + 4)
                    sp.dma_start(grids[bass.ds(b, 1), :, :, :].rearrange("a p c t -> p (a c t)"), grid[:, u, :, :].rearrange("p c t -> p (c t)")).then_inc(sent[u], 16)
                block_steps(work, sp)
                sp.wait_ge(sent[0], 16 * (TWO + 2))
                sp.wait_ge(sent[1], 16 * (TWO + 1))


GI = 4
NGRP = NK // GI


def peer_experts(nc, name, xT, uT_dram, v_dram, grids, yT):
    HALF = TOK // 2
    with Stage(nc, name) as st:
        sb, sem = st.sb, st.sem
        u = sb("u", [P, 2, GI, KD, NK])
        v = sb("v", [P, 2, GI, D])
        gates = sb("gates", [P, 2, NBLK, GI * BLK])
        act_s = sb("act", [P, 2, TOK])
        w = sb("w", [P, 2, GI, TOK])
        bank = st.banks("bank", 8)
        u_in, v_in, g_in = ([sem(f"{n}_loaded{i}") for i in range(2)] for n in ("u", "v", "gates"))
        dots, gelus, weighed = sem("dots"), sem("gelus"), sem("weighed")
        sums, added = sem("sums"), sem("sums_added")

        with nc.Block() as block:
            @block.sync
            def _(sp):
                def load_u(g, p):
                    sp.dma_start(u[:, p, :, :, :].rearrange("p a b c -> p (a b c)"), uT_dram[bass.ds(g, 1), :, :].rearrange("a p x -> p (a x)")).then_inc(u_in[p], 16)

                def load_rest(g, p):
                    sp.dma_start(gates[:, p, :, :], grids[:, :, bass.ds(g * GI, GI), :].rearrange("b p c t -> p b (c t)")).then_inc(g_in[p], 16)
                    sp.dma_start(v[:, p, :, :].rearrange("p a b -> p (a b)"), v_dram[:, bass.ds(g * GI * D, GI * D)]).then_inc(v_in[p], 16)

                for p in range(2):
                    load_u(p, p)
                    load_rest(p, p)
                with sp.Fori(1, NGRP // 2) as m:
                    for p in range(2):
                        sp.wait_ge(dots, (m * 2 + p - 1) * GI)
                        load_u(m * 2 + p, p)
                        sp.wait_ge(sums, (m * 2 + p - 1) * KD)
                        load_rest(m * 2 + p, p)

            def halves(eng, first, second):
                first(0, 0, 0, True)
                with eng.Fori(0, NGRP // 2 - 1) as m:
                    first(m * 2 + 1, 1, m, False)
                    second(m * 2, 0, m)
                    first(m * 2 + 2, 0, m + 1, False)
                    second(m * 2 + 1, 1, m)
                first(NGRP - 1, 1, NGRP // 2 - 1, False)
                second(NGRP - 2, 0, NGRP // 2 - 1)
                second(NGRP - 1, 1, NGRP // 2 - 1)

            @block.tensor
            def _(pe):
                def first(g, p, m, start):
                    pe.wait_ge(u_in[p], m * 16 + 16)
                    for j in range(GI):
                        if not start or j >= 2:
                            pe.wait_ge(gelus, g * GI + j - 1)
                        for i in range(2):
                            for k in range(KD):
                                mm = nc.tensor.matmul(bank[:, 2 * (j % 2) + i, 0:HALF], u[:, p, j, k, :], xT[:, k, i * HALF:(i + 1) * HALF],
                                                      start=k == 0, stop=k == KD - 1)
                        mm.then_inc(dots, 1)

                def second(g, p, m):
                    pe.wait_ge(v_in[p], m * 16 + 16)
                    pe.wait_ge(weighed, g * GI + GI)
                    for c in range(KD):
                        pe.wait_ge(added, g * KD + c + 1)
                        for i in range(2):
                            for j in range(GI):
                                mm = nc.tensor.matmul(bank[:, 4 + 2 * (c % 2) + i, 0:HALF], v[:, p, j, c * P:(c + 1) * P], w[:, p, j, i * HALF:(i + 1) * HALF],
                                                      start=j == 0, stop=j == GI - 1)
                        mm.then_inc(sums, 1)
                halves(pe, first, second)

            @block.scalar
            def _(act):
                def first(g, p, m, start):
                    for j in range(GI):
                        act.wait_ge(dots, g * GI + j + 1)
                        if not start or j >= 2:
                            act.wait_ge(weighed, g * GI + j - 1)
                        nc.scalar.activation(act_s[:, j % 2, :].rearrange("p (a x) -> p a x", a=2), bank[:, 2 * (j % 2):2 * (j % 2) + 2, 0:HALF],
                                             ACT.Gelu).then_inc(gelus, 1)
                halves(act, first, lambda g, p, m: None)

            @block.vector
            def _(dve):
                for i in range(2):
                    nc.vector.memset(yT[:, 4 * i:4 * i + 4, :], 0.0).then_inc(added, 1)

                def first(g, p, m, start):
                    dve.wait_ge(g_in[p], m * 16 + 16)
                    for j in range(GI):
                        dve.wait_ge(gelus, g * GI + j + 1)
                        nc.vector.tensor_tensor(w[:, p, j, :].rearrange("p (b t) -> p b t", t=BLK), act_s[:, j % 2, :].rearrange("p (b t) -> p b t", t=BLK),
                                                gates[:, p, :, j * BLK:(j + 1) * BLK], ALU.mult).then_inc(weighed, 1)

                def second(g, p, m):
                    for c in range(KD):
                        dve.wait_ge(sums, g * KD + c + 1)
                        y = yT[:, c, :].rearrange("p (a x) -> p a x", a=2)
                        nc.vector.tensor_tensor(y, y, bank[:, 4 + 2 * (c % 2):6 + 2 * (c % 2), 0:HALF], ALU.add).then_inc(added, 1)
                halves(dve, first, second)


def peer_norm(nc, name, C, yT, gain_dram, shift_dram, x):
    with Stage(nc, name) as st:
        gain, shift = st.sb("gain", [P, D]), st.sb("shift", [P, D])
        pad = st.sb("pad", [P, KD, P])
        stats, mv = st.sb("stats", [P, 2, 6]), st.sb("mv", [P, 6])
        bank = st.banks("bank", 4)
        here, padded = st.sem("rows_loaded"), st.sem("samples_padded")
        turned, added = st.sem("turned"), st.sem("residual_added")
        s_sum, s_root, s_norm, chain = st.sem("statistics"), st.sem("deviation"), st.sem("normed"), st.sem("vector_chain")
        with nc.Block() as block:
            @block.sync
            def _(sp):
                sp.dma_start(gain[:, :], gain_dram.partition_broadcast(P)).then_inc(here, 16)
                sp.dma_start(shift[:, :], shift_dram.partition_broadcast(P)).then_inc(here, 16)

            @block.gpsimd
            def _(pool):
                nc.gpsimd.memset(pad[:, :, :], 0.0).then_inc(padded, 1)
                pool.wait_ge(padded, 1)
                nc.gpsimd.tensor_copy(pad[:, :, :].rearrange("p k (b s) -> p k b s", s=SEG)[:, :, :, 1:1 + NS],
                                      yT[:, :, SEQ:TOK].rearrange("p k (b s) -> p k b s", s=NS)).then_inc(padded, 1)

            @block.tensor
            def _(pe):
                for t in range(TILES):
                    if t == SAMP:
                        pe.wait_ge(padded, 2)
                    if t >= 2:
                        pe.wait_ge(added, t - 1)
                    for k in range(KD):
                        src = yT[:, k, t * P:(t + 1) * P] if t < SAMP else pad[:, k, :]
                        mm = nc.tensor.transpose(bank[:, 2 * (t % 2) + k // 4, k % 4 * P:(k % 4 + 1) * P], src, C["ident"])
                    mm.then_inc(turned, 1)

            @block.scalar
            def _(act):
                for t in range(TILES):
                    layer_norm_scalar(nc, act, x, t, s_sum, s_root, s_norm, mv)

            @block.vector
            def _(dve):
                ch = Chain(dve, chain)
                dve.wait_ge(here, 32)
                for t in range(TILES):
                    dve.wait_ge(turned, t + 1)
                    nc.vector.scalar_tensor_tensor(out=x[:, t, :], in0=x[:, t, :], scalar=ALPHA,
                                                   in1=bank[:, 2 * (t % 2):2 + 2 * (t % 2), :].rearrange("p a b -> p (a b)"),
                                                   op0=ALU.mult, op1=ALU.add).then_inc(added, 1)
                    dve.wait_ge(added, t + 1)
                    layer_norm_vector(nc, dve, ch, x, t, s_sum, s_root, s_norm, stats, mv, gain[:, :], shift[:, :])


def mlstm(nc, C, A, proj, mix, O):
    VA = DV + 1
    PB = 3
    with Stage(nc, "mlstm") as st:
        sb, sem = st.sb, st.sem
        bias = sb("bias", [P, 2 * H])
        mh = sb("mh", [P, H * DV])
        g16, g16b = sb("g16", [P, 2 * H]), sb("g16b", [P, 2 * H])
        lf, e, m, mu_b = sb("lf", [P, H]), sb("e", [P, H]), sb("m", [P, H]), sb("mu_b", [P, 2 * H])
        mx, ml_bl = sb("mx", [P, H]), sb("ml_bl", [P, 2 * H])
        ex_in, ex = sb("ex_in", [P, 4, H]), sb("ex", [P, 4, H])
        Em = sb("Em", [P, H, P])
        big = sb("big", [P, H, P])
        qT, kT, qpT = (sb(n, [P, PAIRS, P]) for n in ("qT", "kT", "qpT"))
        attT = sb("attT", [P, H, P])
        qp, kw = sb("qp", [P, AW]), sb("kw", [P, AW])
        va = sb("va", [P, H, VA])
        den = sb("den", [P, 3, H])
        ms = sb("ms", [P, 3, H])
        Sp = sb("Sp", [P, PAIRS, VA])
        Ss = sb("Ss", [P, NB, PAIRS, VA])
        dsel, dec = sb("dsel", [P, NB, H]), sb("dec", [P, NB, H])
        bank = st.banks("bank", 8)
        here, init = sem("arrays_loaded"), sem("state_zeroed")
        pre, cap, cap2, em, ln = sem("gate_sums"), sem("gate_tanh"), sem("gates_capped"), sem("forget_exp"), sem("forget_log")
        lf_ok, cum, diag, ebc, mu_ok, lastr = sem("log_forget"), sem("cumulated"), sem("diagonals"), sem("e_spread"), sem("mu_ready"), sem("last_rows")
        emx, exq, exs = sem("score_exponents"), sem("small_exponents"), sem("exps")
        qk_t, qk_tk, qk, att, att_t, att_tk = sem("qk_turned"), sem("qk_turned_kept"), sem("qk_products"), sem("weights_ready"), sem("weights_turned"), sem("weights_turned_kept")
        qp_ok, num, sig, ms_ok, root = sem("scaled_ready"), sem("numerators"), sem("output_gates"), sem("mean_squares"), sem("roots")
        spread, spread_used, stp, tile_ok, dsel_ok = sem("spread_ready"), sem("spread_used"), sem("state_products"), sem("tile_done"), sem("decay_rows")
        chain, outs, dcol = sem("vector_chain"), sem("outputs_stored"), sem("decays_spread")
        NUM = ((5, 6), (7, 0))
        hb = lambda h: bank[:, NUM[h % 2][h // 2 // PB], h // 2 % PB * VA:(h // 2 % PB + 1) * VA]

        with nc.Block() as block:
            @block.sync
            def _(sp):
                for dst, src in ((bias[:, 0:H], A["b_i_o"].partition_broadcast(P)), (bias[:, H:2 * H], A["b_f_o"].partition_broadcast(P)),
                                 (mh[:, :], A["mh_norm_o"].partition_broadcast(P)), (Ss[:, :, :, :], A["cn_s"])):
                    sp.dma_start(dst, src).then_inc(here, 16)
                sp.wait_ge(tile_ok, SAMP)
                sp.dma_start(O["cn_p"], Sp[:, :, :]).then_inc(outs, 16)
                sp.dma_start(O["m_p"], m[:, :]).then_inc(outs, 16)
                sp.wait_ge(outs, 32)
                sp.dma_start(m[:, :], A["m_s"]).then_inc(here, 16)
                sp.wait_ge(tile_ok, TILES)
                sp.dma_start(O["cn_s"], Ss[:, :, :, :]).then_inc(outs, 16)
                sp.dma_start(O["m_s"], m[:, :]).then_inc(outs, 16)
                sp.wait_ge(outs, 64)

            @block.tensor
            def _(pe):
                mmul, turn_ = nc.tensor.matmul, nc.tensor.transpose
                for t in range(TILES):
                    one = t < SAMP
                    q, k = proj[:, t, 0:AW], proj[:, t, AW:2 * AW]
                    if t:
                        pe.wait_ge(tile_ok, t)
                    for i, x in enumerate((q, k)):
                        for p in range(PAIRS):
                            mm = turn_(bank[:, 3 + i, p * P:(p + 1) * P], x[:, p * P:(p + 1) * P], C["ident"])
                    mm.then_inc(qk_t, 1)
                    pe.wait_ge(qk_tk, 2 * (t + 1))
                    for g in range(2):
                        for p in range(PAIRS):
                            mm = mmul(bank[:, 5 + g, p * P:(p + 1) * P], qT[g * 64:(g + 1) * 64, p, :], kT[g * 64:(g + 1) * 64, p, :], start=True, stop=True)
                    mm.then_inc(qk, 1)
                    pe.wait_ge(lf_ok, t + 1)
                    mmul(bank[:, 0, 0:H], C["upto" if one else "upto16"], lf[:, :], start=True, stop=True).then_inc(cum, 1)
                    pe.wait_ge(diag, t + 1)
                    for i in range(2):
                        mm = mmul(bank[:, 1 + i, :], C["ones"], big[:, 4 * i:4 * i + 4, :].rearrange("p a b -> p (a b)"), start=True, stop=True)
                    mm.then_inc(ebc, 1)
                    pe.wait_ge(mu_ok, t + 1)
                    mmul(bank[:, 0, 2 * H:4 * H], C["last" if one else "last_s"], mu_b[:, :], start=True, stop=True).then_inc(lastr, 1)
                    pe.wait_ge(qp_ok, t + 1)
                    for p in range(PAIRS):
                        mm = turn_(bank[:, 3, p * P:(p + 1) * P], qp[:, p * P:(p + 1) * P], C["ident"])
                    mm.then_inc(qk_t, 1)
                    pe.wait_ge(att, t + 1)
                    for h in range(H):
                        mm = turn_(bank[:, 1 + h // 4, h % 4 * P:(h % 4 + 1) * P], big[:, h, :], C["ident"])
                    mm.then_inc(att_t, 1)
                    pe.wait_ge(att_tk, 3 * (t + 1))
                    for h in range(H):
                        p, g = h // 2, h % 2
                        half = slice(g * 64, (g + 1) * 64)
                        mm = mmul(hb(h), attT[:, h, :], va[:, h, :], start=True, stop=False)
                        if one:
                            mm = mmul(hb(h), qpT[half, p, :], Sp[half, p, :], start=False, stop=True)
                        else:
                            if g == 0:
                                pe.wait_ge(spread, p + 1)
                            for b in range(NB):
                                mm = mmul(hb(h), big[half, b, :], Ss[half, b, p, :], start=False, stop=b == NB - 1)
                            if g:
                                mm.then_inc(spread_used, 1)
                    mm.then_inc(num, 1) if one else None
                    if one:
                        for h in range(H):
                            p, g = h // 2, h % 2
                            mm = mmul(bank[g * 64:(g + 1) * 64, 1 + p // PB, p % PB * VA:(p % PB + 1) * VA], kw[:, h * 64:(h + 1) * 64], va[:, h, :], start=True, stop=True)
                        mm.then_inc(stp, 1)
                    else:
                        pe.wait_ge(dsel_ok, 1)
                        mmul(bank[:, 3, 0:NB * H], C["ones"], dsel[:, :, :].rearrange("p a b -> p (a b)"), start=True, stop=True).then_inc(dcol, 1)
                        for p in range(PAIRS):
                            pe.wait_ge(spread, PAIRS + p + 1)
                            for g in range(2):
                                for b in range(NB):
                                    mm = mmul(bank[g * 64:(g + 1) * 64, 1 + b // 2, b % 2 * VA:(b % 2 + 1) * VA], big[:, b, g * 64:(g + 1) * 64], va[:, 2 * p + g, :],
                                              start=True, stop=True)
                            mm.then_inc(stp, 1)

            @block.scalar
            def _(act):
                a_, cp = nc.scalar.activation, nc.scalar.copy
                flat = lambda x: x[:, :, :].rearrange("p a b -> p (a b)")
                for t in range(TILES):
                    act.wait_ge(qk_t, 2 * t + 1)
                    cp(flat(qT), bank[:, 3, :]).then_inc(qk_tk, 1)
                    cp(flat(kT), bank[:, 4, :]).then_inc(qk_tk, 1)
                    act.wait_ge(pre, t + 1)
                    a_(g16b[:, :], g16[:, :], ACT.Tanh, scale=1.0 / CAP).then_inc(cap, 1)
                    act.wait_ge(cap2, t + 1)
                    a_(lf[:, :], g16[:, H:2 * H], ACT.Exp, scale=-1.0).then_inc(em, 1)
                    act.wait_ge(em, 2 * t + 2)
                    a_(lf[:, :], lf[:, :], ACT.Ln).then_inc(ln, 1)
                    act.wait_ge(exq, t + 1)
                    a_(flat(ex), flat(ex_in), ACT.Exp).then_inc(exs, 1)
                    act.wait_ge(emx, t + 1)
                    a_(flat(Em), flat(Em), ACT.Exp).then_inc(exs, 1)
                    act.wait_ge(qk_t, 2 * t + 2)
                    cp(flat(qpT), bank[:, 3, :]).then_inc(att_tk, 1)
                    act.wait_ge(att_t, t + 1)
                    for i in range(2):
                        cp(attT[:, 4 * i:4 * i + 4, :].rearrange("p a b -> p (a b)"), bank[:, 1 + i, :]).then_inc(att_tk, 1)
                    o = proj[:, t, 2 * AW + H * DV:2 * AW + 2 * H * DV]
                    a_(o, o, ACT.Sigmoid).then_inc(sig, 1)
                    act.wait_ge(ms_ok, t + 1)
                    a_(ms[:, 2, :], ms[:, 1, :], ACT.Sqrt).then_inc(root, 1)

            @block.vector
            def _(dve):
                V = nc.vector
                ch = Chain(dve, chain)
                tt, tsc, stt = V.tensor_tensor, V.tensor_scalar, V.scalar_tensor_tensor
                flat = lambda x: x.rearrange("p a b -> p (a b)")
                V.memset(va[:, :, DV:VA], 1.0)
                ch(V.memset(Sp[:, :, :], 0.0))
                ch(V.memset(m[:, :], 0.0))
                dve.wait_ge(here, 64)
                for t in range(TILES):
                    one = t < SAMP
                    q, k, v = proj[:, t, 0:AW], proj[:, t, AW:2 * AW], proj[:, t, 2 * AW:2 * AW + H * DV]
                    gates = proj[:, t, INO - 2 * H:INO]
                    h3 = lambda x: x.rearrange("p (h d) -> p h d", h=H)
                    if not one:
                        dve.wait_ge(here, 80)
                    tt(g16[:, :], gates, bias[:, :], ALU.add).then_inc(pre, 1)
                    V.tensor_copy(va[:, :, 0:DV], h3(v))
                    dve.wait_ge(cap, t + 1)
                    tsc(g16[:, :], g16b[:, :], CAP, None, ALU.mult).then_inc(cap2, 1)
                    dve.wait_ge(em, 2 * t + 1)
                    tsc(lf[:, :], lf[:, :], 1.0, None, ALU.add).then_inc(em, 1)
                    dve.wait_ge(ln, t + 1)
                    if not one:
                        ch(tsc(lf[:, :], lf[:, :], C["real"], None, ALU.mult))
                    tsc(lf[:, :], lf[:, :], -1.0, None, ALU.mult).then_inc(lf_ok, 1)
                    dve.wait_ge(cum, t + 1)
                    ch(V.tensor_copy(mu_b[:, H:2 * H], bank[:, 0, 0:H]))
                    ch(tt(e[:, :], g16[:, 0:H], mu_b[:, H:2 * H], ALU.subtract))
                    tt(big[:, :, :], mid(C["ident"], H), last(e[:, :], P), ALU.mult).then_inc(diag, 1)
                    dve.wait_ge(ebc, t + 1)
                    ch(tt(Em[:, :, :], bank[:, 1:3, :].rearrange("p a (h x) -> p (a h) x", x=P), mid(C["causal" if one else "causal_s"], H), ALU.add))
                    ch(V.tensor_reduce(mx[:, :], Em[:, :, :], AX, ALU.max))
                    tt(mu_b[:, 0:H], mx[:, :], m[:, :], ALU.max).then_inc(mu_ok, 1)
                    dve.wait_ge(mu_ok, t + 1)
                    tt(Em[:, :, :], Em[:, :, :], last(mu_b[:, 0:H], P), ALU.subtract).then_inc(emx, 1)
                    tt(ex_in[:, 0, :], m[:, :], mu_b[:, 0:H], ALU.subtract)
                    stt(ex_in[:, 1, :], mu_b[:, 0:H], -1.0, mu_b[:, H:2 * H], ALU.mult, ALU.subtract)
                    dve.wait_ge(lastr, t + 1)
                    ch(V.tensor_copy(ml_bl[:, :], bank[:, 0, 2 * H:4 * H]))
                    tt(ex_in[:, 2, :], e[:, :], ml_bl[:, 0:H], ALU.subtract)
                    tt(ex_in[:, 3, :], m[:, :], ml_bl[:, 0:H], ALU.subtract).then_inc(exq, 1)
                    dve.wait_ge(exq, t + 1)
                    tt(m[:, :], ml_bl[:, 0:H], ml_bl[:, H:2 * H], ALU.add)
                    dve.wait_ge(exs, 2 * (t + 1))
                    stt(h3(qp[:, :]), h3(q), HD ** -0.5, last(ex[:, 0, :], 64), ALU.mult, ALU.mult).then_inc(qp_ok, 1)
                    if not one:
                        ch(tsc(ex[:, 2, :], ex[:, 2, :], C["real"], None, ALU.mult))
                    ch(tt(h3(kw[:, :]), h3(k), last(ex[:, 2, :], 64), ALU.mult))
                    dve.wait_ge(qk, t + 1)
                    b4 = big[:, :, :].rearrange("p (q g) x -> p q g x", g=2)
                    e4 = Em[:, :, :].rearrange("p (q g) x -> p q g x", g=2)
                    for g in range(2):
                        ins = stt(b4[:, :, g, :], bank[:, 5 + g, :].rearrange("p (q x) -> p q x", x=P), HD ** -0.5, e4[:, :, g, :], ALU.mult, ALU.mult)
                    ins.then_inc(att, 1)
                    if not one:
                        dve.wait_ge(att_tk, 3 * (t + 1))
                        for p in range(PAIRS):
                            if p:
                                dve.wait_ge(spread_used, p)
                            tt(big[:, :, :], mid(qpT[:, p, :], NSEG), C["seg_of_col"].rearrange("p (c x) -> p c x", x=P), ALU.mult).then_inc(spread, 1)
                        dve.wait_ge(spread_used, PAIRS)
                        tt(dsel[:, :, :], mid(ex[:, 3, :], NB), last(C["newest"], H), ALU.mult).then_inc(dsel_ok, 1)
                        dve.wait_ge(dcol, 1)
                        ch(V.tensor_copy(flat(dec[:, :, :]), bank[:, 3, 0:NB * H]))
                        for p in range(PAIRS):
                            tt(big[:, :, :], mid(kw[:, p * P:(p + 1) * P], NSEG), last(C["seg_of_row"], P), ALU.mult).then_inc(spread, 1)
                            for g in range(2):
                                half = slice(g * 64, (g + 1) * 64)
                                ins = tt(Ss[half, :, p, :], Ss[half, :, p, :], dec[half, :, 2 * p + g:2 * p + g + 1].to_broadcast([64, NB, VA]), ALU.mult)
                            ch(ins)
                            dve.wait_ge(stp, SAMP + p + 1)
                            s4 = Ss[:, :, p, :].rearrange("p (a c) x -> p a c x", c=2)
                            ch(tt(s4, s4, bank[:, 1:5, 0:2 * VA].rearrange("p a (c x) -> p a c x", x=VA), ALU.add))
                    else:
                        dve.wait_ge(num, t + 1)
                        dve.wait_ge(stp, t + 1)
                        for h in range(H):
                            p, g = h // 2, h % 2
                            half = slice(g * 64, (g + 1) * 64)
                            ins = stt(Sp[half, p, :], Sp[half, p, :], ex[half, 3, h:h + 1], bank[half, 1 + p // PB, p % PB * VA:(p % PB + 1) * VA], ALU.mult, ALU.add)
                        ch(ins)
                    for h in range(H):
                        ins = V.tensor_copy(den[:, 0, h:h + 1], hb(h)[:, DV:VA])
                    ch(ins)
                    ch(tsc(den[:, 1, :], den[:, 0, :], -1.0, None, ALU.mult))
                    ch(tt(den[:, 0, :], den[:, 0, :], den[:, 1, :], ALU.max))
                    ch(tt(den[:, 0, :], den[:, 0, :], ex[:, 1, :], ALU.max))
                    ch(V.reciprocal(den[:, 2, :], den[:, 0, :]))
                    d4 = den[:, 2, :].rearrange("p (q g) -> p q g", g=2)
                    for g in range(2):
                        for i, n in enumerate((PB, PAIRS - PB)):
                            a = slice(i * PB, i * PB + n)
                            ins = tt(e4[:, a, g, :], bank[:, NUM[g][i], 0:n * VA].rearrange("p (q x) -> p q x", x=VA)[:, :, 0:DV], last(d4[:, a, g], DV), ALU.mult)
                    ch(ins)
                    ch(tt(big[:, :, :], Em[:, :, :], Em[:, :, :], ALU.mult))
                    ch(V.tensor_reduce(ms[:, 0, :], big[:, :, :], AX, ALU.add))
                    tsc(ms[:, 1, :], ms[:, 0, :], 1.0 / DV, 1e-6, ALU.mult, ALU.add).then_inc(ms_ok, 1)
                    dve.wait_ge(root, t + 1)
                    ch(V.reciprocal(ms[:, 0, :], ms[:, 2, :]))
                    ch(tt(Em[:, :, :], Em[:, :, :], last(ms[:, 0, :], DV), ALU.mult))
                    ch(tt(flat(Em[:, :, :]), flat(Em[:, :, :]), mh[:, :], ALU.mult))
                    dve.wait_ge(sig, t + 1)
                    tt(mix[:, t, :], flat(Em[:, :, :]), proj[:, t, 2 * AW + H * DV:2 * AW + 2 * H * DV], ALU.mult).then_inc(tile_ok, 1)
                    dve.wait_ge(tile_ok, t + 1)


def build(nc, A, O):
    with ExitStack() as ctx:
        consts = ctx.enter_context(nc.sbuf_tensor("const_tile", [P, CONST_N], F32))
        C = {k: consts[:, CONST_AT[k]:CONST_AT[k] + w] for k, w in CONST_COLS.items()}
        load(nc, [(consts[:, :], A["consts"])])
        with nc.sbuf_tensor("mix_a", [P, TILES, AW], F32) as mix_a, nc.sbuf_tensor("mix_b", [P, TILES, AW], F32) as mix_b:
            for part, (lo, hi), mixer, mix in ((0, (0, RW), rwkv, mix_a), (1, (RW, INE), mla, mix_b)):
                with nc.sbuf_tensor(f"proj_e{part}", [P, TILES, hi - lo], F32) as proj:
                    with nc.sbuf_tensor(f"xT_e{part}", [P, KD, TILES * P], F32) as xT:
                        load(nc, [(xT[:, :, :], A["xT0"].rearrange("(k p) t -> p k t", p=P))])
                        project(nc, f"in_e{part}", A["w_in_e"][:, lo:hi], hi - lo, xT, proj)
                    mixer(nc, C, A, proj, mix, O)
            with nc.sbuf_tensor("x_e", [P, TILES, D], F32) as x:
                load(nc, [(x[:, :, :], A["x0"].rearrange("(t p) d -> p t d", p=P))])
                half = lambda t, k: (mix_a if k < 4 else mix_b)[:, t, k % 4 * P:(k % 4 + 1) * P]
                out_project(nc, "out_e", C, half, A["w_out_e"], A["ln1_g0"], A["ln1_b0"], x)
                store(nc, [(A["x_mid"].rearrange("(t p) d -> p t d", p=P), x[:, :, :])])
        x = ctx.enter_context(nc.sbuf_tensor("x", [P, TILES, D], F32))
        load(nc, [(x[:, :, :], A["x_mid"].rearrange("(t p) d -> p t d", p=P))])
        peer(nc, 0, C, A, x)
        with nc.sbuf_tensor("mix_o", [P, TILES, D], F32) as mix:
            with nc.sbuf_tensor("proj_o", [P, TILES, INO], F32) as proj:
                with nc.sbuf_tensor("xT_o", [P, KD, TILES * P], F32) as xT:
                    turn(nc, "turn_o", C, x, xT, False)
                    project(nc, "in_o", A["w_in_o"], INO, xT, proj)
                mlstm(nc, C, A, proj, mix, O)
            out_project(nc, "out_o", C, lambda t, k: mix[:, t, k * P:(k + 1) * P], A["w_out_o"], A["ln1_g1"], A["ln1_b1"], x)
        peer(nc, 1, C, A, x)
        store(nc, [(O["y"].rearrange("(t p) d -> p t d", p=P), x[:, :, :]),
                   (O["shift"][0:1, :], A["x0"][SEQ - 1:SEQ, :]),
                   (O["shift"][1:1 + NB, :], A["x0"][SEQ:, :].rearrange("(b s) d -> b s d", s=SEG)[:, NS, :])])


def peer(nc, layer, C, A, x):
    n = str(layer)
    with nc.sbuf_tensor("xT_p" + n, [P, KD, TOK], F32) as xT:
        turn(nc, "turn_p" + n, C, x, xT, True)
        with nc.sbuf_tensor("picks" + n, [P, 3, TOK], F32) as picks:
            peer_select(nc, "select" + n, C, xT, A["wq" + n], A["k1T" + n], A["k2T" + n], picks)
            peer_spread(nc, "spread" + n, C, picks, A["grids"])
        with nc.sbuf_tensor("yT" + n, [P, KD, TOK], F32) as yT:
            peer_experts(nc, "experts" + n, xT, A["uT" + n], A["v" + n], A["grids"], yT)
            peer_norm(nc, "norm" + n, C, yT, A["ln2_g" + n], A["ln2_b" + n], x)


def store(nc, pairs):
    with Stage(nc, f"store{nc.next_id()}") as st:
        sent = st.sem("arrays_stored")
        with nc.Block() as block:
            @block.sync
            def _(sp):
                for dst, src in pairs:
                    sp.dma_start(dst, src).then_inc(sent, 16)
                sp.wait_ge(sent, 16 * len(pairs))


def load(nc, pairs):
    with Stage(nc, f"load{nc.next_id()}") as st:
        here = st.sem("arrays_loaded")
        with nc.Block() as block:
            @block.sync
            def _(sp):
                for dst, src in pairs:
                    sp.dma_start(dst, src).then_inc(here, 16)
                sp.wait_ge(here, 16 * len(pairs))


def layouts(i):
    f = lambda a: np.ascontiguousarray(a)
    pad = np.zeros((NB, SEG, D), np.float32)
    pad[:, 0] = i["state_shift"][0]
    pad[:, 1:1 + NS] = i["x_sample"]
    x0 = np.concatenate([i["x_prompt"][0], pad.reshape(P, D)], 0)
    a = {"x0": x0, "xT0": f(x0.T)}
    for n in ("w_in_e", "mu_e", "w0_e", "w2_e", "a0_e", "a2_e", "g2_e", "kk_e", "ka_e", "lnx_w_e", "lnx_b_e"):
        a[n] = i[n][0]
    a["rk_e"] = i["rk_e"][0].reshape(-1)
    w = np.zeros((NB, PAIRS, 2, HD, 2, HD), np.float32)
    s = i["state_wkv"][0].reshape(NB, PAIRS, 2, HD, HD)
    for g in range(2):
        w[:, :, g, :, g, :] = s[:, :, g].transpose(0, 1, 3, 2)
    a["wkv_s"] = w.reshape(NB, PAIRS, P, P)
    a["w_uq_e"], a["q_norm_e"], a["kv_norm_e"] = i["w_uq_e"][0], i["q_norm_e"][0], i["kv_norm_e"][0]
    a["w_uk_e"], a["w_uv_e"] = i["w_uk_e"][0].reshape(KV, -1), i["w_uv_e"][0].reshape(KV, -1)
    a["w_ukT_e"] = f(i["w_uk_e"][0].transpose(2, 1, 0))
    a["page_table"] = i["page_table"].reshape(1, -1)
    c = i["cache_ckv"][0]
    a["cache_ckv"] = c
    a["keysT"] = f(c.reshape(-1, PAGE, 2, P).transpose(0, 3, 2, 1)).reshape(-1, P, 2 * PAGE)
    a["kpesT"] = f(i["cache_kpe"][0].transpose(0, 2, 1))
    a["w_out_e"], a["w_in_o"], a["w_out_o"] = i["w_out_e"][0], i["w_in_o"][0], i["w_out_o"][0]
    for l in range(2):
        n = str(l)
        for k in ("ln1_g", "ln1_b", "ln2_g", "ln2_b"):
            a[k + n] = i[k][l]
        a["wq" + n], a["k1T" + n], a["k2T" + n] = i["peer_wq"][l], f(i["peer_k1"][l].T), f(i["peer_k2"][l].T)
        u = i["peer_u"][l].reshape(NK, NGRP, GI, KD, P)
        a["uT" + n] = f(u.transpose(1, 4, 2, 3, 0)).reshape(NGRP, P, GI * KD * NK)
        a["v" + n] = i["peer_v"][l].reshape(NK, NK * D)
    a["b_i_o"], a["b_f_o"], a["mh_norm_o"] = i["b_i_o"][0], i["b_f_o"][0], i["mh_norm_o"][0]
    cn = np.concatenate([i["state_mlstm_c"][0], i["state_mlstm_n"][0][:, :, None, :]], 2)
    cn = cn.reshape(NB, PAIRS, 2, DV + 1, HD).transpose(2, 4, 0, 1, 3)
    a["cn_s"] = f(cn).reshape(P, NB, PAIRS, DV + 1)
    a["m_s"] = np.repeat(i["state_mlstm_m"][0], SEG, axis=0)
    a["consts"] = np.concatenate(list(constants().values()), 1)
    return a


OUTPUTS = {"cn_p": (P, PAIRS, DV + 1), "cn_s": (P, NB, PAIRS, DV + 1), "m_p": (P, H), "m_s": (P, H), "y": (TILES * P, D), "shift": (1 + NB, D), "ckv": (TILES * P, KV), "kpe": (TILES * P, RP), "wkv_p": (PAIRS, P, P), "wkv_s": (PAIRS, NB, P, P)}
SCRATCH = {"x_mid": (TILES * P, D), "grids": (NBLK, P, NK, BLK), "new_rows": (P, KV), "last_rows": (1, SAMP, RW)}


def kernel(**inputs):
    from concourse import bacc
    from concourse.bass_utils import run_bass_kernel_spmd

    given = layouts({k: np.asarray(v) for k, v in inputs.items()})
    nc = bacc.Bacc("TRN2", target_bir_lowering=False, num_devices=1)
    A, O, arrays = {}, {}, {}
    for n, v in given.items():
        arrays["in_" + n] = np.ascontiguousarray(v)
        A[n] = nc.dram_tensor("in_" + n, v.shape, mybir.dt.from_np(v.dtype), kind="ExternalInput").ap()
    for n, shape in SCRATCH.items():
        A[n] = nc.dram_tensor("scratch_" + n, shape, F32, kind="Internal").ap()
    for n, shape in OUTPUTS.items():
        O[n] = nc.dram_tensor("out_" + n, shape, F32, kind="ExternalOutput").ap()
    build(nc, A, O)
    r = run_bass_kernel_spmd(nc, [arrays], core_ids=[0]).results[0]
    got = {n: np.asarray(r["out_" + n]) for n in OUTPUTS}

    def rows(a):
        return a[:SEQ][None], a[SEQ:].reshape(NB, SEG, -1)[:, 1:1 + NS]

    def wkv(a):
        a = a.reshape(PAIRS, -1, 2, HD, 2, HD)
        a = np.stack([a[:, :, g, :, g, :] for g in range(2)], 2)
        return a.transpose(1, 0, 2, 4, 3).reshape(-1, H, HD, HD)[None]

    def cell(a):
        a = a.reshape(2, HD, -1, PAIRS, DV + 1).transpose(2, 3, 0, 4, 1).reshape(-1, H, DV + 1, HD)
        return a[None, :, :, :DV], a[None, :, :, DV]

    y_p, y_s = rows(got["y"])
    ckv_p, ckv_s = rows(got["ckv"])
    kpe_p, kpe_s = rows(got["kpe"])
    c_p, n_p = cell(got["cn_p"])
    c_s, n_s = cell(got["cn_s"])
    out = (y_p, y_s, ckv_p[None], kpe_p[None], ckv_s[None], kpe_s[None],
           got["shift"][None, 0:1], got["shift"][None, 1:], wkv(got["wkv_p"][:, None]), wkv(got["wkv_s"]),
           c_p, c_s, n_p, n_s, got["m_p"][None, 0:1], got["m_s"][None, ::SEG])
    return tuple(np.ascontiguousarray(a) for a in out)
```

```python
from contextlib import ExitStack

import numpy as np
import concourse.bass as bass
from concourse import mybir

ALU = mybir.AluOpType
ACT = mybir.ActivationFunctionType
F32 = mybir.dt.float32
U32 = mybir.dt.uint32
AX = mybir.AxisListType.X

P = 128
D = 1024
KD = D // P
SEQ = 512
NB = 8
NS = 4
TILES = SEQ // P + 1
SAMP = TILES - 1
SEG = 16
NSEG = P // SEG
TOK = SEQ + NB * NS
H = 8
HD = 64
AW = H * HD
PAIRS = H // 2
RW = 3 * AW + 64 + 64 + 128
QL, KV, RP = 384, 256, 32
INE = RW + QL + KV + RP
DV = 128
INO = 2 * AW + 2 * H * DV + 2 * H
NPAGE, PAGE = 32, 128
PAST = NPAGE * PAGE
ALPHA = 4.0 ** 0.25
SM = (64 + 32) ** -0.5
NEG = -1.0e30
NK = 128
PH, PK = 8, 16
HK = PH * PK
CAP = 15.0



def constants():
    r = np.arange(P)
    row, col = r[:, None], r[None, :]
    same = row // SEG == col // SEG
    real = (r % SEG >= 1) & (r % SEG <= NS)
    c = {}
    c["ident"] = row == col
    c["iota"] = np.broadcast_to(col, (P, P))
    c["upto16"] = same & (row <= col)
    c["before16"] = same & (row < col)
    c["after16"] = same & (row > col)
    c["upto"] = row <= col
    c["pair"] = row // HD == col // HD
    c["seg_of_row"] = row // SEG == np.arange(NSEG)[None, :]
    c["seg_of_col"] = np.broadcast_to((np.arange(NSEG)[:, None] == r[None, :] // SEG).reshape(1, -1), (P, NSEG * P))
    c["real"] = real[:, None]
    c["ones"] = np.ones((P, P))
    c["negc"] = np.full((P, 1), -np.exp(-0.5))
    c["negc_real"] = real[:, None] * -np.exp(-0.5)
    c["causal"] = np.where(col <= row, 0.0, NEG)
    c["causal_s"] = np.where(same & (col <= row) & real[None, :], 0.0, NEG)
    c["last"] = (row == P - 1) & (col >= 0)
    c["last_s"] = row == SEG * (col // SEG) + NS
    c["newest"] = (row == SEG * np.arange(NSEG)[None, :] + NS)
    pos = np.concatenate([np.arange(SEQ), PAST + np.arange(P) % SEG - 1.0])
    inv = (np.float32(10000.0) ** (-np.arange(0, RP, 2, dtype=np.float32) / np.float32(RP))).astype(np.float32)
    ang = pos.astype(np.float32)[:, None] * inv[None, :]
    lay = lambda a: a.reshape(TILES, P, RP // 2).transpose(1, 0, 2).reshape(P, -1)
    c["cos"], c["sin"] = lay(np.cos(ang)), lay(np.sin(ang))
    q = r % NS
    s = np.arange(SEG)
    c["newmask"] = np.where((s[None, :] >= 1) & (s[None, :] <= q[:, None] + 1), 0.0, NEG)
    return {k: np.ascontiguousarray(v, dtype=np.float32) for k, v in c.items()}


CONST_COLS = {k: v.shape[1] for k, v in constants().items()}
CONST_AT, _n = {}, 0
for _k, _w in CONST_COLS.items():
    CONST_AT[_k] = _n
    _n += _w
CONST_N = _n


class Stage:

    def __init__(self, nc, name):
        self.nc, self.name, self.ctx, self.sems = nc, name, ExitStack(), []

    def sb(self, name, shape, dt=F32):
        return self.ctx.enter_context(self.nc.sbuf_tensor(f"{self.name}_{name}", shape, dt))

    def banks(self, name, n=1):
        return self.ctx.enter_context(self.nc.psum_tensor(f"{self.name}_{name}", [P, n, 512], F32))

    def sem(self, name):
        s = self.nc.alloc_semaphore(f"{self.name}_{name}")
        self.sems.append(s)
        return s

    def __enter__(self):
        return self

    def __exit__(self, *exc):
        self.ctx.close()
        if exc[0] is None:
            self.nc.clear_and_free_semaphores(self.sems)
            self.nc.all_engine_barrier()
        return False


class Chain:

    def __init__(self, eng, sem):
        self.eng, self.sem, self.n = eng, sem, 0

    def __call__(self, ins):
        self.n += 1
        ins.then_inc(self.sem, 1)
        self.eng.wait_ge(self.sem, self.n)


def mid(ap, n):
    return ap.unsqueeze(1).to_broadcast([ap.shape[0], n, ap.shape[1]])


def last(ap, n):
    return ap.unsqueeze(2).to_broadcast([ap.shape[0], ap.shape[1], n])


def project(nc, name, w_dram, n_cols, xT, out):
    chunks = [(a, min(512, n_cols - a)) for a in range(0, n_cols, 512)]
    with Stage(nc, name) as st:
        w = st.sb("w", [P, 2, KD, 512])
        acc = st.banks("acc", 4)
        w_in = [st.sem(f"w_loaded{i}") for i in range(2)]
        tile_done = st.sem("tile_multiplied")
        kept = [st.sem("kept_by_vector"), st.sem("kept_by_scalar")]
        wv = w_dram.rearrange("(k p) n -> p k n", p=P)
        with nc.Block() as block:
            @block.sync
            def _(sp):
                for n, (a, m) in enumerate(chunks):
                    if n >= 2:
                        sp.wait_ge(tile_done, TILES * (n - 1))
                    sp.dma_start(w[:, n % 2, :, 0:m], wv[:, :, a:a + m]).then_inc(w_in[n % 2], 16)

            @block.tensor
            def _(pe):
                for n, (a, m) in enumerate(chunks):
                    pe.wait_ge(w_in[n % 2], 16 * (n // 2 + 1))
                    for t in range(TILES):
                        i = n * TILES + t
                        if i >= 4:
                            pe.wait_ge(kept[i % 2], (i - 4) // 2 + 1)
                        for k in range(KD):
                            mm = nc.tensor.matmul(acc[:, i % 4, 0:m], xT[:, k, t * P:(t + 1) * P],
                                                  w[:, n % 2, k, 0:m], start=k == 0, stop=k == KD - 1)
                        mm.then_inc(tile_done, 1)

            def keep(eng, copy, par):
                for n, (a, m) in enumerate(chunks):
                    for t in range(TILES):
                        i = n * TILES + t
                        if i % 2 == par:
                            eng.wait_ge(tile_done, i + 1)
                            copy(out[:, t, a:a + m], acc[:, i % 4, 0:m]).then_inc(kept[par], 1)

            @block.vector
            def _(dve):
                keep(dve, nc.vector.tensor_copy, 0)

            @block.scalar
            def _(act):
                keep(act, nc.scalar.copy, 1)


def rwkv(nc, C, A, proj, mix, O):
    with Stage(nc, "rwkv") as st:
        sb, sem = st.sb, st.sem
        names = ["mu", "w0", "a0", "kk", "ka", "rk", "lnw", "lnb"]
        width = {"mu": RW}
        row = {n: sb("row_" + n, [P, width.get(n, AW)]) for n in names}
        wa2 = sb("wa2", [P, AW])
        g2 = sb("g2", [P, AW])
        lwaT = sb("lwaT", [P, P])
        lgT = sb("lgT", [P, P])
        a_s = sb("a", [P, AW])
        z_s = sb("z", [P, AW])
        g_s = sb("g", [P, AW])
        logd = sb("logd", [P, AW])
        kk = sb("kk", [P, AW])
        kp = sb("kp", [P, AW])
        tmp = sb("tmp", [P, 2 * AW])
        nrm = sb("nrm", [P, 4, H])
        e_in, e_neg, e_ex, e_rev = (sb(n, [P, AW]) for n in ("e_in", "e_neg", "e_ex", "e_rev"))
        e_chunk = sb("e_chunk", [P, PAIRS * NSEG])
        at, bt, kt, rt = e_ex, e_neg, sb("kt", [P, AW]), e_in
        bend, kend = e_rev, sb("kend", [P, AW])
        atT, btT, ktT, rtT = (sb(n, [P, PAIRS, P]) for n in ("atT", "btT", "ktT", "rtT"))
        mats = sb("mats", [P, 8, PAIRS, P])
        M, MT, M2, M2T, KAT, RBT, RKT, R = (mats[:, i, :, :] for i in range(8))
        bexp, kexp = (mats[:, i:i + 2, :, :].rearrange("p a b c -> p (a b) c") for i in (0, 2))
        Wp, U0 = (sb(n, [P, PAIRS, 2, HD]) for n in ("Wp", "U0"))
        GT = sb("GT", [P, PAIRS, P])
        y0 = sb("y0", [P, H, HD])
        Pbd, Qbd = (sb(n, [P, PAIRS, NSEG, P]) for n in ("Pbd", "Qbd"))
        prev = Pbd[:, :, :, :].rearrange("p a b c -> p (a b c)")[:, 0:RW]
        S = sb("S", [P, NSEG + 1, PAIRS, P])
        bank = st.banks("bank", 8)

        rows_in, prev_in, s_in = sem("rows_loaded"), sem("previous_rows"), sem("sample_states_loaded")
        prev_zero, last_in = sem("previous_zeroed"), sem("last_rows_stored")
        mixed, lora_t, lora_in, lora_out = sem("tokens_shifted"), sem("lora_transposed"), sem("lora_inputs"), sem("lora_products")
        gates_z, gates = sem("gate_sums"), sem("gates_ready")
        sq_sum, root = sem("square_sums"), sem("key_norms")
        logd_ok, sums, exps = sem("log_decay"), sem("decay_sums"), sem("decay_exps")
        scaled, turned, turned_kept = sem("scaled"), sem("operands_turned"), sem("turned_kept")
        gram, gram_kept = sem("gram_products"), sem("gram_kept")
        step_pe, step_kept = sem("solve_products"), sem("solve_kept")
        yg, yg_kept = sem("chunk_outputs"), sem("chunk_outputs_kept")
        expd, pq, pq_kept = sem("keys_spread"), sem("transitions"), sem("transitions_kept")
        sc, sc_kept = sem("scan_product"), sem("scan_state")
        gexp, y1, var_ok, dev_ok, out_ok = sem("queries_spread"), sem("state_outputs"), sem("variances"), sem("deviations"), sem("tile_done")
        chain, pchain, out_s, s_used = sem("vector_chain"), sem("pool_chain"), sem("states_stored"), sem("state_seeded")

        with nc.Block() as block:
            @block.sync
            def _(sp):
                for n, src in (("mu", A["mu_e"]), ("w0", A["w0_e"]), ("a0", A["a0_e"]), ("kk", A["kk_e"]),
                               ("ka", A["ka_e"]), ("rk", A["rk_e"]), ("lnw", A["lnx_w_e"]), ("lnb", A["lnx_b_e"])):
                    sp.dma_start(row[n][:, :], src.partition_broadcast(P)).then_inc(rows_in, 16)
                sp.dma_start(wa2[0:64, :], A["w2_e"]).then_inc(rows_in, 16)
                sp.dma_start(wa2[64:128, :], A["a2_e"]).then_inc(rows_in, 16)
                sp.dma_start(g2[:, :], A["g2_e"]).then_inc(rows_in, 16)
                sp.dma_start(A["last_rows"], proj[P - 1:P, 0:SAMP, 0:RW]).then_inc(last_in, 16)
                sp.wait_ge(last_in, 16)
                sp.wait_ge(prev_zero, 1)
                for t in range(TILES):
                    if t:
                        sp.wait_ge(out_ok, t)
                    sp.dma_start(prev[1:P, :], proj[0:P - 1, t, 0:RW]).then_inc(prev_in, 16)
                    if t:
                        sp.dma_start(prev[0:1, :], A["last_rows"][:, t - 1, :]).then_inc(prev_in, 16)
                sp.wait_ge(out_ok, SAMP)
                sp.dma_start(O["wkv_p"].rearrange("q p i -> p q i"), S[:, NSEG, :, :]).then_inc(out_s, 16)
                sp.wait_ge(out_s, 16)
                sp.dma_start(S[:, 0:NSEG, :, :], A["wkv_s"].rearrange("b q p i -> p b q i")).then_inc(s_in, 16)
                sp.wait_ge(out_ok, TILES)
                sp.dma_start(O["wkv_s"].rearrange("q b p i -> p q b i"), Pbd[:, :, :, :]).then_inc(out_s, 16)
                sp.wait_ge(out_s, 32)

            @block.tensor
            def _(pe):
                mmul = nc.tensor.matmul
                pe.wait_ge(rows_in, 16 * 11)
                for t in range(TILES):
                    v = proj[:, t, 2 * AW:3 * AW]
                    pe.wait_ge(mixed, t + 1)
                    if t:
                        pe.wait_ge(out_ok, t)
                    nc.tensor.transpose(bank[:, 0, 0:P], proj[:, t, 3 * AW:3 * AW + P], C["ident"])
                    nc.tensor.transpose(bank[:, 0, P:2 * P], proj[:, t, 3 * AW + P:RW], C["ident"]).then_inc(lora_t, 1)
                    pe.wait_ge(lora_in, 3 * (t + 1))
                    mmul(bank[:, 1, :], lwaT[0:64, :], wa2[0:64, :], start=True, stop=True)
                    mmul(bank[:, 2, :], lwaT[64:P, :], wa2[64:P, :], start=True, stop=True)
                    mmul(bank[:, 3, :], lgT[:, :], g2[:, :], start=True, stop=True).then_inc(lora_out, 1)
                    pe.wait_ge(logd_ok, t + 1)
                    mmul(bank[:, 4, :], C["upto16"], logd[:, :], start=True, stop=True)
                    mmul(bank[:, 5, :], C["before16"], logd[:, :], start=True, stop=True)
                    mmul(bank[:, 6, :], C["after16"], logd[:, :], start=True, stop=True)
                    for q in range(PAIRS):
                        mm = mmul(bank[:, 7, q * NSEG:(q + 1) * NSEG], logd[:, q * P:(q + 1) * P], C["seg_of_row"],
                                  start=True, stop=True)
                    mm.then_inc(sums, 1)
                    pe.wait_ge(scaled, t + 1)
                    pe.wait_ge(gates, 3 * (t + 1))
                    for i, x in enumerate((at, bt, kt, rt)):
                        for q in range(PAIRS):
                            mm = nc.tensor.transpose(bank[:, i, q * P:(q + 1) * P], x[:, q * P:(q + 1) * P], C["ident"])
                    mm.then_inc(turned, 1)
                    for g in range(2):
                        n = 2 * t + g
                        half = slice(g * HD, (g + 1) * HD)
                        pe.wait_ge(turned_kept, 4 * (t + 1))
                        if g:
                            pe.wait_ge(yg_kept, 2 * n)
                        for i, (x, y) in enumerate(((atT, btT), (btT, atT), (ktT, atT), (btT, rtT), (ktT, rtT))):
                            for q in range(PAIRS):
                                mm = mmul(bank[:, i, q * P:(q + 1) * P], x[half, q, :], y[half, q, :], start=True, stop=True)
                            mm.then_inc(gram, 1)
                        hd = lambda x, q: x[:, (2 * q + g) * HD:(2 * q + g + 1) * HD]
                        pe.wait_ge(gram_kept, 6 * n + 4)
                        for q in range(PAIRS):
                            mm = mmul(bank[:, 5, q * HD:(q + 1) * HD], KAT[:, q, :], hd(v, q), start=True, stop=True)
                        mm.then_inc(step_pe, 1)
                        pe.wait_ge(step_kept, 6 * n + 1)
                        seq = ((MT, M, M2, M2T), (M2T, M2, M, MT), (MT, M, M2, M2T))
                        for s, (xT, x, nx, nxT) in enumerate(seq):
                            for q in range(PAIRS if s < 2 else 0):
                                mmul(bank[:, 0, q * P:(q + 1) * P], xT[:, q, :], x[:, q, :], start=True, stop=True)
                            for q in range(PAIRS):
                                mmul(bank[:, 1, q * P:(q + 1) * P], x[:, q, :], xT[:, q, :], start=True, stop=True)
                            for q in range(PAIRS):
                                mm = mmul(bank[:, 2, q * P:(q + 1) * P], xT[:, q, :], R[:, q, :], start=True, stop=True)
                            mm.then_inc(step_pe, 1)
                            pe.wait_ge(step_kept, 6 * n + 2 + s)
                        for q in range(PAIRS):
                            mm = mmul(bank[:, 3, q * P:(q + 1) * P], M2T[:, q, :], R[:, q, :], start=True, stop=True)
                        mm.then_inc(step_pe, 1)
                        pe.wait_ge(step_kept, 6 * n + 6)
                        for q in range(PAIRS):
                            mmul(bank[half, 4, q * P:(q + 1) * P], Wp[:, q, g, :], RBT[:, q, :], start=True, stop=True)
                        for q in range(PAIRS):
                            mmul(bank[:, 5, q * HD:(q + 1) * HD], RBT[:, q, :], U0[:, q, g, :], start=True, stop=False)
                            mm = mmul(bank[:, 5, q * HD:(q + 1) * HD], RKT[:, q, :], hd(v, q), start=False, stop=True)
                        mm.then_inc(yg, 1)
                    for q in range(PAIRS):
                        n = PAIRS * t + q
                        pe.wait_ge(expd, 2 * (n + 1))
                        pe.wait_ge(pq_kept, 4 * n) if n else None
                        pe.wait_ge(yg_kept, 4 * (t + 1))
                        wq = Wp[:, q, :, :].rearrange("p a b -> p (a b)")
                        uq = U0[:, q, :, :].rearrange("p a b -> p (a b)")
                        for i in range(2):
                            mm = mmul(bank[:, i, :], wq, bexp[:, 4 * i:4 * i + 4, :].rearrange("p a b -> p (a b)"), start=True, stop=True)
                        for c in range(NSEG):
                            o = bank[:, 2 + c // 4, (c % 4) * P:(c % 4 + 1) * P]
                            mmul(o, bexp[:, c, :], uq, start=True, stop=False)
                            mm = mmul(o, kexp[:, c, :], v[:, q * P:(q + 1) * P], start=False, stop=True)
                        mm.then_inc(pq, 1)
                    for c in range(NSEG):
                        n = NSEG * t + c
                        pe.wait_ge(pq_kept, 4 * PAIRS * (t + 1))
                        if n:
                            pe.wait_ge(sc_kept, n)
                        if c == 0 and t < SAMP:
                            pe.wait_ge(s_used, t + 1)
                        elif c == 0:
                            pe.wait_ge(s_in, 16)
                        for q in range(PAIRS):
                            mm = mmul(bank[:, 4 + c % 2, q * P:(q + 1) * P], Pbd[:, q, c, :], S[:, c, q, :], start=True, stop=True)
                        mm.then_inc(sc, 1)
                    for q in range(PAIRS):
                        n = PAIRS * t + q
                        pe.wait_ge(gexp, n + 1)
                        for c in range(NSEG):
                            mm = mmul(bank[:, 6, q * P:(q + 1) * P], (bexp if q % 2 == 0 else kexp)[:, c, :], S[:, c, q, :],
                                      start=c == 0, stop=c == NSEG - 1)
                        mm.then_inc(y1, 1)

            @block.scalar
            def _(act):
                a_ = nc.scalar.activation
                for t in range(TILES):
                    act.wait_ge(lora_t, t + 1)
                    a_(lwaT[0:64, :], bank[0:64, 0, 0:P], ACT.Tanh).then_inc(lora_in, 1)
                    nc.scalar.copy(lwaT[64:P, :], bank[64:P, 0, 0:P]).then_inc(lora_in, 1)
                    a_(lgT[:, :], bank[:, 0, P:2 * P], ACT.Sigmoid).then_inc(lora_in, 1)
                    act.wait_ge(lora_out, t + 1)
                    nc.scalar.copy(g_s[:, :], bank[:, 3, :]).then_inc(gates, 1)
                    act.wait_ge(gates_z, 2 * (t + 1))
                    a_(z_s[:, :], z_s[:, :], ACT.Sigmoid).then_inc(gates, 1)
                    a_(a_s[:, :], a_s[:, :], ACT.Sigmoid).then_inc(gates, 1)
                    act.wait_ge(sq_sum, t + 1)
                    a_(nrm[:, 1, :], nrm[:, 0, :], ACT.Sqrt).then_inc(root, 1)
                    act.wait_ge(sums, t + 1)
                    a_(e_in[:, :], bank[:, 4, :], ACT.Exp).then_inc(exps, 1)
                    a_(e_neg[:, :], bank[:, 4, :], ACT.Exp, scale=-1.0).then_inc(exps, 1)
                    a_(e_ex[:, :], bank[:, 5, :], ACT.Exp).then_inc(exps, 1)
                    a_(e_rev[:, :], bank[:, 6, :], ACT.Exp).then_inc(exps, 1)
                    a_(e_chunk[:, :], bank[:, 7, 0:PAIRS * NSEG], ACT.Exp).then_inc(exps, 1)
                    act.wait_ge(turned, t + 1)
                    for i, x in enumerate((atT, btT, ktT, rtT)):
                        nc.scalar.copy(x[:, :, :].rearrange("p a b -> p (a b)"), bank[:, i, :]).then_inc(turned_kept, 1)
                    act.wait_ge(var_ok, t + 1)
                    a_(nrm[:, 1, :], nrm[:, 0, :], ACT.Sqrt).then_inc(dev_ok, 1)

            @block.gpsimd
            def _(pool):
                nc.gpsimd.memset(prev[0:1, :], 0.0).then_inc(prev_zero, 1)

            @block.vector
            def _(dve):
                V = nc.vector
                ch = Chain(dve, chain)
                tt, stt, tsc = V.tensor_tensor, V.scalar_tensor_tensor, V.tensor_scalar
                flat = lambda x: x[:, :, :].rearrange("p a b -> p (a b)")
                h3 = lambda x: x.rearrange("p (h d) -> p h d", h=H)
                dve.wait_ge(rows_in, 16 * 11)
                for t in range(TILES):
                    r, k, v = (proj[:, t, i * AW:(i + 1) * AW] for i in range(3))
                    rw = proj[:, t, 0:RW]
                    if t == 0:
                        dve.wait_ge(prev_zero, 1)
                    dve.wait_ge(last_in, 16)
                    dve.wait_ge(prev_in, 16 * (2 * t + 1))
                    ch(tt(prev[:, :], prev[:, :], rw, ALU.subtract))
                    ch(tt(prev[:, :], prev[:, :], row["mu"][:, :], ALU.mult))
                    tt(rw, rw, prev[:, :], ALU.add).then_inc(mixed, 1)
                    dve.wait_ge(mixed, t + 1)
                    dve.wait_ge(lora_out, t + 1)
                    tt(z_s[:, :], bank[:, 1, :], row["w0"][:, :], ALU.add).then_inc(gates_z, 1)
                    tt(a_s[:, :], bank[:, 2, :], row["a0"][:, :], ALU.add).then_inc(gates_z, 1)
                    ch(tt(kk[:, :], k, row["kk"][:, :], ALU.mult))
                    ch(tt(tmp[:, 0:AW], kk[:, :], kk[:, :], ALU.mult))
                    V.tensor_reduce(nrm[:, 0, :], h3(tmp[:, 0:AW]), AX, ALU.add).then_inc(sq_sum, 1)
                    dve.wait_ge(gates, 3 * (t + 1))
                    real = "negc" if t < SAMP else "negc_real"
                    tsc(logd[:, :], z_s[:, :], C[real], None, ALU.mult).then_inc(logd_ok, 1)
                    dve.wait_ge(root, t + 1)
                    ch(tsc(nrm[:, 2, :], nrm[:, 1, :], 1e-12, None, ALU.max))
                    ch(V.reciprocal(nrm[:, 1, :], nrm[:, 2, :]))
                    if t == SAMP:
                        ch(tsc(nrm[:, 1, :], nrm[:, 1, :], C["real"], None, ALU.mult))
                    ch(tt(h3(kk[:, :]), h3(kk[:, :]), last(nrm[:, 1, :], HD), ALU.mult))
                    ch(stt(tmp[:, 0:AW], a_s[:, :], -1.0, row["ka"][:, :], ALU.add, ALU.mult))
                    ch(stt(kp[:, :], tmp[:, 0:AW], 1.0, k, ALU.add, ALU.mult))
                    if t == SAMP:
                        ch(tsc(kp[:, :], kp[:, :], C["real"], None, ALU.mult))
                    ch(tt(a_s[:, :], a_s[:, :], kk[:, :], ALU.mult))
                    ch(tt(tmp[:, 0:AW], r, kp[:, :], ALU.mult))
                    ch(tt(tmp[:, 0:AW], tmp[:, 0:AW], row["rk"][:, :], ALU.mult))
                    ch(V.tensor_reduce(nrm[:, 3, :], h3(tmp[:, 0:AW]), AX, ALU.add))
                    dve.wait_ge(exps, 5 * (t + 1))
                    stt(at[:, :], e_ex[:, :], -1.0, kk[:, :], ALU.mult, ALU.mult)
                    tt(kt[:, :], e_neg[:, :], kp[:, :], ALU.mult)
                    tt(bt[:, :], e_neg[:, :], a_s[:, :], ALU.mult)
                    ch(tt(rt[:, :], e_in[:, :], r, ALU.mult))
                    tt(kend[:, :], e_rev[:, :], kp[:, :], ALU.mult).then_inc(scaled, 1)
                    dve.wait_ge(scaled, t + 1)
                    ch(tt(bend[:, :], e_rev[:, :], a_s[:, :], ALU.mult))
                    for g in range(2):
                        n = 2 * t + g
                        half = slice(g * HD, (g + 1) * HD)
                        masks = ("after16", "before16", "before16", "upto16", "upto16")
                        for i, (x, m) in enumerate(zip((M, MT, KAT, RBT, RKT), masks)):
                            dve.wait_ge(gram, 5 * n + i + 1)
                            tt(x[:, :, :], bank[:, i, :].rearrange("p (a b) -> p a b", b=P), mid(C[m], PAIRS), ALU.mult).then_inc(gram_kept, 1)
                            if i == 2:
                                V.tensor_copy(R[:, :, 0:HD], at[:, :].rearrange("p (q g d) -> p q g d", g=2, d=HD)[:, :, g, :]).then_inc(gram_kept, 1)
                        dve.wait_ge(step_pe, 5 * n + 1)
                        V.tensor_copy(R[:, :, HD:P], bank[:, 5, 0:PAIRS * HD].rearrange("p (q d) -> p q d", d=HD)).then_inc(step_kept, 1)
                        for s, (nx, nxT) in enumerate(((M2, M2T), (M, MT), (M2, M2T))):
                            dve.wait_ge(step_pe, 5 * n + 2 + s)
                            if s < 2:
                                V.tensor_copy(flat(nx), bank[:, 0, :])
                            ch(V.tensor_copy(flat(nxT), bank[:, 1, :]))
                            tt(flat(R), flat(R), bank[:, 2, :], ALU.add).then_inc(step_kept, 1)
                            dve.wait_ge(step_kept, 6 * n + 2 + s)
                        dve.wait_ge(step_pe, 5 * n + 5)
                        b3 = bank[:, 3, :].rearrange("p (q x) -> p q x", x=P)
                        tt(Wp[:, :, g, :], R[:, :, 0:HD], b3[:, :, 0:HD], ALU.add).then_inc(step_kept, 1)
                        tt(U0[:, :, g, :], R[:, :, HD:P], b3[:, :, HD:P], ALU.add).then_inc(step_kept, 1)
                        dve.wait_ge(yg, n + 1)
                        tt(GT[half, :, :], bank[half, 4, :].rearrange("p (q x) -> p q x", x=P), rtT[half, :, :], ALU.add).then_inc(yg_kept, 1)
                        V.tensor_copy(y0[:, :, :].rearrange("p (q g) d -> p q g d", g=2)[:, :, g, :],
                                      bank[:, 5, 0:PAIRS * HD].rearrange("p (q d) -> p q d", d=HD)).then_inc(yg_kept, 1)
                    for q in range(PAIRS):
                        n = PAIRS * t + q
                        if q:
                            dve.wait_ge(pq, n)
                        for x, y in ((bexp, bend), (kexp, kend)):
                            tt(x[:, :, :], mid(y[:, q * P:(q + 1) * P], NSEG), last(C["seg_of_row"], P), ALU.mult).then_inc(expd, 1)
                        dve.wait_ge(pq, n + 1)
                        tt(Qbd[:, q, :, :], bank[:, 2:4, :].rearrange("p a (c x) -> p (a c) x", x=P), mid(C["pair"], NSEG), ALU.mult).then_inc(pq_kept, 1)
                        tt(Pbd[:, q, :, :], bank[:, 0:2, :].rearrange("p a (c x) -> p (a c) x", x=P), mid(C["pair"], NSEG), ALU.mult).then_inc(pq_kept, 1)
                        d3 = tmp[:, 0:NSEG * P].rearrange("p (c x) -> p c x", x=P)
                        tt(d3, mid(C["ident"], NSEG), last(e_chunk[:, q * NSEG:(q + 1) * NSEG], P), ALU.mult).then_inc(pq_kept, 1)
                        dve.wait_ge(pq_kept, 4 * n + 3)
                        tt(Pbd[:, q, :, :], Pbd[:, q, :, :], d3, ALU.add).then_inc(pq_kept, 1)
                        dve.wait_ge(pq_kept, 4 * n + 4)
                    sflat = lambda c: S[:, c, :, :]
                    if t == 0:
                        V.memset(sflat(0), 0.0).then_inc(s_used, 1)
                    elif t < SAMP:
                        V.tensor_copy(sflat(0), sflat(NSEG)).then_inc(s_used, 1)
                    if t < SAMP:
                        dve.wait_ge(s_used, t + 1)
                    for c in range(NSEG):
                        n = NSEG * t + c
                        dve.wait_ge(sc, n + 1)
                        b = bank[:, 4 + c % 2, :].rearrange("p (q x) -> p q x", x=P)
                        o = S[:, c + 1, :, :] if t < SAMP else Pbd[:, :, c, :]
                        tt(o, b, Qbd[:, :, c, :], ALU.add).then_inc(sc_kept, 1)
                    for q in range(PAIRS):
                        n = PAIRS * t + q
                        if q == 0:
                            dve.wait_ge(pq, PAIRS * (t + 1))
                        if q >= 2:
                            dve.wait_ge(y1, n - 1)
                        tt((bexp if q % 2 == 0 else kexp)[:, :, :], mid(GT[:, q, :], NSEG),
                           C["seg_of_col"].rearrange("p (c x) -> p c x", x=P), ALU.mult).then_inc(gexp, 1)
                    dve.wait_ge(y1, PAIRS * (t + 1))
                    y = tmp[:, 0:AW]
                    y2 = tmp[:, AW:2 * AW]
                    dve.wait_ge(yg_kept, 4 * (t + 1))
                    ch(tt(h3(y), bank[:, 6, :].rearrange("p (h d) -> p h d", h=H), y0[:, :, :], ALU.add))
                    ch(V.tensor_reduce(nrm[:, 0, :], h3(y), AX, ALU.add))
                    ch(tsc(nrm[:, 0, :], nrm[:, 0, :], 1.0 / HD, None, ALU.mult))
                    ch(tt(h3(y), h3(y), last(nrm[:, 0, :], HD), ALU.subtract))
                    ch(tt(y2, y, y, ALU.mult))
                    ch(V.tensor_reduce(nrm[:, 2, :], h3(y2), AX, ALU.add))
                    tsc(nrm[:, 0, :], nrm[:, 2, :], 1.0 / HD, 64e-5, ALU.mult, ALU.add).then_inc(var_ok, 1)
                    dve.wait_ge(dev_ok, t + 1)
                    ch(V.reciprocal(nrm[:, 2, :], nrm[:, 1, :]))
                    ch(tt(h3(y), h3(y), last(nrm[:, 2, :], HD), ALU.mult))
                    ch(tt(y, y, row["lnw"][:, :], ALU.mult))
                    ch(tt(y, y, row["lnb"][:, :], ALU.add))
                    ch(tt(h3(y2), h3(v), last(nrm[:, 3, :], HD), ALU.mult))
                    ch(tt(y, y, y2, ALU.add))
                    tt(mix[:, t, 0:AW], y, g_s[:, :], ALU.mult).then_inc(out_ok, 1)
                    dve.wait_ge(out_ok, t + 1)


def mla(nc, C, A, proj, mix, O):
    QH = 64 + RP
    ROWS = H * NS
    GB = P // ROWS
    JP = 4
    JB = NPAGE // JP
    STEPS = JB + 1
    UNITS = 2 * JB * GB
    RING, KRING = 6, 5
    KR = KV + RP
    ORDER = [SAMP] + list(range(SAMP))
    with Stage(nc, "mla") as st:
        sb, sem = st.sb, st.sem
        wuq = sb("wuq", [P, 3, H * QH])
        wuk = sb("wuk", [P, 2, H * 64])
        wuv = sb("wuv", [P, 2, H * 64])
        wukT = sb("wukT", [64, H, KV])
        qnorm, kvnorm = sb("qnorm", [P, QL]), sb("kvnorm", [P, KV])
        pages = sb("pages", [1, NB * NPAGE], mybir.dt.int32)
        cn = sb("cn", [P, TILES, KV])
        kr = sb("kr", [P, TILES, RP])
        kpad = sb("kpad", [P, QH])
        cqn, sq = sb("cqn", [P, QL]), sb("sq", [P, QL])
        ms = sb("ms", [P, 6])
        q_s = sb("q", [P, H * QH])
        rt1, rt2 = sb("rt1", [P, H, RP // 2]), sb("rt2", [P, H, RP // 2])
        cqT, cT = sb("cqT", [P, 3, P]), sb("cT", [P, 2, P])
        Vs = sb("Vs", [P, SAMP, H * 64])
        qT = sb("qT", [QH, H, P])
        mx, neg, tot, inv = (sb(n, [P, H]) for n in ("mx", "neg", "tot", "inv"))
        prob, probT = sb("prob", [P, 2, SEQ]), sb("probT", [P, 2, SEQ])
        qlT = sb("qlT", [QH, 3, NB * ROWS])
        knT = sb("knT", [QH, 3, P])
        keys = sb("keys", [QH, KRING, JP, 3, PAGE])
        vals = sb("vals", [P, RING, JP, KV])
        vnew = sb("vnew", [SEG, NB, KV])
        KT = sb("KT", [QH, H, SEQ])
        pp, ppT = sb("pp", [P, JP * PAGE]), sb("ppT", [P, JP, P])
        top, ntop = sb("top", [P, 2]), sb("ntop", [P, 2])
        part, shrink, total = sb("part", [P, 2]), sb("shrink", [P, 2]), sb("total", [P, 2])
        o_s = sb("o", [P, KV])
        oT = sb("oT", [P, 2, H, NB * SEG])
        bank = st.banks("bank", 8)

        here, pad0 = sem("weights_loaded"), sem("pads_zeroed")
        sq_in, rt_in = sem("mean_squares"), sem("roots")
        norm, flipped, flip_kept = sem("rows_normed"), sem("rows_turned"), sem("turned_kept")
        q_ok, q_kept, roped = sem("queries"), sem("queries_kept"), sem("queries_rotated")
        qt, qt_kept = sem("queries_turned"), sem("turned_queries_kept")
        kv, kv_kept = sem("keys_and_values"), sem("keys_and_values_kept")
        sc, sm, ex = sem("scores"), sem("score_maxima"), sem("exps")
        pt, pt_kept, pv, tile_ok = sem("probs_turned"), sem("turned_probs_kept"), sem("head_outputs"), sem("tile_done")
        chain = sem("vector_chain")
        ql, ql_kept = sem("latent_queries"), sem("latent_queries_kept")
        new_out, new_in, stores = sem("new_rows_stored"), sem("new_rows_loaded"), sem("outputs_stored")
        kin = [sem(f"keys_loaded{i}") for i in range(KRING)]
        vin = [sem(f"values_loaded{i}") for i in range(RING)]
        pin = sem("page_table_loaded")
        ps, gv = sem("page_scores"), sem("page_values")
        s_sc, s_mx, s_ex = sem("step_scores"), sem("step_maximum"), sem("step_exps")
        s_pt, s_ptk, s_pv, s_add = sem("step_turned"), sem("step_turned_kept"), sem("step_values"), sem("step_added")
        masked = sem("new_scores_masked")
        go, gl, gl_kept, fin = sem("group_normed"), sem("group_latents_turned"), sem("group_latents_kept"), sem("sample_outputs")

        def steps_after(t, i):
            if i < 1 or i > 8:
                return []
            c = (t * 8 + i - 1) // 2
            u = c // JB * STEPS + c % JB + 1
            if i % 2 == 1:
                return [("s", u)]
            out = [("v", u)]
            if c % JB == JB - 1:
                out += [("end", c // JB)]
                if c == JB - 1:
                    out += [("s", STEPS), ("v", STEPS)]
            return out

        def page(eng, n, i):
            g, j, b = n // (JB * GB), n // GB % JB, n % GB
            at = (GB * g + b) * NPAGE + JP * j + i
            return eng.value_load(pages[0:1, at:at + 1], min_val=0, max_val=A["keysT"].shape[0] - 1)

        with nc.Block() as block:
            @block.sync
            def _(sp):
                for dst, src in ((wuq[:, :, :], A["w_uq_e"].rearrange("(k p) n -> p k n", p=P)),
                                 (wuk[:, :, :], A["w_uk_e"].rearrange("(k p) n -> p k n", p=P)),
                                 (wuv[:, :, :], A["w_uv_e"].rearrange("(k p) n -> p k n", p=P)),
                                 (wukT[:, :, :], A["w_ukT_e"]),
                                 (qnorm[:, :], A["q_norm_e"].partition_broadcast(P)),
                                 (kvnorm[:, :], A["kv_norm_e"].partition_broadcast(P))):
                    sp.dma_start(dst, src).then_inc(here, 16)
                sp.dma_start(pages[:, :], A["page_table"]).then_inc(pin, 16)
                sp.wait_ge(pin, 16)
                for n in range(UNITS):
                    if n >= KRING:
                        sp.wait_ge(ps, n - KRING + 1)
                    for i in range(JP):
                        sp.dma_start(keys[:, n % KRING, i, :, :].rearrange("p a b -> p (a b)"),
                                     A["keysT"][bass.ds(page(sp, n, i), 1), :, :].rearrange("a p x -> p (a x)")).then_inc(kin[n % KRING], 16)

            @block.gpsimd
            def _(pool):
                nc.gpsimd.memset(oT[:, :, :, :], 0.0).then_inc(pad0, 1)
                pool.wait_ge(norm, 1)
                pool.dma_start(A["new_rows"], cn[:, SAMP, :]).then_inc(new_out, 16)
                pool.wait_ge(new_out, 16)
                pool.dma_start(vnew[:, :, :], A["new_rows"].rearrange("(b s) c -> s b c", s=SEG)).then_inc(new_in, 16)
                pool.wait_ge(pin, 16)
                for n in range(UNITS):
                    if n >= RING:
                        pool.wait_ge(gv, n - RING + 1)
                    for i in range(JP):
                        pool.dma_start(vals[:, n % RING, i, :], A["cache_ckv"][bass.ds(page(pool, n, i), 1), :, :].rearrange("a p x -> p (a x)")).then_inc(vin[n % RING], 16)

            @block.tensor
            def _(pe):
                mmul, turn = nc.tensor.matmul, nc.tensor.transpose
                pe.wait_ge(here, 16 * 6)

                def scores(u):
                    g, j = u // STEPS, u % STEPS - 1
                    for b in range(GB):
                        s = GB * g + b
                        cols = slice(s * ROWS, (s + 1) * ROWS)
                        if j < 0:
                            for k in range(3):
                                mm = mmul(bank[b * ROWS:(b + 1) * ROWS, 6, 0:SEG], qlT[:, k, cols], knT[:, k, s * SEG:(s + 1) * SEG],
                                          start=k == 0, stop=k == 2)
                        else:
                            n = (g * JB + j) * GB + b
                            pe.wait_ge(kin[n % KRING], 16 * JP * (n // KRING + 1))
                            o = bank[b * ROWS:(b + 1) * ROWS, 6, :].rearrange("p (i x) -> p i x", i=JP)
                            for k in range(3):
                                mm = mmul(o, qlT[:, k, cols], keys[:, n % KRING, :, k, :], start=k == 0, stop=k == 2)
                            mm.then_inc(ps, 1)
                    if j < 0:
                        mm.then_inc(s_sc, 1)

                def values(u):
                    g, j = u // STEPS, u % STEPS - 1
                    pe.wait_ge(s_ex, u + 1)
                    w = SEG if j < 0 else PAGE
                    for i in range(1 if j < 0 else JP):
                        mm = turn(bank[0:w, 7, i * P:(i + 1) * P], pp[:, i * w:(i + 1) * w], C["ident"])
                    mm.then_inc(s_pt, 1)
                    pe.wait_ge(s_ptk, u + 1)
                    if u:
                        pe.wait_ge(s_add, u)
                    if u == 0:
                        pe.wait_ge(new_in, 16)
                    for b in range(GB):
                        o = bank[b * ROWS:(b + 1) * ROWS, 0, 0:KV]
                        cols = slice(b * ROWS, (b + 1) * ROWS)
                        if j < 0:
                            mm = mmul(o, ppT[0:SEG, 0, cols], vnew[:, GB * g + b, :], start=True, stop=True)
                            if b == GB - 1:
                                mm.then_inc(s_pv, 1)
                        else:
                            n = (g * JB + j) * GB + b
                            pe.wait_ge(vin[n % RING], 16 * JP * (n // RING + 1))
                            for i in range(JP):
                                mm = mmul(o, ppT[:, i, cols], vals[:, n % RING, i, :], start=i == 0, stop=i == JP - 1)
                            mm.then_inc(gv, 1)

                def group_end(g):
                    pe.wait_ge(go, g + 1)
                    for k in range(2):
                        mm = turn(bank[:, 7, k * P:(k + 1) * P], o_s[:, k * P:(k + 1) * P], C["ident"])
                    mm.then_inc(gl, 1)
                    pe.wait_ge(gl_kept, 2 * (g + 1))

                def take(steps):
                    for what, u in steps:
                        {"s": scores, "v": values, "end": group_end}[what](u)

                for pos, t in enumerate(ORDER):
                    pe.wait_ge(norm, pos + 1)
                    if pos:
                        pe.wait_ge(ql_kept, 7)
                        pe.wait_ge(s_add, 1 + 4 * t + t // 2)
                        if t:
                            pe.wait_ge(tile_ok, t)
                    for i in range(3):
                        turn(bank[:, 0, i * P:(i + 1) * P], cqn[:, i * P:(i + 1) * P], C["ident"])
                    for i in range(2):
                        if t < SAMP:
                            turn(bank[:, 1, i * P:(i + 1) * P], cn[:, t, i * P:(i + 1) * P], C["ident"])
                        else:
                            turn(bank[0:QH, 1, i * P:(i + 1) * P], cn[:, t, i * QH:(i + 1) * QH], C["ident"])
                    turn(bank[0:QH, 3, 0:P], kpad[:, :], C["ident"]).then_inc(flipped, 1)
                    pe.wait_ge(flip_kept, 3 * (pos + 1))
                    for x in range(2):
                        for k in range(3):
                            mm = mmul(bank[:, 2 + x, 0:384], cqT[:, k, :], wuq[:, k, x * 384:(x + 1) * 384], start=k == 0, stop=k == 2)
                    mm.then_inc(q_ok, 1)
                    if t < SAMP:
                        for h in range(H):
                            for k in range(2):
                                mmul(bank[0:64, 6 + h // 4, h % 4 * P:(h % 4 + 1) * P], wuk[:, k, h * 64:(h + 1) * 64], cT[:, k, :],
                                     start=k == 0, stop=k == 1)
                        for k in range(2):
                            mm = mmul(bank[:, 0, :], cT[:, k, :], wuv[:, k, :], start=k == 0, stop=k == 1)
                        mm.then_inc(kv, 1)
                    pe.wait_ge(roped, pos + 1)
                    for h in range(H):
                        mm = turn(bank[0:QH, 4 + h // 4, h % 4 * P:(h % 4 + 1) * P], q_s[:, h * QH:(h + 1) * QH], C["ident"])
                    mm.then_inc(qt, 1)
                    pe.wait_ge(qt_kept, 2 * (pos + 1))
                    if t == SAMP:
                        for k in range(3):
                            m = min(QH, KV - k * QH)
                            for h in range(H):
                                mm = mmul(bank[0:m, 2 + 2 * k + h // 4, h % 4 * P:(h % 4 + 1) * P], wukT[:, h, k * QH:k * QH + m], qT[0:64, h, :],
                                          start=True, stop=True)
                        mm.then_inc(ql, 1)
                        pe.wait_ge(ql_kept, 7)
                        take([("s", 0), ("v", 0)])
                        continue
                    pe.wait_ge(kv_kept, 3 * (t + 1))
                    n_k = (t + 1) * P
                    for i in range(H + 2):
                        if i < H:
                            n = H * t + i
                            if i >= 2:
                                pe.wait_ge(ex, n - 1)
                            mmul(bank[:, 2 + i % 2, 0:n_k], qT[:, i, :], KT[:, i, 0:n_k], start=True, stop=True).then_inc(sc, 1)
                        if 1 <= i <= H:
                            n = H * t + i - 1
                            pe.wait_ge(ex, n + 1)
                            if i >= 3:
                                pe.wait_ge(pt_kept, n - 1)
                            for k in range(t + 1):
                                mm = turn(bank[:, 4 + (i - 1) % 2, k * P:(k + 1) * P], prob[:, (i - 1) % 2, k * P:(k + 1) * P], C["ident"])
                            mm.then_inc(pt, 1)
                        if i >= 2:
                            h, n = i - 2, H * t + i - 2
                            pe.wait_ge(pt_kept, n + 1)
                            for k in range(t + 1):
                                mm = mmul(bank[:, 1, h * 64:(h + 1) * 64], probT[:, h % 2, k * P:(k + 1) * P], Vs[:, k, h * 64:(h + 1) * 64],
                                          start=k == 0, stop=k == t)
                            mm.then_inc(pv, 1)
                        take(steps_after(t, i))
                for h in range(H):
                    for k in range(2):
                        mm = mmul(bank[:, 0, h * 64:(h + 1) * 64], oT[:, k, h, :], wuv[:, k, h * 64:(h + 1) * 64], start=k == 0, stop=k == 1)
                mm.then_inc(fin, 1)

            @block.scalar
            def _(act):
                a_, cp = nc.scalar.activation, nc.scalar.copy

                def exps(u):
                    j = u % STEPS - 1
                    w = SEG if j < 0 else JP * PAGE
                    act.wait_ge(s_mx, u + 1)
                    if u:
                        act.wait_ge(s_pt, u)
                    if j >= 0:
                        a_(shrink[:, u % 2:u % 2 + 1], top[:, 1 - u % 2:2 - u % 2], ACT.Exp, bias=ntop[:, u % 2:u % 2 + 1], scale=SM)
                    a_(pp[:, 0:w], bank[:, 6, 0:w], ACT.Exp, bias=ntop[:, u % 2:u % 2 + 1], scale=SM, accum_out=part[:, u % 2:u % 2 + 1]).then_inc(s_ex, 1)

                def turned(u):
                    act.wait_ge(s_pt, u + 1)
                    if u % STEPS == 0:
                        cp(ppT[0:SEG, 0, :], bank[0:SEG, 7, 0:P]).then_inc(s_ptk, 1)
                    else:
                        cp(ppT[:, :, :].rearrange("p a b -> p (a b)"), bank[:, 7, :]).then_inc(s_ptk, 1)

                def take(steps):
                    for what, u in steps:
                        {"s": exps, "v": turned, "end": lambda g: None}[what](u)

                for pos, t in enumerate(ORDER):
                    act.wait_ge(sq_in, pos + 1)
                    a_(ms[:, 2:4], ms[:, 0:2], ACT.Sqrt).then_inc(rt_in, 1)
                    act.wait_ge(flipped, pos + 1)
                    cp(cqT[:, :, :].rearrange("p a b -> p (a b)"), bank[:, 0, 0:3 * P]).then_inc(flip_kept, 1)
                    if t < SAMP:
                        cp(cT[:, :, :].rearrange("p a b -> p (a b)"), bank[:, 1, 0:2 * P]).then_inc(flip_kept, 1)
                        act.wait_ge(kv, t + 1)
                        for i in range(2):
                            cp(KT[0:64, 4 * i:4 * i + 4, t * P:(t + 1) * P], bank[0:64, 6 + i, :].rearrange("p (h x) -> p h x", h=4)).then_inc(kv_kept, 1)
                        cp(Vs[:, t, :], bank[:, 0, :]).then_inc(kv_kept, 1)
                    else:
                        cp(knT[:, 0:2, :].rearrange("p a b -> p (a b)"), bank[0:QH, 1, 0:2 * P]).then_inc(flip_kept, 1)
                    act.wait_ge(qt, pos + 1)
                    for i in range(2):
                        cp(qT[:, 4 * i:4 * i + 4, :].rearrange("p a b -> p (a b)"), bank[0:QH, 4 + i, :]).then_inc(qt_kept, 1)
                    if t == SAMP:
                        act.wait_ge(ql, 1)
                        for k in range(3):
                            m = min(QH, KV - k * QH)
                            for i in range(2):
                                src = bank[0:m, 2 + 2 * k + i, :].rearrange("p (h b s) -> p h b s", h=4, s=SEG)[:, :, :, 1:1 + NS]
                                dst = qlT[0:m, k, :].rearrange("p (b h q) -> p h b q", h=H, q=NS)[:, 4 * i:4 * i + 4, :, :]
                                cp(dst, src).then_inc(ql_kept, 1)
                        act.wait_ge(qt_kept, 2)
                        cp(qlT[64:QH, 2, :].rearrange("p (b h q) -> p h b q", h=H, q=NS),
                           qT[64:QH, :, :].rearrange("p h (b s) -> p h b s", s=SEG)[:, :, :, 1:1 + NS]).then_inc(ql_kept, 1)
                        take([("s", 0), ("v", 0)])
                        continue
                    n_k = (t + 1) * P
                    for i in range(H + 2):
                        if i < H:
                            n = H * t + i
                            act.wait_ge(sm, n + 1)
                            if i >= 2:
                                act.wait_ge(pt, n - 1)
                            a_(prob[:, i % 2, 0:n_k], bank[:, 2 + i % 2, 0:n_k], ACT.Exp, bias=neg[:, i:i + 1], scale=SM,
                               accum_out=tot[:, i:i + 1]).then_inc(ex, 1)
                        if 1 <= i <= H:
                            n = H * t + i - 1
                            act.wait_ge(pt, n + 1)
                            if i >= 3:
                                act.wait_ge(pv, n - 1)
                            cp(probT[:, (i - 1) % 2, 0:n_k], bank[:, 4 + (i - 1) % 2, 0:n_k]).then_inc(pt_kept, 1)
                        take(steps_after(t, i))
                act.wait_ge(norm, TILES)
                act.dma_start(O["ckv"].rearrange("(t p) c -> p t c", p=P), cn[:, :, :]).then_inc(stores, 16)
                act.dma_start(O["kpe"].rearrange("(t p) c -> p t c", p=P), kr[:, :, :]).then_inc(stores, 16)
                act.wait_ge(stores, 32)

            @block.vector
            def _(dve):
                V = nc.vector
                ch = Chain(dve, chain)
                tt, tsc, st2 = V.tensor_tensor, V.tensor_scalar, V.scalar_tensor_tensor
                dve.wait_ge(here, 16 * 6)
                dve.wait_ge(pad0, 1)

                def maximum(u):
                    g, j = u // STEPS, u % STEPS - 1
                    now, before = slice(u % 2, u % 2 + 1), slice(1 - u % 2, 2 - u % 2)
                    if j < 0:
                        dve.wait_ge(s_sc, g + 1)
                        tt(bank[:, 6, 0:SEG], bank[:, 6, 0:SEG], C["newmask"], ALU.add).then_inc(masked, 1)
                        dve.wait_ge(masked, g + 1)
                        ch(V.tensor_reduce(top[:, now], bank[:, 6, 0:SEG], AX, ALU.max))
                    else:
                        dve.wait_ge(ps, (g * JB + j + 1) * GB)
                        ch(V.tensor_reduce(top[:, now], bank[:, 6, :], AX, ALU.max))
                        ch(tt(top[:, now], top[:, now], top[:, before], ALU.max))
                    tsc(ntop[:, now], top[:, now], -SM, None, ALU.mult).then_inc(s_mx, 1)

                def add(u):
                    g, j = u // STEPS, u % STEPS - 1
                    now, before = slice(u % 2, u % 2 + 1), slice(1 - u % 2, 2 - u % 2)
                    dve.wait_ge(s_ex, u + 1)
                    if j < 0:
                        ch(V.tensor_copy(total[:, now], part[:, now]))
                        dve.wait_ge(s_pv, g + 1)
                        V.tensor_copy(o_s[:, :], bank[:, 0, 0:KV]).then_inc(s_add, 1)
                    else:
                        st2(out=total[:, now], in0=total[:, before], scalar=shrink[:, now], in1=part[:, now], op0=ALU.mult, op1=ALU.add)
                        dve.wait_ge(gv, (g * JB + j + 1) * GB)
                        dve.wait_ge(s_add, u)
                        st2(out=o_s[:, :], in0=o_s[:, :], scalar=shrink[:, now], in1=bank[:, 0, 0:KV], op0=ALU.mult, op1=ALU.add).then_inc(s_add, 1)

                def group_end(g):
                    u = (g + 1) * STEPS - 1
                    now = slice(u % 2, u % 2 + 1)
                    dve.wait_ge(s_add, u + 1)
                    ch(V.reciprocal(total[:, now], total[:, now]))
                    tsc(o_s[:, :], o_s[:, :], total[:, now], None, ALU.mult).then_inc(go, 1)
                    dve.wait_ge(gl, g + 1)
                    for k in range(2):
                        for b in range(GB):
                            s = GB * g + b
                            ins = V.tensor_copy(oT[:, k, :, s * SEG + 1:s * SEG + 1 + NS],
                                                bank[:, 7, k * P + b * ROWS:k * P + (b + 1) * ROWS].rearrange("p (h q) -> p h q", h=H))
                        ins.then_inc(gl_kept, 1)

                def take(steps):
                    for what, u in steps:
                        {"s": maximum, "v": add, "end": group_end}[what](u)

                for pos, t in enumerate(ORDER):
                    cq = proj[:, t, 0:QL]
                    ckv = proj[:, t, QL:QL + KV]
                    kpe = proj[:, t, QL + KV:QL + KV + RP]
                    ch(tt(sq[:, :], cq, cq, ALU.mult))
                    ch(V.tensor_reduce(ms[:, 4:5], sq[:, :], AX, ALU.add))
                    ch(tt(sq[:, 0:KV], ckv, ckv, ALU.mult))
                    ch(V.tensor_reduce(ms[:, 5:6], sq[:, 0:KV], AX, ALU.add))
                    ch(tsc(ms[:, 0:1], ms[:, 4:5], 1.0 / QL, 1e-6, ALU.mult, ALU.add))
                    tsc(ms[:, 1:2], ms[:, 5:6], 1.0 / KV, 1e-6, ALU.mult, ALU.add).then_inc(sq_in, 1)
                    dve.wait_ge(rt_in, pos + 1)
                    ch(V.reciprocal(ms[:, 4:6], ms[:, 2:4]))
                    ch(tsc(cqn[:, :], cq, ms[:, 4:5], None, ALU.mult))
                    tt(cqn[:, :], cqn[:, :], qnorm[:, :], ALU.mult)
                    ch(tsc(cn[:, t, :], ckv, ms[:, 5:6], None, ALU.mult))
                    ch(tt(cn[:, t, :], cn[:, t, :], kvnorm[:, :], ALU.mult))
                    cos, sin = (C[n][:, t * 16:(t + 1) * 16] for n in ("cos", "sin"))

                    def rotate(x1, x2, cs, sn, y1, y2, a, b):
                        tt(a, x1, cs, ALU.mult)
                        ch(tt(b, x2, sn, ALU.mult))
                        ch(tt(b, a, b, ALU.subtract))
                        ch(tt(a, x1, sn, ALU.mult))
                        ch(V.tensor_copy(y1, b))
                        ch(tt(b, x2, cs, ALU.mult))
                        ch(tt(y2, a, b, ALU.add))

                    rotate(kpe[:, 0:16], kpe[:, 16:32], cos, sin, kr[:, t, 0:16], kr[:, t, 16:32], rt1[:, 0, :], rt2[:, 0, :])
                    if t == SAMP:
                        V.tensor_copy(kpad[:, 0:64], cn[:, t, 2 * QH:KV])
                    V.tensor_copy(kpad[:, 64:QH], kr[:, t, :]).then_inc(norm, 1)
                    dve.wait_ge(flipped, pos + 1)
                    if t < SAMP:
                        V.tensor_copy(KT[64:QH, :, t * P:(t + 1) * P], mid(bank[64:QH, 3, 0:P], H)).then_inc(flip_kept, 1)
                    else:
                        V.tensor_copy(knT[:, 2, :], bank[0:QH, 3, 0:P]).then_inc(flip_kept, 1)
                    dve.wait_ge(q_ok, pos + 1)
                    ch(V.tensor_copy(q_s[:, :].rearrange("p (a x) -> p a x", a=2), bank[:, 2:4, 0:384]))
                    q3 = q_s[:, :].rearrange("p (h x) -> p h x", h=H)
                    x1, x2 = q3[:, :, 64:80], q3[:, :, 80:96]
                    rotate(x1, x2, mid(cos, H), mid(sin, H), x1, x2, rt1[:, :, :], rt2[:, :, :])
                    V.tensor_copy(rt1[:, 0, 0:1], rt2[:, 0, 0:1]).then_inc(roped, 1)
                    if t == SAMP:
                        take([("s", 0), ("v", 0)])
                        continue
                    for h in range(H + 2):
                        if h < H:
                            n = H * t + h
                            dve.wait_ge(sc, n + 1)
                            b = bank[:, 2 + h % 2, :]
                            ch(tt(b[:, t * P:(t + 1) * P], b[:, t * P:(t + 1) * P], C["causal"], ALU.add))
                            ch(V.tensor_reduce(mx[:, h:h + 1], b[:, 0:(t + 1) * P], AX, ALU.max))
                            tsc(neg[:, h:h + 1], mx[:, h:h + 1], -SM, None, ALU.mult).then_inc(sm, 1)
                        take(steps_after(t, h))
                    dve.wait_ge(ex, H * (t + 1))
                    ch(V.reciprocal(inv[:, :], tot[:, :]))
                    dve.wait_ge(pv, H * (t + 1))
                    tt(mix[:, t, :].rearrange("p (h d) -> p h d", h=H), bank[:, 1, :].rearrange("p (h d) -> p h d", h=H),
                       last(inv[:, :], 64), ALU.mult).then_inc(tile_ok, 1)
                dve.wait_ge(fin, 1)
                ch(V.tensor_copy(mix[:, SAMP, :], bank[:, 0, :]))


GT = SAMP - 1
DENSE = TOK - P
SAMP_AT = GT * P
START = [t * P for t in range(GT)] + [DENSE, SAMP_AT]
T_ROWS = [P] * SAMP + [NB * NS]


def turn(nc, name, C, x, xT, compact):
    with Stage(nc, name) as st:
        bank = st.banks("bank", 4)
        turned, kept = st.sem("rows_turned"), st.sem("columns_kept")
        with nc.Block() as block:
            @block.tensor
            def _(pe):
                for t in range(TILES):
                    for i in range(2):
                        n = 2 * t + i
                        if n >= 4:
                            pe.wait_ge(kept, n - 3)
                        for k in range(4):
                            mm = nc.tensor.transpose(bank[:, n % 4, k * P:(k + 1) * P], x[:, t, (4 * i + k) * P:(4 * i + k + 1) * P], C["ident"])
                        mm.then_inc(turned, 1)

            @block.vector
            def _(dve):
                for t in range(TILES):
                    for i in range(2):
                        n = 2 * t + i
                        dve.wait_ge(turned, n + 1)
                        src = bank[:, n % 4, :].rearrange("p (k x) -> p k x", k=4)
                        dst = xT[:, 4 * i:4 * i + 4, :]
                        if t < SAMP or not compact:
                            at = START[t] if compact else t * P
                            nc.vector.tensor_copy(dst[:, :, at:at + P], src).then_inc(kept, 1)
                        else:
                            nc.vector.tensor_copy(dst[:, :, SAMP_AT:DENSE].rearrange("p k (b s) -> p k b s", s=NS),
                                                  src.rearrange("p k (b s) -> p k b s", s=SEG)[:, :, :, 1:1 + NS]).then_inc(kept, 1)


def layer_norm_vector(nc, dve, ch, x, t, sem_sum, sem_root, sem_norm, stats, mv, gain, shift):
    V = nc.vector
    V.bn_stats(stats[:, 0, :], x[:, t, 0:512])
    ch(V.bn_stats(stats[:, 1, :], x[:, t, 512:D]))
    ch(V.bn_aggr(mv[:, 0:2], stats[:, :, :]))
    V.tensor_scalar(mv[:, 2:3], mv[:, 1:2], 1e-5, None, ALU.add).then_inc(sem_sum, 1)
    dve.wait_ge(sem_root, t + 1)
    ch(V.reciprocal(mv[:, 4:5], mv[:, 3:4]))
    V.scalar_tensor_tensor(out=mv[:, 5:6], in0=mv[:, 0:1], scalar=-1.0, in1=mv[:, 4:5], op0=ALU.mult, op1=ALU.mult).then_inc(sem_sum, 1)
    dve.wait_ge(sem_norm, t + 1)
    ch(V.tensor_tensor(x[:, t, :], x[:, t, :], gain, ALU.mult))
    ch(V.tensor_tensor(x[:, t, :], x[:, t, :], shift, ALU.add))


def layer_norm_scalar(nc, act, x, t, sem_sum, sem_root, sem_norm, mv):
    act.wait_ge(sem_sum, 2 * t + 1)
    nc.scalar.activation(mv[:, 3:4], mv[:, 2:3], ACT.Sqrt).then_inc(sem_root, 1)
    act.wait_ge(sem_sum, 2 * t + 2)
    nc.scalar.activation(x[:, t, :], x[:, t, :], ACT.Identity, bias=mv[:, 5:6], scale=mv[:, 4:5]).then_inc(sem_norm, 1)


def out_project(nc, name, C, mixed, w_dram, gain_dram, shift_dram, x):
    with Stage(nc, name) as st:
        w = st.sb("w", [P, KD, D])
        gain, shift = st.sb("gain", [P, D]), st.sb("shift", [P, D])
        mT = st.sb("mT", [P, 2, KD, P])
        stats, mv = st.sb("stats", [P, 2, 6]), st.sb("mv", [P, 6])
        bank = st.banks("bank", 8)
        here = st.sem("weights_loaded")
        turned, kept, done, added = st.sem("turned"), st.sem("turned_kept"), st.sem("products"), st.sem("residual_added")
        s_sum, s_root, s_norm, chain = st.sem("statistics"), st.sem("deviation"), st.sem("normed"), st.sem("vector_chain")
        with nc.Block() as block:
            @block.sync
            def _(sp):
                sp.dma_start(w[:, :, :], w_dram.rearrange("(k p) n -> p k n", p=P)).then_inc(here, 16)
                sp.dma_start(gain[:, :], gain_dram.partition_broadcast(P)).then_inc(here, 16)
                sp.dma_start(shift[:, :], shift_dram.partition_broadcast(P)).then_inc(here, 16)

            @block.tensor
            def _(pe):
                def turns(t):
                    for i in range(2):
                        n = 2 * t + i
                        if n >= 4:
                            pe.wait_ge(kept, n - 3)
                        for k in range(4):
                            mm = nc.tensor.transpose(bank[:, n % 4, k * P:(k + 1) * P], mixed(t, 4 * i + k), C["ident"])
                        mm.then_inc(turned, 1)

                turns(0)
                pe.wait_ge(here, 48)
                for t in range(TILES):
                    if t + 1 < TILES:
                        turns(t + 1)
                    pe.wait_ge(kept, 2 * (t + 1))
                    if t >= 2:
                        pe.wait_ge(added, t - 1)
                    for i in range(2):
                        for k in range(KD):
                            mm = nc.tensor.matmul(bank[:, 4 + 2 * (t % 2) + i, :], mT[:, t % 2, k, :], w[:, k, i * 512:(i + 1) * 512],
                                                  start=k == 0, stop=k == KD - 1)
                    mm.then_inc(done, 1)

            @block.scalar
            def _(act):
                def keep(t):
                    if t >= 2:
                        act.wait_ge(done, t - 1)
                    for i in range(2):
                        act.wait_ge(turned, 2 * t + i + 1)
                        nc.scalar.copy(mT[:, t % 2, 4 * i:4 * i + 4, :].rearrange("p a b -> p (a b)"), bank[:, (2 * t + i) % 4, :]).then_inc(kept, 1)

                keep(0)
                for t in range(TILES):
                    if t + 1 < TILES:
                        keep(t + 1)
                    layer_norm_scalar(nc, act, x, t, s_sum, s_root, s_norm, mv)

            @block.vector
            def _(dve):
                ch = Chain(dve, chain)
                dve.wait_ge(here, 48)
                for t in range(TILES):
                    dve.wait_ge(done, t + 1)
                    nc.vector.scalar_tensor_tensor(out=x[:, t, :], in0=x[:, t, :], scalar=ALPHA,
                                                   in1=bank[:, 4 + 2 * (t % 2):6 + 2 * (t % 2), :].rearrange("p a b -> p (a b)"),
                                                   op0=ALU.mult, op1=ALU.add).then_inc(added, 1)
                    dve.wait_ge(added, t + 1)
                    layer_norm_vector(nc, dve, ch, x, t, s_sum, s_root, s_norm, stats, mv, gain[:, :], shift[:, :])


def peer_select(nc, name, C, xT, wq_dram, k1T_dram, k2T_dram, picks, expert, gate):
    T4 = SEQ // P
    rows = T_ROWS
    HALF = TOK // 2
    with Stage(nc, name) as st:
        sb, sem = st.sb, st.sem
        wq = sb("wq", [P, 2, KD, 512])
        kT = sb("kT", [P, 2, NK])
        qT = sb("qT", [P, 2, TOK])
        s = sb("scores", [P, 2, TILES, NK])
        s2 = sb("scores_rest", [P, TILES, NK])
        val = sb("val", [P, TILES, PH, 2, PK])
        idx = sb("idx", [P, TILES, PH, 2, PK], U32)
        idxf = sb("idxf", [P, PH, 2, PK])
        cand, cand2 = sb("cand", [P, PH, PK * PK]), sb("cand_rest", [P, PH, PK * PK])
        top, sel = sb("top", [P, PH, PK]), sb("sel", [P, PH, PK], U32)
        ab, abf = sb("ab", [P, 2, HK], U32), sb("abf", [P, 2, HK])
        out = sb("out", [P, 3, HK])
        eg, zg = sb("eg", [P, PH, PK]), sb("zg", [P, 2, PH])
        bank = st.banks("bank", 8)
        w_in, k_in = [sem("wq_loaded0"), sem("wq_loaded1")], sem("sub_keys_loaded")
        q_ok, q_kept, s_ok, s_kept, s_used = sem("queries"), sem("queries_kept"), sem("scores"), sem("scores_kept"), sem("scores_ranked")
        chain, diff, expd = sem("vector_chain"), sem("gate_logits"), sem("gate_exps")
        out_ok, turned, kept = sem("picks_ready"), sem("picks_turned"), sem("picks_kept")
        NC_ = 2 * PH
        FINAL = [t for t in range(TILES) if t != GT] + [GT]
        with nc.Block() as block:
            @block.sync
            def _(sp):
                sp.dma_start(kT[:, 0, :], k1T_dram).then_inc(k_in, 16)
                sp.dma_start(kT[:, 1, :], k2T_dram).then_inc(k_in, 16)
                wv = wq_dram.rearrange("(k p) n -> p k n", p=P)
                for n in range(4):
                    if n >= 2:
                        sp.wait_ge(q_ok, 4 * (n - 1))
                    sp.dma_start(wq[:, n % 2, :, :], wv[:, :, n * 512:(n + 1) * 512]).then_inc(w_in[n % 2], 16)

            @block.tensor
            def _(pe):
                pe.wait_ge(k_in, 32)
                for c in range(NC_ + 1):
                    if c < NC_:
                        n = c // 4
                        pe.wait_ge(w_in[n % 2], 16 * (n // 2 + 1))
                        if c >= 2:
                            pe.wait_ge(q_kept, c - 1)
                        for i in range(2):
                            for k in range(KD):
                                mm = nc.tensor.matmul(bank[:, 2 * (c % 2) + i, 0:HALF], wq[:, n % 2, k, c % 4 * P:(c % 4 + 1) * P],
                                                      xT[:, k, i * HALF:(i + 1) * HALF], start=k == 0, stop=k == KD - 1)
                        mm.then_inc(q_ok, 1)
                    if c:
                        d = c - 1
                        pe.wait_ge(q_kept, d + 1)
                        if d >= 2:
                            pe.wait_ge(s_kept, 2 * (d - 1))
                        for t in range(TILES):
                            o = bank[0:rows[t], 4 + 2 * (d % 2) + t // T4, t % T4 * P:(t % T4 + 1) * P]
                            mm = nc.tensor.matmul(o, qT[:, d % 2, START[t]:START[t] + rows[t]], kT[:, d % 2, :], start=True, stop=True)
                        mm.then_inc(s_ok, 1)
                pe.wait_ge(s_kept, 2 * NC_)
                for n, t in enumerate(FINAL[:-1]):
                    r = rows[t]
                    pe.wait_ge(out_ok, n + 1)
                    if n >= 2:
                        pe.wait_ge(kept, n - 1)
                    for i in range(3):
                        mm = nc.tensor.transpose(bank[:, n % 2, i * P:i * P + r], out[0:r, i, :], C["ident"][0:r, 0:r])
                    mm.then_inc(turned, 1)

            @block.scalar
            def _(act):
                for c in range(NC_ + 1):
                    if c < NC_:
                        act.wait_ge(q_ok, c + 1)
                        if c >= 2:
                            act.wait_ge(s_ok, c - 1)
                        nc.scalar.copy(qT[:, c % 2, :].rearrange("p (a x) -> p a x", a=2), bank[:, 2 * (c % 2):2 * (c % 2) + 2, 0:HALF]).then_inc(q_kept, 1)
                    if c:
                        d = c - 1
                        act.wait_ge(s_ok, d + 1)
                        if d >= 2:
                            act.wait_ge(s_used, d - 1)
                        nc.scalar.copy(s[:, d % 2, 0:T4, :].rearrange("p a b -> p (a b)"), bank[:, 4 + 2 * (d % 2), :]).then_inc(s_kept, 1)
                        nc.scalar.copy(s[0:rows[T4], d % 2, T4, :], bank[0:rows[T4], 5 + 2 * (d % 2), 0:P]).then_inc(s_kept, 1)
                for n, t in enumerate(FINAL):
                    act.wait_ge(diff, n + 1)
                    nc.scalar.activation(eg[0:rows[t], :, :], eg[0:rows[t], :, :], ACT.Exp).then_inc(expd, 1)
                    if t == GT:
                        continue
                    act.wait_ge(turned, n + 1)
                    src = bank[:, n % 2, 0:3 * P].rearrange("p (i x) -> p i x", i=3)[:, :, 0:rows[t]]
                    nc.scalar.copy(picks[:, :, START[t]:START[t] + rows[t]], src).then_inc(kept, 1)

            @block.vector
            def _(dve):
                V = nc.vector
                ch = Chain(dve, chain)
                tt = V.tensor_tensor

                def best16(items):
                    for n, step in enumerate((
                            lambda a, r, v, i: V.max(v[:, 0:8], a),
                            lambda a, r, v, i: V.max_index(i[:, 0:8], v[:, 0:8], a),
                            lambda a, r, v, i: V.match_replace(r, v[:, 0:8], a, NEG),
                            lambda a, r, v, i: V.max(v[:, 8:16], r),
                            lambda a, r, v, i: V.max_index(i[:, 8:16], v[:, 8:16], r))):
                        for item in items:
                            ins = step(*item)
                        ch(ins)

                for c in range(NC_):
                    h, half = c // 2, c % 2
                    dve.wait_ge(s_kept, 2 * (c + 1))
                    best16([(s[0:rows[t], c % 2, t, :], s2[0:rows[t], t, :], val[0:rows[t], t, h, half, :], idx[0:rows[t], t, h, half, :])
                            for t in range(TILES)])
                    V.tensor_copy(zg[0:1, 0, 0:1], val[0:1, 0, h, half, 0:1]).then_inc(s_used, 1)
                for n, t in enumerate(FINAL):
                    r = slice(0, rows[t])
                    c4 = cand[r].rearrange("p h (a b) -> p h a b", b=PK)
                    v1 = val[r, t, :, 0, :].unsqueeze(3).to_broadcast([rows[t], PH, PK, PK])
                    v2 = val[r, t, :, 1, :].unsqueeze(2).to_broadcast([rows[t], PH, PK, PK])
                    V.tensor_copy(idxf[r], idx[r, t])
                    ch(tt(c4, v1, v2, ALU.add))
                    best16([(cand[r, h, :], cand2[r, h, :], top[r, h, :], sel[r, h, :]) for h in range(PH)])
                    flat = sel[r].rearrange("p h k -> p (h k)")
                    V.tensor_scalar(ab[r, 0, :], flat, 4, None, ALU.logical_shift_right)
                    V.tensor_scalar(ab[r, 1, :], flat, PK - 1, None, ALU.bitwise_and)
                    ch(tt(eg[r], top[r], top[r, :, 0:1].to_broadcast([rows[t], PH, PK]), ALU.subtract))
                    V.tensor_copy(abf[r], ab[r]).then_inc(diff, 1)
                    dve.wait_ge(diff, n + 1)
                    if n:
                        dve.wait_ge(turned, n)
                    for i in range(2):
                        e = cand[r].rearrange("p h x -> p (h x)")
                        e3 = e.rearrange("p (n a) -> p n a", a=PK)
                        ch(tt(e3, last(abf[r, i, :], PK), mid(C["iota"][r, 0:PK], HK), ALU.is_equal))
                        e4 = e.rearrange("p (h k a) -> p h k a", h=PH, a=PK)
                        ch(tt(e4, e4, idxf[r, :, i, :].unsqueeze(2).to_broadcast([rows[t], PH, PK, PK]), ALU.mult))
                        ch(V.tensor_reduce(out[r, i, :], e3, AX, ALU.add))
                    dve.wait_ge(expd, n + 1)
                    ch(V.tensor_reduce(zg[r, 0, :], eg[r], AX, ALU.add))
                    ch(V.reciprocal(zg[r, 1, :], zg[r, 0, :]))
                    tt(out[r, 2, :].rearrange("p (h k) -> p h k", h=PH), eg[r], last(zg[r, 1, :], PK), ALU.mult).then_inc(out_ok, 1)
                    dve.wait_ge(out_ok, n + 1)
                ch(V.scalar_tensor_tensor(out=abf[:, 0, :], in0=out[:, 0, :], scalar=float(NK), in1=out[:, 1, :], op0=ALU.mult, op1=ALU.add))
                V.tensor_copy(expert, abf[:, 0, :])
                ch(V.tensor_copy(gate, out[:, 2, :]))


BLK = 32
NBLK = DENSE // BLK


def peer_spread(nc, name, C, picks, grids):
    G4 = BLK // 4
    with Stage(nc, name) as st:
        sb, sem = st.sb, st.sem
        rowhot, colhot = sb("rowhot", [P, 4, 4, NK]), sb("colhot", [P, 4, 4, NK])
        grid = sb("grid", [P, 2, NK, BLK])
        bank = st.banks("bank", 4)
        marked, kept, free = sem("picks_marked"), sem("grids_kept"), sem("marks_used")
        sent = [sem("grid_sent0"), sem("grid_sent1")]
        TWO = NBLK // 2

        def block_steps(work, eng):
            with eng.Fori(0, TWO) as m:
                for u in range(2):
                    work(m * 2 + u, u, m)
            work(NBLK - 1, (NBLK - 1) % 2, TWO)

        with nc.Block() as block:
            @block.vector
            def _(dve):
                def work(b, u, m):
                    for j in range(G4):
                        dve.wait_ge(free, b * G4 + j + 1)
                        nc.vector.tensor_tensor(colhot[:, j % 4, :, :], mid(C["iota"], 4), last(picks[:, 1, bass.ds(b * BLK + 4 * j, 4)], NK), ALU.is_equal)
                        for i in range(4):
                            tok = b * BLK + (4 * j + i)
                            ins = nc.vector.tensor_scalar(rowhot[:, j % 4, i, :], C["iota"], picks[:, 0, bass.ds(tok, 1)],
                                                          picks[:, 2, bass.ds(tok, 1)], ALU.is_equal, ALU.mult)
                        ins.then_inc(marked, 1)
                block_steps(work, dve)

            @block.tensor
            def _(pe):
                pe.sem_inc(free, 4)
                def work(b, u, m):
                    for j in range(G4):
                        pe.wait_ge(marked, b * G4 + j + 1)
                        pe.wait_ge(kept, b * G4 + j + 1)
                        for i in range(4):
                            mm = nc.tensor.matmul(bank[:, j % 4, i * NK:(i + 1) * NK], rowhot[:, j % 4, i, :], colhot[:, j % 4, i, :], start=True, stop=True)
                        mm.then_inc(free, 1)
                block_steps(work, pe)

            @block.scalar
            def _(act):
                act.sem_inc(kept, 4)
                def work(b, u, m):
                    act.wait_ge(sent[u], m * 16 + 16)
                    for j in range(G4):
                        act.wait_ge(free, b * G4 + j + 5)
                        nc.scalar.copy(grid[:, u, :, 4 * j:4 * j + 4], bank[:, j % 4, :].rearrange("p (t x) -> p x t", t=4)).then_inc(kept, 1)
                block_steps(work, act)

            @block.sync
            def _(sp):
                for u in range(2):
                    sp.sem_inc(sent[u], 16)
                def work(b, u, m):
                    sp.wait_ge(kept, b * G4 + G4 + 4)
                    sp.dma_start(grids[bass.ds(b, 1), :, :, :].rearrange("a p c t -> p (a c t)"), grid[:, u, :, :].rearrange("p c t -> p (c t)")).then_inc(sent[u], 16)
                block_steps(work, sp)
                sp.wait_ge(sent[0], 16 * (TWO + 2))
                sp.wait_ge(sent[1], 16 * (TWO + 1))


GI = 4
NGRP = NK // GI
PER = 2 * HK * GI // NK


def peer_experts(nc, name, xT, x_rows, expert, gate, uT_dram, v_dram, u_rows, v_rows, grids, yT, y_rows):
    with Stage(nc, name) as st:
        sb, sem = st.sb, st.sem
        u = sb("u", [P, 2, GI, KD, NK])
        v = sb("v", [P, 2, GI, D])
        gates = sb("gates", [P, 2, NBLK, GI * BLK])
        act_s = sb("act", [P, 2, DENSE])
        w = sb("w", [P, 2, GI, DENSE])
        RING = 4
        rows = sb("rows", [P, RING, D])
        idx8 = sb("idx8", [P, 2, PER], U32)
        some = sb("some", [P, 2, PER])
        dot, weight = sb("dot", [P, HK]), sb("weight", [P, HK])
        bank = st.banks("bank", 8)
        u_in, v_in, g_in = ([sem(f"{n}_loaded{i}") for i in range(2)] for n in ("u", "v", "gates"))
        dots, gelus, weighed = sem("dots"), sem("gelus"), sem("weighed")
        sums, added = sem("sums"), sem("sums_added")
        row_in = [sem(f"row_gathered{i}") for i in range(RING)]
        slot_taken = sem("slot_taken")
        row_used, idx_ok, some_ok, dot_ok, weight_ok = sem("row_used"), sem("places_ready"), sem("weights_ready"), sem("row_dots"), sem("row_gelus")
        MID = NGRP // 4

        def halves(eng, first, second, between):
            first(0, 0, 0, True)
            with eng.Fori(0, MID) as m:
                first(m * 2 + 1, 1, m, False)
                second(m * 2, 0, m, "u")
                first(m * 2 + 2, 0, m + 1, False)
                second(m * 2 + 1, 1, m, "u")
            between()
            with eng.Fori(MID, NGRP // 2 - 1) as m:
                first(m * 2 + 1, 1, m, False)
                second(m * 2, 0, m, "v")
                first(m * 2 + 2, 0, m + 1, False)
                second(m * 2 + 1, 1, m, "v")
            first(NGRP - 1, 1, NGRP // 2 - 1, False)
            second(NGRP - 2, 0, NGRP // 2 - 1, "v")
            second(NGRP - 1, 1, NGRP // 2 - 1, "v")

        with nc.Block() as block:
            @block.sync
            def _(sp):
                def load_u(g, p):
                    sp.dma_start(u[:, p, :, :, :].rearrange("p a b c -> p (a b c)"), uT_dram[bass.ds(g, 1), :, :].rearrange("a p x -> p (a x)")).then_inc(u_in[p], 16)

                def load_rest(g, p):
                    sp.dma_start(gates[:, p, :, :], grids[:, :, bass.ds(g * GI, GI), :].rearrange("b p c t -> p b (c t)")).then_inc(g_in[p], 16)
                    sp.dma_start(v[:, p, :, :].rearrange("p a b -> p (a b)"), v_dram[:, bass.ds(g * GI * D, GI * D)]).then_inc(v_in[p], 16)

                for p in range(2):
                    load_u(p, p)
                    load_rest(p, p)
                with sp.Fori(1, NGRP // 2) as m:
                    for p in range(2):
                        sp.wait_ge(dots, (m * 2 + p - 1) * GI)
                        load_u(m * 2 + p, p)
                        sp.wait_ge(sums, (m * 2 + p - 1) * KD)
                        load_rest(m * 2 + p, p)

            @block.gpsimd
            def _(pool):
                def gather(g, p, table, places):
                    nc.gpsimd.tensor_copy(idx8[:, p, :], expert[:, bass.ds(places * PER, PER)]).then_inc(idx_ok, 1)
                    for c in range(PER):
                        pool.wait_ge(row_used, g * PER + c + 1)
                        if c == 0:
                            pool.wait_ge(idx_ok, g + 1)
                        pool.sem_inc(slot_taken, 1)
                        pool.indirect_dma_start(rows[:, c % RING, :], None, table, bass.IndirectOffsetOnAxis(ap=idx8[:, p, c:c + 1], axis=0)).then_inc(row_in[c % RING], 16)

                with pool.Fori(0, MID) as m:
                    for p in range(2):
                        gather(m * 2 + p, p, u_rows, m * 2 + p)
                with pool.Fori(MID, NGRP // 2) as m:
                    for p in range(2):
                        gather(m * 2 + p, p, v_rows, m * 2 + p - 2 * MID)

            @block.tensor
            def _(pe):
                def first(g, p, m, start):
                    pe.wait_ge(u_in[p], m * 16 + 16)
                    for j in range(GI):
                        if not start:
                            pe.wait_ge(gelus, g * GI + j - 3)
                        for k in range(KD):
                            mm = nc.tensor.matmul(bank[:, j, 0:DENSE], u[:, p, j, k, :], xT[:, k, 0:DENSE], start=k == 0, stop=k == KD - 1)
                        mm.then_inc(dots, 1)

                def second(g, p, m, which):
                    pe.wait_ge(v_in[p], m * 16 + 16)
                    pe.wait_ge(weighed, g * GI + GI)
                    for c in range(KD):
                        pe.wait_ge(added, g * KD + c + 1)
                        for j in range(GI):
                            mm = nc.tensor.matmul(bank[:, 4 + c % 4, 0:DENSE], v[:, p, j, c * P:(c + 1) * P], w[:, p, j, :], start=j == 0, stop=j == GI - 1)
                        mm.then_inc(sums, 1)
                halves(pe, first, second, lambda: None)

            @block.scalar
            def _(act):
                def first(g, p, m, start):
                    for j in range(GI):
                        act.wait_ge(dots, g * GI + j + 1)
                        if not start or j >= 2:
                            act.wait_ge(weighed, g * GI + j - 1)
                        nc.scalar.activation(act_s[:, j % 2, :], bank[:, j, 0:DENSE], ACT.Gelu).then_inc(gelus, 1)

                def between():
                    act.wait_ge(dot_ok, 2 * MID)
                    nc.scalar.activation(dot[:, :], dot[:, :], ACT.Gelu).then_inc(weight_ok, 1)
                halves(act, first, lambda g, p, m, which: None, between)

            @block.vector
            def _(dve):
                V = nc.vector
                for i in range(4):
                    V.memset(yT[:, 2 * i:2 * i + 2, :], 0.0).then_inc(added, 1)
                    V.memset(y_rows[:, i * 256:(i + 1) * 256], 0.0).then_inc(row_used, 1)

                def first(g, p, m, start):
                    dve.wait_ge(g_in[p], m * 16 + 16)
                    for j in range(GI):
                        dve.wait_ge(gelus, g * GI + j + 1)
                        V.tensor_tensor(w[:, p, j, :].rearrange("p (b t) -> p b t", t=BLK), act_s[:, j % 2, :].rearrange("p (b t) -> p b t", t=BLK),
                                        gates[:, p, :, j * BLK:(j + 1) * BLK], ALU.mult).then_inc(weighed, 1)

                def second(g, p, m, which):
                    if which == "v":
                        V.tensor_copy(some[:, p, :], weight[:, bass.ds((g - 2 * MID) * PER, PER)]).then_inc(some_ok, 1)
                        dve.wait_ge(some_ok, g - 2 * MID + 1)
                    for c in range(KD):
                        dve.wait_ge(sums, g * KD + c + 1)
                        V.tensor_tensor(yT[:, c, :], yT[:, c, :], bank[:, 4 + c % 4, 0:DENSE], ALU.add).then_inc(added, 1)
                        dve.wait_ge(row_in[c % RING], (g * 2 + (c // RING + 1)) * 16)
                        r = rows[:, c % RING, :]
                        if which == "u":
                            V.tensor_tensor_reduce(r, r, x_rows, 1.0, 0.0, ALU.mult, ALU.add, some[:, p, c:c + 1]).then_inc(row_used, 1)
                        else:
                            dve.wait_ge(row_used, g * PER + c + 4)
                            V.scalar_tensor_tensor(out=y_rows, in0=r, scalar=some[:, p, c:c + 1], in1=y_rows, op0=ALU.mult, op1=ALU.add).then_inc(row_used, 1)
                    if which == "u":
                        dve.wait_ge(row_used, g * PER + PER + 4)
                        V.tensor_copy(dot[:, bass.ds(g * PER, PER)], some[:, p, :]).then_inc(dot_ok, 1)

                def between():
                    dve.wait_ge(weight_ok, 1)
                    V.tensor_tensor(weight[:, :], dot[:, :], gate, ALU.mult).then_inc(weight_ok, 1)
                    dve.wait_ge(weight_ok, 2)
                halves(dve, first, second, between)


def peer_norm(nc, name, C, yT, y_rows, gain_dram, shift_dram, x):
    with Stage(nc, name) as st:
        gain, shift = st.sb("gain", [P, D]), st.sb("shift", [P, D])
        pad = st.sb("pad", [P, KD, P])
        stats, mv = st.sb("stats", [P, 2, 6]), st.sb("mv", [P, 6])
        bank = st.banks("bank", 4)
        here, padded = st.sem("rows_loaded"), st.sem("samples_padded")
        turned, added = st.sem("turned"), st.sem("residual_added")
        s_sum, s_root, s_norm, chain = st.sem("statistics"), st.sem("deviation"), st.sem("normed"), st.sem("vector_chain")
        with nc.Block() as block:
            @block.sync
            def _(sp):
                sp.dma_start(gain[:, :], gain_dram.partition_broadcast(P)).then_inc(here, 16)
                sp.dma_start(shift[:, :], shift_dram.partition_broadcast(P)).then_inc(here, 16)

            @block.gpsimd
            def _(pool):
                nc.gpsimd.memset(pad[:, :, :], 0.0).then_inc(padded, 1)
                pool.wait_ge(padded, 1)
                nc.gpsimd.tensor_copy(pad[:, :, :].rearrange("p k (b s) -> p k b s", s=SEG)[:, :, :, 1:1 + NS],
                                      yT[:, :, SAMP_AT:DENSE].rearrange("p k (b s) -> p k b s", s=NS)).then_inc(padded, 1)

            @block.tensor
            def _(pe):
                for t in range(TILES):
                    if t == GT:
                        continue
                    if t == SAMP:
                        pe.wait_ge(padded, 2)
                    if t >= 2:
                        pe.wait_ge(added, t - 1)
                    for k in range(KD):
                        src = yT[:, k, t * P:(t + 1) * P] if t < SAMP else pad[:, k, :]
                        mm = nc.tensor.transpose(bank[:, 2 * (t % 2) + k // 4, k % 4 * P:(k % 4 + 1) * P], src, C["ident"])
                    mm.then_inc(turned, 1)

            @block.scalar
            def _(act):
                for t in range(TILES):
                    layer_norm_scalar(nc, act, x, t, s_sum, s_root, s_norm, mv)

            @block.vector
            def _(dve):
                ch = Chain(dve, chain)
                dve.wait_ge(here, 32)
                for t in range(TILES):
                    if t != GT:
                        dve.wait_ge(turned, t + 1 - (t > GT))
                    nc.vector.scalar_tensor_tensor(out=x[:, t, :], in0=x[:, t, :], scalar=ALPHA,
                                                   in1=y_rows if t == GT else bank[:, 2 * (t % 2):2 + 2 * (t % 2), :].rearrange("p a b -> p (a b)"),
                                                   op0=ALU.mult, op1=ALU.add).then_inc(added, 1)
                    dve.wait_ge(added, t + 1)
                    layer_norm_vector(nc, dve, ch, x, t, s_sum, s_root, s_norm, stats, mv, gain[:, :], shift[:, :])


def mlstm(nc, C, A, proj, mix, O):
    VA = DV + 1
    PB = 3
    with Stage(nc, "mlstm") as st:
        sb, sem = st.sb, st.sem
        bias = sb("bias", [P, 2 * H])
        mh = sb("mh", [P, H * DV])
        g16, g16b = sb("g16", [P, 2 * H]), sb("g16b", [P, 2 * H])
        lf, e, m, mu_b = sb("lf", [P, H]), sb("e", [P, H]), sb("m", [P, H]), sb("mu_b", [P, 2 * H])
        mx, ml_bl = sb("mx", [P, H]), sb("ml_bl", [P, 2 * H])
        ex_in, ex = sb("ex_in", [P, 4, H]), sb("ex", [P, 4, H])
        Em = sb("Em", [P, H, P])
        big = sb("big", [P, H, P])
        qT, kT, qpT = (sb(n, [P, PAIRS, P]) for n in ("qT", "kT", "qpT"))
        attT = sb("attT", [P, H, P])
        qp, kw = sb("qp", [P, AW]), sb("kw", [P, AW])
        va = sb("va", [P, H, VA])
        den = sb("den", [P, 3, H])
        ms = sb("ms", [P, 3, H])
        Sp = sb("Sp", [P, PAIRS, VA])
        Ss = sb("Ss", [P, NB, PAIRS, VA])
        dsel, dec = sb("dsel", [P, NB, H]), sb("dec", [P, NB, H])
        bank = st.banks("bank", 8)
        here, init = sem("arrays_loaded"), sem("state_zeroed")
        pre, cap, cap2, em, ln = sem("gate_sums"), sem("gate_tanh"), sem("gates_capped"), sem("forget_exp"), sem("forget_log")
        lf_ok, cum, diag, ebc, mu_ok, lastr = sem("log_forget"), sem("cumulated"), sem("diagonals"), sem("e_spread"), sem("mu_ready"), sem("last_rows")
        emx, exq, exs = sem("score_exponents"), sem("small_exponents"), sem("exps")
        qk_t, qk_tk, qk, att, att_t, att_tk = sem("qk_turned"), sem("qk_turned_kept"), sem("qk_products"), sem("weights_ready"), sem("weights_turned"), sem("weights_turned_kept")
        qp_ok, num, sig, ms_ok, root = sem("scaled_ready"), sem("numerators"), sem("output_gates"), sem("mean_squares"), sem("roots")
        spread, spread_used, stp, tile_ok, dsel_ok = sem("spread_ready"), sem("spread_used"), sem("state_products"), sem("tile_done"), sem("decay_rows")
        chain, outs, dcol = sem("vector_chain"), sem("outputs_stored"), sem("decays_spread")
        NUM = ((5, 6), (7, 0))
        hb = lambda h: bank[:, NUM[h % 2][h // 2 // PB], h // 2 % PB * VA:(h // 2 % PB + 1) * VA]

        with nc.Block() as block:
            @block.sync
            def _(sp):
                for dst, src in ((bias[:, 0:H], A["b_i_o"].partition_broadcast(P)), (bias[:, H:2 * H], A["b_f_o"].partition_broadcast(P)),
                                 (mh[:, :], A["mh_norm_o"].partition_broadcast(P)), (Ss[:, :, :, :], A["cn_s"])):
                    sp.dma_start(dst, src).then_inc(here, 16)
                sp.wait_ge(tile_ok, SAMP)
                sp.dma_start(O["cn_p"], Sp[:, :, :]).then_inc(outs, 16)
                sp.dma_start(O["m_p"], m[:, :]).then_inc(outs, 16)
                sp.wait_ge(outs, 32)
                sp.dma_start(m[:, :], A["m_s"]).then_inc(here, 16)
                sp.wait_ge(tile_ok, TILES)
                sp.dma_start(O["cn_s"], Ss[:, :, :, :]).then_inc(outs, 16)
                sp.dma_start(O["m_s"], m[:, :]).then_inc(outs, 16)
                sp.wait_ge(outs, 64)

            @block.tensor
            def _(pe):
                mmul, turn_ = nc.tensor.matmul, nc.tensor.transpose
                for t in range(TILES):
                    one = t < SAMP
                    q, k = proj[:, t, 0:AW], proj[:, t, AW:2 * AW]
                    if t:
                        pe.wait_ge(tile_ok, t)
                    for i, x in enumerate((q, k)):
                        for p in range(PAIRS):
                            mm = turn_(bank[:, 3 + i, p * P:(p + 1) * P], x[:, p * P:(p + 1) * P], C["ident"])
                    mm.then_inc(qk_t, 1)
                    pe.wait_ge(qk_tk, 2 * (t + 1))
                    for g in range(2):
                        for p in range(PAIRS):
                            mm = mmul(bank[:, 5 + g, p * P:(p + 1) * P], qT[g * 64:(g + 1) * 64, p, :], kT[g * 64:(g + 1) * 64, p, :], start=True, stop=True)
                    mm.then_inc(qk, 1)
                    pe.wait_ge(lf_ok, t + 1)
                    mmul(bank[:, 0, 0:H], C["upto" if one else "upto16"], lf[:, :], start=True, stop=True).then_inc(cum, 1)
                    pe.wait_ge(diag, t + 1)
                    for i in range(2):
                        mm = mmul(bank[:, 1 + i, :], C["ones"], big[:, 4 * i:4 * i + 4, :].rearrange("p a b -> p (a b)"), start=True, stop=True)
                    mm.then_inc(ebc, 1)
                    pe.wait_ge(mu_ok, t + 1)
                    mmul(bank[:, 0, 2 * H:4 * H], C["last" if one else "last_s"], mu_b[:, :], start=True, stop=True).then_inc(lastr, 1)
                    pe.wait_ge(qp_ok, t + 1)
                    for p in range(PAIRS):
                        mm = turn_(bank[:, 3, p * P:(p + 1) * P], qp[:, p * P:(p + 1) * P], C["ident"])
                    mm.then_inc(qk_t, 1)
                    pe.wait_ge(att, t + 1)
                    for h in range(H):
                        mm = turn_(bank[:, 1 + h // 4, h % 4 * P:(h % 4 + 1) * P], big[:, h, :], C["ident"])
                    mm.then_inc(att_t, 1)
                    pe.wait_ge(att_tk, 3 * (t + 1))
                    for h in range(H):
                        p, g = h // 2, h % 2
                        half = slice(g * 64, (g + 1) * 64)
                        mm = mmul(hb(h), attT[:, h, :], va[:, h, :], start=True, stop=False)
                        if one:
                            mm = mmul(hb(h), qpT[half, p, :], Sp[half, p, :], start=False, stop=True)
                        else:
                            if g == 0:
                                pe.wait_ge(spread, p + 1)
                            for b in range(NB):
                                mm = mmul(hb(h), big[half, b, :], Ss[half, b, p, :], start=False, stop=b == NB - 1)
                            if g:
                                mm.then_inc(spread_used, 1)
                    mm.then_inc(num, 1) if one else None
                    if one:
                        for h in range(H):
                            p, g = h // 2, h % 2
                            mm = mmul(bank[g * 64:(g + 1) * 64, 1 + p // PB, p % PB * VA:(p % PB + 1) * VA], kw[:, h * 64:(h + 1) * 64], va[:, h, :], start=True, stop=True)
                        mm.then_inc(stp, 1)
                    else:
                        pe.wait_ge(dsel_ok, 1)
                        mmul(bank[:, 3, 0:NB * H], C["ones"], dsel[:, :, :].rearrange("p a b -> p (a b)"), start=True, stop=True).then_inc(dcol, 1)
                        for p in range(PAIRS):
                            pe.wait_ge(spread, PAIRS + p + 1)
                            for g in range(2):
                                for b in range(NB):
                                    mm = mmul(bank[g * 64:(g + 1) * 64, 1 + b // 2, b % 2 * VA:(b % 2 + 1) * VA], big[:, b, g * 64:(g + 1) * 64], va[:, 2 * p + g, :],
                                              start=True, stop=True)
                            mm.then_inc(stp, 1)

            @block.scalar
            def _(act):
                a_, cp = nc.scalar.activation, nc.scalar.copy
                flat = lambda x: x[:, :, :].rearrange("p a b -> p (a b)")
                for t in range(TILES):
                    act.wait_ge(qk_t, 2 * t + 1)
                    cp(flat(qT), bank[:, 3, :]).then_inc(qk_tk, 1)
                    cp(flat(kT), bank[:, 4, :]).then_inc(qk_tk, 1)
                    act.wait_ge(pre, t + 1)
                    a_(g16b[:, :], g16[:, :], ACT.Tanh, scale=1.0 / CAP).then_inc(cap, 1)
                    act.wait_ge(cap2, t + 1)
                    a_(lf[:, :], g16[:, H:2 * H], ACT.Exp, scale=-1.0).then_inc(em, 1)
                    act.wait_ge(em, 2 * t + 2)
                    a_(lf[:, :], lf[:, :], ACT.Ln).then_inc(ln, 1)
                    act.wait_ge(exq, t + 1)
                    a_(flat(ex), flat(ex_in), ACT.Exp).then_inc(exs, 1)
                    act.wait_ge(emx, t + 1)
                    a_(flat(Em), flat(Em), ACT.Exp).then_inc(exs, 1)
                    act.wait_ge(qk_t, 2 * t + 2)
                    cp(flat(qpT), bank[:, 3, :]).then_inc(att_tk, 1)
                    act.wait_ge(att_t, t + 1)
                    for i in range(2):
                        cp(attT[:, 4 * i:4 * i + 4, :].rearrange("p a b -> p (a b)"), bank[:, 1 + i, :]).then_inc(att_tk, 1)
                    o = proj[:, t, 2 * AW + H * DV:2 * AW + 2 * H * DV]
                    a_(o, o, ACT.Sigmoid).then_inc(sig, 1)
                    act.wait_ge(ms_ok, t + 1)
                    a_(ms[:, 2, :], ms[:, 1, :], ACT.Sqrt).then_inc(root, 1)

            @block.vector
            def _(dve):
                V = nc.vector
                ch = Chain(dve, chain)
                tt, tsc, stt = V.tensor_tensor, V.tensor_scalar, V.scalar_tensor_tensor
                flat = lambda x: x.rearrange("p a b -> p (a b)")
                V.memset(va[:, :, DV:VA], 1.0)
                ch(V.memset(Sp[:, :, :], 0.0))
                ch(V.memset(m[:, :], 0.0))
                dve.wait_ge(here, 64)
                for t in range(TILES):
                    one = t < SAMP
                    q, k, v = proj[:, t, 0:AW], proj[:, t, AW:2 * AW], proj[:, t, 2 * AW:2 * AW + H * DV]
                    gates = proj[:, t, INO - 2 * H:INO]
                    h3 = lambda x: x.rearrange("p (h d) -> p h d", h=H)
                    if not one:
                        dve.wait_ge(here, 80)
                    tt(g16[:, :], gates, bias[:, :], ALU.add).then_inc(pre, 1)
                    V.tensor_copy(va[:, :, 0:DV], h3(v))
                    dve.wait_ge(cap, t + 1)
                    tsc(g16[:, :], g16b[:, :], CAP, None, ALU.mult).then_inc(cap2, 1)
                    dve.wait_ge(em, 2 * t + 1)
                    tsc(lf[:, :], lf[:, :], 1.0, None, ALU.add).then_inc(em, 1)
                    dve.wait_ge(ln, t + 1)
                    if not one:
                        ch(tsc(lf[:, :], lf[:, :], C["real"], None, ALU.mult))
                    tsc(lf[:, :], lf[:, :], -1.0, None, ALU.mult).then_inc(lf_ok, 1)
                    dve.wait_ge(cum, t + 1)
                    ch(V.tensor_copy(mu_b[:, H:2 * H], bank[:, 0, 0:H]))
                    ch(tt(e[:, :], g16[:, 0:H], mu_b[:, H:2 * H], ALU.subtract))
                    tt(big[:, :, :], mid(C["ident"], H), last(e[:, :], P), ALU.mult).then_inc(diag, 1)
                    dve.wait_ge(ebc, t + 1)
                    ch(tt(Em[:, :, :], bank[:, 1:3, :].rearrange("p a (h x) -> p (a h) x", x=P), mid(C["causal" if one else "causal_s"], H), ALU.add))
                    ch(V.tensor_reduce(mx[:, :], Em[:, :, :], AX, ALU.max))
                    tt(mu_b[:, 0:H], mx[:, :], m[:, :], ALU.max).then_inc(mu_ok, 1)
                    dve.wait_ge(mu_ok, t + 1)
                    tt(Em[:, :, :], Em[:, :, :], last(mu_b[:, 0:H], P), ALU.subtract).then_inc(emx, 1)
                    tt(ex_in[:, 0, :], m[:, :], mu_b[:, 0:H], ALU.subtract)
                    stt(ex_in[:, 1, :], mu_b[:, 0:H], -1.0, mu_b[:, H:2 * H], ALU.mult, ALU.subtract)
                    dve.wait_ge(lastr, t + 1)
                    ch(V.tensor_copy(ml_bl[:, :], bank[:, 0, 2 * H:4 * H]))
                    tt(ex_in[:, 2, :], e[:, :], ml_bl[:, 0:H], ALU.subtract)
                    tt(ex_in[:, 3, :], m[:, :], ml_bl[:, 0:H], ALU.subtract).then_inc(exq, 1)
                    dve.wait_ge(exq, t + 1)
                    tt(m[:, :], ml_bl[:, 0:H], ml_bl[:, H:2 * H], ALU.add)
                    dve.wait_ge(exs, 2 * (t + 1))
                    stt(h3(qp[:, :]), h3(q), HD ** -0.5, last(ex[:, 0, :], 64), ALU.mult, ALU.mult).then_inc(qp_ok, 1)
                    if not one:
                        ch(tsc(ex[:, 2, :], ex[:, 2, :], C["real"], None, ALU.mult))
                    ch(tt(h3(kw[:, :]), h3(k), last(ex[:, 2, :], 64), ALU.mult))
                    dve.wait_ge(qk, t + 1)
                    b4 = big[:, :, :].rearrange("p (q g) x -> p q g x", g=2)
                    e4 = Em[:, :, :].rearrange("p (q g) x -> p q g x", g=2)
                    for g in range(2):
                        ins = stt(b4[:, :, g, :], bank[:, 5 + g, :].rearrange("p (q x) -> p q x", x=P), HD ** -0.5, e4[:, :, g, :], ALU.mult, ALU.mult)
                    ins.then_inc(att, 1)
                    if not one:
                        dve.wait_ge(att_tk, 3 * (t + 1))
                        for p in range(PAIRS):
                            if p:
                                dve.wait_ge(spread_used, p)
                            tt(big[:, :, :], mid(qpT[:, p, :], NSEG), C["seg_of_col"].rearrange("p (c x) -> p c x", x=P), ALU.mult).then_inc(spread, 1)
                        dve.wait_ge(spread_used, PAIRS)
                        tt(dsel[:, :, :], mid(ex[:, 3, :], NB), last(C["newest"], H), ALU.mult).then_inc(dsel_ok, 1)
                        dve.wait_ge(dcol, 1)
                        ch(V.tensor_copy(flat(dec[:, :, :]), bank[:, 3, 0:NB * H]))
                        for p in range(PAIRS):
                            tt(big[:, :, :], mid(kw[:, p * P:(p + 1) * P], NSEG), last(C["seg_of_row"], P), ALU.mult).then_inc(spread, 1)
                            for g in range(2):
                                half = slice(g * 64, (g + 1) * 64)
                                ins = tt(Ss[half, :, p, :], Ss[half, :, p, :], dec[half, :, 2 * p + g:2 * p + g + 1].to_broadcast([64, NB, VA]), ALU.mult)
                            ch(ins)
                            dve.wait_ge(stp, SAMP + p + 1)
                            s4 = Ss[:, :, p, :].rearrange("p (a c) x -> p a c x", c=2)
                            ch(tt(s4, s4, bank[:, 1:5, 0:2 * VA].rearrange("p a (c x) -> p a c x", x=VA), ALU.add))
                    else:
                        dve.wait_ge(num, t + 1)
                        dve.wait_ge(stp, t + 1)
                        for h in range(H):
                            p, g = h // 2, h % 2
                            half = slice(g * 64, (g + 1) * 64)
                            ins = stt(Sp[half, p, :], Sp[half, p, :], ex[half, 3, h:h + 1], bank[half, 1 + p // PB, p % PB * VA:(p % PB + 1) * VA], ALU.mult, ALU.add)
                        ch(ins)
                    for h in range(H):
                        ins = V.tensor_copy(den[:, 0, h:h + 1], hb(h)[:, DV:VA])
                    ch(ins)
                    ch(tsc(den[:, 1, :], den[:, 0, :], -1.0, None, ALU.mult))
                    ch(tt(den[:, 0, :], den[:, 0, :], den[:, 1, :], ALU.max))
                    ch(tt(den[:, 0, :], den[:, 0, :], ex[:, 1, :], ALU.max))
                    ch(V.reciprocal(den[:, 2, :], den[:, 0, :]))
                    d4 = den[:, 2, :].rearrange("p (q g) -> p q g", g=2)
                    for g in range(2):
                        for i, n in enumerate((PB, PAIRS - PB)):
                            a = slice(i * PB, i * PB + n)
                            ins = tt(e4[:, a, g, :], bank[:, NUM[g][i], 0:n * VA].rearrange("p (q x) -> p q x", x=VA)[:, :, 0:DV], last(d4[:, a, g], DV), ALU.mult)
                    ch(ins)
                    ch(tt(big[:, :, :], Em[:, :, :], Em[:, :, :], ALU.mult))
                    ch(V.tensor_reduce(ms[:, 0, :], big[:, :, :], AX, ALU.add))
                    tsc(ms[:, 1, :], ms[:, 0, :], 1.0 / DV, 1e-6, ALU.mult, ALU.add).then_inc(ms_ok, 1)
                    dve.wait_ge(root, t + 1)
                    ch(V.reciprocal(ms[:, 0, :], ms[:, 2, :]))
                    ch(tt(Em[:, :, :], Em[:, :, :], last(ms[:, 0, :], DV), ALU.mult))
                    ch(tt(flat(Em[:, :, :]), flat(Em[:, :, :]), mh[:, :], ALU.mult))
                    dve.wait_ge(sig, t + 1)
                    tt(mix[:, t, :], flat(Em[:, :, :]), proj[:, t, 2 * AW + H * DV:2 * AW + 2 * H * DV], ALU.mult).then_inc(tile_ok, 1)
                    dve.wait_ge(tile_ok, t + 1)


def build(nc, A, O):
    with ExitStack() as ctx:
        consts = ctx.enter_context(nc.sbuf_tensor("const_tile", [P, CONST_N], F32))
        C = {k: consts[:, CONST_AT[k]:CONST_AT[k] + w] for k, w in CONST_COLS.items()}
        load(nc, [(consts[:, :], A["consts"])])
        with nc.sbuf_tensor("mix_a", [P, TILES, AW], F32) as mix_a, nc.sbuf_tensor("mix_b", [P, TILES, AW], F32) as mix_b:
            for part, (lo, hi), mixer, mix in ((0, (0, RW), rwkv, mix_a), (1, (RW, INE), mla, mix_b)):
                with nc.sbuf_tensor(f"proj_e{part}", [P, TILES, hi - lo], F32) as proj:
                    with nc.sbuf_tensor(f"xT_e{part}", [P, KD, TILES * P], F32) as xT:
                        load(nc, [(xT[:, :, :], A["xT0"].rearrange("(k p) t -> p k t", p=P))])
                        project(nc, f"in_e{part}", A["w_in_e"][:, lo:hi], hi - lo, xT, proj)
                    mixer(nc, C, A, proj, mix, O)
            with nc.sbuf_tensor("x_e", [P, TILES, D], F32) as x:
                load(nc, [(x[:, :, :], A["x0"].rearrange("(t p) d -> p t d", p=P))])
                half = lambda t, k: (mix_a if k < 4 else mix_b)[:, t, k % 4 * P:(k % 4 + 1) * P]
                out_project(nc, "out_e", C, half, A["w_out_e"], A["ln1_g0"], A["ln1_b0"], x)
                store(nc, [(A["x_mid"].rearrange("(t p) d -> p t d", p=P), x[:, :, :])])
        x = ctx.enter_context(nc.sbuf_tensor("x", [P, TILES, D], F32))
        load(nc, [(x[:, :, :], A["x_mid"].rearrange("(t p) d -> p t d", p=P))])
        peer(nc, 0, C, A, x)
        with nc.sbuf_tensor("mix_o", [P, TILES, D], F32) as mix:
            with nc.sbuf_tensor("proj_o", [P, TILES, INO], F32) as proj:
                with nc.sbuf_tensor("xT_o", [P, KD, TILES * P], F32) as xT:
                    turn(nc, "turn_o", C, x, xT, False)
                    project(nc, "in_o", A["w_in_o"], INO, xT, proj)
                mlstm(nc, C, A, proj, mix, O)
            out_project(nc, "out_o", C, lambda t, k: mix[:, t, k * P:(k + 1) * P], A["w_out_o"], A["ln1_g1"], A["ln1_b1"], x)
        peer(nc, 1, C, A, x)
        store(nc, [(O["y"].rearrange("(t p) d -> p t d", p=P), x[:, :, :]),
                   (O["shift"][0:1, :], A["x0"][SEQ - 1:SEQ, :]),
                   (O["shift"][1:1 + NB, :], A["x0"][SEQ:, :].rearrange("(b s) d -> b s d", s=SEG)[:, NS, :])])


def peer(nc, layer, C, A, x):
    n = str(layer)
    with (nc.sbuf_tensor("xT_p" + n, [P, KD, TOK], F32) as xT, nc.sbuf_tensor("expert" + n, [P, HK], U32) as expert,
          nc.sbuf_tensor("gate" + n, [P, HK], F32) as gate):
        turn(nc, "turn_p" + n, C, x, xT, True)
        with nc.sbuf_tensor("picks" + n, [P, 3, DENSE], F32) as picks:
            peer_select(nc, "select" + n, C, xT, A["wq" + n], A["k1T" + n], A["k2T" + n], picks, expert[:, :], gate[:, :])
            peer_spread(nc, "spread" + n, C, picks, A["grids"])
        with nc.sbuf_tensor("yT" + n, [P, KD, DENSE], F32) as yT, nc.sbuf_tensor("yrows" + n, [P, D], F32) as y_rows:
            peer_experts(nc, "experts" + n, xT, x[:, GT, :], expert, gate[:, :], A["uT" + n], A["v" + n],
                         A["u_rows" + n], A["v_rows" + n], A["grids"], yT, y_rows[:, :])
            peer_norm(nc, "norm" + n, C, yT, y_rows[:, :], A["ln2_g" + n], A["ln2_b" + n], x)


def store(nc, pairs):
    with Stage(nc, f"store{nc.next_id()}") as st:
        sent = st.sem("arrays_stored")
        with nc.Block() as block:
            @block.sync
            def _(sp):
                for dst, src in pairs:
                    sp.dma_start(dst, src).then_inc(sent, 16)
                sp.wait_ge(sent, 16 * len(pairs))


def load(nc, pairs):
    with Stage(nc, f"load{nc.next_id()}") as st:
        here = st.sem("arrays_loaded")
        with nc.Block() as block:
            @block.sync
            def _(sp):
                for dst, src in pairs:
                    sp.dma_start(dst, src).then_inc(here, 16)
                sp.wait_ge(here, 16 * len(pairs))


def layouts(i):
    f = lambda a: np.ascontiguousarray(a)
    pad = np.zeros((NB, SEG, D), np.float32)
    pad[:, 0] = i["state_shift"][0]
    pad[:, 1:1 + NS] = i["x_sample"]
    x0 = np.concatenate([i["x_prompt"][0], pad.reshape(P, D)], 0)
    a = {"x0": x0, "xT0": f(x0.T)}
    for n in ("w_in_e", "mu_e", "w0_e", "w2_e", "a0_e", "a2_e", "g2_e", "kk_e", "ka_e", "lnx_w_e", "lnx_b_e"):
        a[n] = i[n][0]
    a["rk_e"] = i["rk_e"][0].reshape(-1)
    w = np.zeros((NB, PAIRS, 2, HD, 2, HD), np.float32)
    s = i["state_wkv"][0].reshape(NB, PAIRS, 2, HD, HD)
    for g in range(2):
        w[:, :, g, :, g, :] = s[:, :, g].transpose(0, 1, 3, 2)
    a["wkv_s"] = w.reshape(NB, PAIRS, P, P)
    a["w_uq_e"], a["q_norm_e"], a["kv_norm_e"] = i["w_uq_e"][0], i["q_norm_e"][0], i["kv_norm_e"][0]
    a["w_uk_e"], a["w_uv_e"] = i["w_uk_e"][0].reshape(KV, -1), i["w_uv_e"][0].reshape(KV, -1)
    a["w_ukT_e"] = f(i["w_uk_e"][0].transpose(2, 1, 0))
    a["page_table"] = i["page_table"].reshape(1, -1)
    c = i["cache_ckv"][0]
    a["cache_ckv"] = c
    keys = np.concatenate([c, i["cache_kpe"][0]], 2)
    a["keysT"] = f(keys.reshape(-1, PAGE, 3, HD + RP).transpose(0, 3, 2, 1)).reshape(-1, HD + RP, 3 * PAGE)
    a["w_out_e"], a["w_in_o"], a["w_out_o"] = i["w_out_e"][0], i["w_in_o"][0], i["w_out_o"][0]
    for l in range(2):
        n = str(l)
        for k in ("ln1_g", "ln1_b", "ln2_g", "ln2_b"):
            a[k + n] = i[k][l]
        a["wq" + n], a["k1T" + n], a["k2T" + n] = i["peer_wq"][l], f(i["peer_k1"][l].T), f(i["peer_k2"][l].T)
        u = i["peer_u"][l].reshape(NK, NGRP, GI, KD, P)
        a["uT" + n] = f(u.transpose(1, 4, 2, 3, 0)).reshape(NGRP, P, GI * KD * NK)
        a["v" + n] = i["peer_v"][l].reshape(NK, NK * D)
        a["u_rows" + n], a["v_rows" + n] = i["peer_u"][l], i["peer_v"][l]
    a["b_i_o"], a["b_f_o"], a["mh_norm_o"] = i["b_i_o"][0], i["b_f_o"][0], i["mh_norm_o"][0]
    cn = np.concatenate([i["state_mlstm_c"][0], i["state_mlstm_n"][0][:, :, None, :]], 2)
    cn = cn.reshape(NB, PAIRS, 2, DV + 1, HD).transpose(2, 4, 0, 1, 3)
    a["cn_s"] = f(cn).reshape(P, NB, PAIRS, DV + 1)
    a["m_s"] = np.repeat(i["state_mlstm_m"][0], SEG, axis=0)
    a["consts"] = np.concatenate(list(constants().values()), 1)
    return a


OUTPUTS = {"cn_p": (P, PAIRS, DV + 1), "cn_s": (P, NB, PAIRS, DV + 1), "m_p": (P, H), "m_s": (P, H), "y": (TILES * P, D), "shift": (1 + NB, D), "ckv": (TILES * P, KV), "kpe": (TILES * P, RP), "wkv_p": (PAIRS, P, P), "wkv_s": (PAIRS, NB, P, P)}
SCRATCH = {"x_mid": (TILES * P, D), "grids": (NBLK, P, NK, BLK), "new_rows": (P, KV), "last_rows": (1, SAMP, RW)}


def kernel(**inputs):
    from concourse import bacc
    from concourse.bass_utils import run_bass_kernel_spmd

    given = layouts({k: np.asarray(v) for k, v in inputs.items()})
    nc = bacc.Bacc("TRN2", target_bir_lowering=False, num_devices=1)
    A, O, arrays = {}, {}, {}
    for n, v in given.items():
        arrays["in_" + n] = np.ascontiguousarray(v)
        A[n] = nc.dram_tensor("in_" + n, v.shape, mybir.dt.from_np(v.dtype), kind="ExternalInput").ap()
    for n, shape in SCRATCH.items():
        A[n] = nc.dram_tensor("scratch_" + n, shape, F32, kind="Internal").ap()
    for n, shape in OUTPUTS.items():
        O[n] = nc.dram_tensor("out_" + n, shape, F32, kind="ExternalOutput").ap()
    build(nc, A, O)
    r = run_bass_kernel_spmd(nc, [arrays], core_ids=[0]).results[0]
    got = {n: np.asarray(r["out_" + n]) for n in OUTPUTS}

    def rows(a):
        return a[:SEQ][None], a[SEQ:].reshape(NB, SEG, -1)[:, 1:1 + NS]

    def wkv(a):
        a = a.reshape(PAIRS, -1, 2, HD, 2, HD)
        a = np.stack([a[:, :, g, :, g, :] for g in range(2)], 2)
        return a.transpose(1, 0, 2, 4, 3).reshape(-1, H, HD, HD)[None]

    def cell(a):
        a = a.reshape(2, HD, -1, PAIRS, DV + 1).transpose(2, 3, 0, 4, 1).reshape(-1, H, DV + 1, HD)
        return a[None, :, :, :DV], a[None, :, :, DV]

    y_p, y_s = rows(got["y"])
    ckv_p, ckv_s = rows(got["ckv"])
    kpe_p, kpe_s = rows(got["kpe"])
    c_p, n_p = cell(got["cn_p"])
    c_s, n_s = cell(got["cn_s"])
    out = (y_p, y_s, ckv_p[None], kpe_p[None], ckv_s[None], kpe_s[None],
           got["shift"][None, 0:1], got["shift"][None, 1:], wkv(got["wkv_p"][:, None]), wkv(got["wkv_s"]),
           c_p, c_s, n_p, n_s, got["m_p"][None, 0:1], got["m_s"][None, ::SEG])
    return tuple(np.ascontiguousarray(a) for a in out)
```

```python
from contextlib import ExitStack

import numpy as np
import concourse.bass as bass
from concourse import mybir

ALU = mybir.AluOpType
ACT = mybir.ActivationFunctionType
F32 = mybir.dt.float32
U32 = mybir.dt.uint32
AX = mybir.AxisListType.X

P = 128
D = 1024
KD = D // P
SEQ = 512
NB = 8
NS = 4
TILES = SEQ // P + 1
SAMP = TILES - 1
SEG = 16
NSEG = P // SEG
TOK = SEQ + NB * NS
H = 8
HD = 64
AW = H * HD
PAIRS = H // 2
RW = 3 * AW + 64 + 64 + 128
QL, KV, RP = 384, 256, 32
INE = RW + QL + KV + RP
DV = 128
INO = 2 * AW + 2 * H * DV + 2 * H
NPAGE, PAGE = 32, 128
PAST = NPAGE * PAGE
ALPHA = 4.0 ** 0.25
SM = (64 + 32) ** -0.5
NEG = -1.0e30
NK = 128
PH, PK = 8, 16
HK = PH * PK
CAP = 15.0



def constants():
    r = np.arange(P)
    row, col = r[:, None], r[None, :]
    same = row // SEG == col // SEG
    real = (r % SEG >= 1) & (r % SEG <= NS)
    c = {}
    c["ident"] = row == col
    c["iota"] = np.broadcast_to(col, (P, P))
    c["upto16"] = same & (row <= col)
    c["before16"] = same & (row < col)
    c["after16"] = same & (row > col)
    c["upto"] = row <= col
    c["pair"] = row // HD == col // HD
    c["fold"] = row % HD == np.arange(HD)[None, :]
    c["seg_of_row"] = row // SEG == np.arange(NSEG)[None, :]
    c["seg_of_col"] = np.broadcast_to((np.arange(NSEG)[:, None] == r[None, :] // SEG).reshape(1, -1), (P, NSEG * P))
    c["real"] = real[:, None]
    c["ones"] = np.ones((P, P))
    c["negc"] = np.full((P, 1), -np.exp(-0.5))
    c["negc_real"] = real[:, None] * -np.exp(-0.5)
    c["causal"] = np.where(col <= row, 0.0, NEG)
    c["causal_s"] = np.where(same & (col <= row) & real[None, :], 0.0, NEG)
    c["last"] = (row == P - 1) & (col >= 0)
    c["last_s"] = row == SEG * (col // SEG) + NS
    c["newest"] = (row == SEG * np.arange(NSEG)[None, :] + NS)
    pos = np.concatenate([np.arange(SEQ), PAST + np.arange(P) % SEG - 1.0])
    inv = (np.float32(10000.0) ** (-np.arange(0, RP, 2, dtype=np.float32) / np.float32(RP))).astype(np.float32)
    ang = pos.astype(np.float32)[:, None] * inv[None, :]
    lay = lambda a: a.reshape(TILES, P, RP // 2).transpose(1, 0, 2).reshape(P, -1)
    c["cos"], c["sin"] = lay(np.cos(ang)), lay(np.sin(ang))
    q = r % NS
    s = np.arange(SEG)
    c["newmask"] = np.where((s[None, :] >= 1) & (s[None, :] <= q[:, None] + 1), 0.0, NEG)
    return {k: np.ascontiguousarray(v, dtype=np.float32) for k, v in c.items()}


CONST_COLS = {k: v.shape[1] for k, v in constants().items()}
CONST_AT, _n = {}, 0
for _k, _w in CONST_COLS.items():
    CONST_AT[_k] = _n
    _n += _w
CONST_N = _n


class Stage:

    def __init__(self, nc, name):
        self.nc, self.name, self.ctx, self.sems = nc, name, ExitStack(), []

    def sb(self, name, shape, dt=F32):
        return self.ctx.enter_context(self.nc.sbuf_tensor(f"{self.name}_{name}", shape, dt))

    def banks(self, name, n=1):
        return self.ctx.enter_context(self.nc.psum_tensor(f"{self.name}_{name}", [P, n, 512], F32))

    def sem(self, name):
        s = self.nc.alloc_semaphore(f"{self.name}_{name}")
        self.sems.append(s)
        return s

    def __enter__(self):
        return self

    def __exit__(self, *exc):
        self.ctx.close()
        if exc[0] is None:
            self.nc.clear_and_free_semaphores(self.sems)
            self.nc.all_engine_barrier()
        return False


class Chain:

    def __init__(self, eng, sem):
        self.eng, self.sem, self.n = eng, sem, 0

    def __call__(self, ins):
        self.n += 1
        ins.then_inc(self.sem, 1)
        self.eng.wait_ge(self.sem, self.n)


def mid(ap, n):
    return ap.unsqueeze(1).to_broadcast([ap.shape[0], n, ap.shape[1]])


def last(ap, n):
    return ap.unsqueeze(2).to_broadcast([ap.shape[0], ap.shape[1], n])


def project(nc, name, w_dram, n_cols, xT, out):
    chunks = [(a, min(512, n_cols - a)) for a in range(0, n_cols, 512)]
    with Stage(nc, name) as st:
        w = st.sb("w", [P, 2, KD, 512])
        acc = st.banks("acc", 4)
        w_in = [st.sem(f"w_loaded{i}") for i in range(2)]
        tile_done = st.sem("tile_multiplied")
        kept = [st.sem("kept_by_vector"), st.sem("kept_by_scalar")]
        wv = w_dram.rearrange("(k p) n -> p k n", p=P)
        with nc.Block() as block:
            @block.sync
            def _(sp):
                for n, (a, m) in enumerate(chunks):
                    if n >= 2:
                        sp.wait_ge(tile_done, TILES * (n - 1))
                    sp.dma_start(w[:, n % 2, :, 0:m], wv[:, :, a:a + m]).then_inc(w_in[n % 2], 16)

            @block.tensor
            def _(pe):
                for n, (a, m) in enumerate(chunks):
                    pe.wait_ge(w_in[n % 2], 16 * (n // 2 + 1))
                    for t in range(TILES):
                        i = n * TILES + t
                        if i >= 4:
                            pe.wait_ge(kept[i % 2], (i - 4) // 2 + 1)
                        for k in range(KD):
                            mm = nc.tensor.matmul(acc[:, i % 4, 0:m], xT[:, k, t * P:(t + 1) * P],
                                                  w[:, n % 2, k, 0:m], start=k == 0, stop=k == KD - 1)
                        mm.then_inc(tile_done, 1)

            def keep(eng, copy, par):
                for n, (a, m) in enumerate(chunks):
                    for t in range(TILES):
                        i = n * TILES + t
                        if i % 2 == par:
                            eng.wait_ge(tile_done, i + 1)
                            copy(out[:, t, a:a + m], acc[:, i % 4, 0:m]).then_inc(kept[par], 1)

            @block.vector
            def _(dve):
                keep(dve, nc.vector.tensor_copy, 0)

            @block.scalar
            def _(act):
                keep(act, nc.scalar.copy, 1)


def rwkv(nc, C, A, proj, mix, O):
    with Stage(nc, "rwkv") as st:
        sb, sem = st.sb, st.sem
        names = ["mu", "w0", "a0", "kk", "ka", "rk", "lnw", "lnb"]
        width = {"mu": RW}
        row = {n: sb("row_" + n, [P, width.get(n, AW)]) for n in names}
        wa2 = sb("wa2", [P, AW])
        g2 = sb("g2", [P, AW])
        lwaT = sb("lwaT", [P, P])
        lgT = sb("lgT", [P, P])
        a_s = sb("a", [P, AW])
        z_s = sb("z", [P, AW])
        g_s = sb("g", [P, AW])
        logd = sb("logd", [P, AW])
        kk = sb("kk", [P, AW])
        kp = sb("kp", [P, AW])
        tmp = sb("tmp", [P, 2 * AW])
        nrm = sb("nrm", [P, 4, H])
        e_in, e_neg, e_ex, e_rev = (sb(n, [P, AW]) for n in ("e_in", "e_neg", "e_ex", "e_rev"))
        e_chunk = sb("e_chunk", [P, PAIRS * NSEG])
        at, bt, kt, rt = e_ex, e_neg, sb("kt", [P, AW]), e_in
        bend, kend = e_rev, sb("kend", [P, AW])
        atT, btT, ktT, rtT = (sb(n, [P, PAIRS, P]) for n in ("atT", "btT", "ktT", "rtT"))
        mats = sb("mats", [P, 8, PAIRS, P])
        Wp, U0 = (sb(n, [P, PAIRS, 2, HD]) for n in ("Wp", "U0"))
        GT = sb("GT", [P, PAIRS, P])
        y0 = sb("y0", [P, H, HD])
        Pbd, Qbd = (sb(n, [P, PAIRS, NSEG, P]) for n in ("Pbd", "Qbd"))
        S = sb("S", [P, NSEG + 1, PAIRS, P])
        prev = mats[:, :, :, :].rearrange("p a b c -> p (a b c)")[:, 0:RW]
        solve = [[mats[:, i, :, :] for i in range(8)], [S[:, i, :, :] for i in range(8)]]
        spread = lambda i: mats[:, i:i + 2, :, :].rearrange("p a b c -> p (a b) c")
        bexp, kexp = [spread(0), spread(4)], [spread(2), spread(6)]
        qexp = [spread(2 * q) for q in range(PAIRS)]
        bank = st.banks("bank", 8)

        rows_in, prev_in, s_in = sem("rows_loaded"), sem("previous_rows"), sem("sample_states_loaded")
        prev_zero, last_in = sem("previous_zeroed"), sem("last_rows_stored")
        mixed, lora_t, lora_in, lora_out = sem("tokens_shifted"), sem("lora_transposed"), sem("lora_inputs"), sem("lora_products")
        gates_z, gates = sem("gate_sums"), sem("gates_ready")
        sq_sum, root = sem("square_sums"), sem("key_norms")
        logd_ok, sums, exps = sem("log_decay"), sem("decay_sums"), sem("decay_exps")
        scaled, turned, turned_kept = sem("scaled"), sem("operands_turned"), sem("turned_kept")
        both = lambda name: [sem(name + "_even"), sem(name + "_odd")]
        gram, gram_kept, step_pe, step_kept = both("gram_products"), both("gram_kept"), both("solve_products"), both("solve_kept")
        pow_kept, yg, yg_kept = both("powers_kept"), both("chunk_outputs"), both("chunk_outputs_kept")
        zeroed, expd, pq, p_kept, q_kept = sem("off_diagonals_zeroed"), sem("keys_spread"), sem("transitions"), sem("transitions_kept"), sem("inputs_kept")
        sc, sc_kept = sem("scan_product"), sem("scan_state")
        gexp, y1, var_ok, dev_ok, out_ok = sem("queries_spread"), sem("state_outputs"), sem("variances"), sem("deviations"), sem("tile_done")
        chain, pchain, out_s, s_used = sem("vector_chain"), sem("pool_chain"), sem("states_stored"), sem("state_seeded")

        with nc.Block() as block:
            @block.sync
            def _(sp):
                for n, src in (("mu", A["mu_e"]), ("w0", A["w0_e"]), ("a0", A["a0_e"]), ("kk", A["kk_e"]),
                               ("ka", A["ka_e"]), ("rk", A["rk_e"]), ("lnw", A["lnx_w_e"]), ("lnb", A["lnx_b_e"])):
                    sp.dma_start(row[n][:, :], src.partition_broadcast(P)).then_inc(rows_in, 16)
                sp.dma_start(wa2[0:64, :], A["w2_e"]).then_inc(rows_in, 16)
                sp.dma_start(wa2[64:128, :], A["a2_e"]).then_inc(rows_in, 16)
                sp.dma_start(g2[:, :], A["g2_e"]).then_inc(rows_in, 16)
                sp.dma_start(A["last_rows"], proj[P - 1:P, 0:SAMP, 0:RW]).then_inc(last_in, 16)
                sp.wait_ge(last_in, 16)
                sp.wait_ge(prev_zero, 1)
                for t in range(TILES):
                    if t:
                        sp.wait_ge(y1, t)
                    sp.dma_start(prev[1:P, :], proj[0:P - 1, t, 0:RW]).then_inc(prev_in, 16)
                    if t:
                        sp.dma_start(prev[0:1, :], A["last_rows"][:, t - 1, :]).then_inc(prev_in, 16)
                sp.wait_ge(sc_kept, NSEG * SAMP)
                sp.dma_start(O["wkv_p"].rearrange("q p i -> p q i"), S[:, NSEG, :, :]).then_inc(out_s, 16)
                sp.wait_ge(out_s, 16)
                for g in range(2):
                    sp.wait_ge(yg_kept[g], 2 * TILES)
                sp.dma_start(S[:, 0:NSEG, :, :], A["wkv_s"].rearrange("b q p i -> p b q i")).then_inc(s_in, 16)
                sp.wait_ge(out_ok, TILES)
                sp.dma_start(O["wkv_s"].rearrange("q b p i -> p q b i"), Pbd[:, :, :, :]).then_inc(out_s, 16)
                sp.wait_ge(out_s, 32)

            @block.tensor
            def _(pe):
                mmul = nc.tensor.matmul
                pe.wait_ge(rows_in, 16 * 11)
                for t in range(TILES):
                    v = proj[:, t, 2 * AW:3 * AW]
                    pe.wait_ge(mixed, t + 1)
                    nc.tensor.transpose(bank[:, 0, 0:P], proj[:, t, 3 * AW:3 * AW + P], C["ident"])
                    nc.tensor.transpose(bank[:, 0, P:2 * P], proj[:, t, 3 * AW + P:RW], C["ident"]).then_inc(lora_t, 1)
                    pe.wait_ge(lora_in, 3 * (t + 1))
                    mmul(bank[:, 1, :], lwaT[0:64, :], wa2[0:64, :], start=True, stop=True)
                    mmul(bank[:, 2, :], lwaT[64:P, :], wa2[64:P, :], start=True, stop=True)
                    mmul(bank[:, 3, :], lgT[:, :], g2[:, :], start=True, stop=True).then_inc(lora_out, 1)
                    pe.wait_ge(logd_ok, t + 1)
                    mmul(bank[:, 4, :], C["upto16"], logd[:, :], start=True, stop=True)
                    mmul(bank[:, 5, :], C["before16"], logd[:, :], start=True, stop=True)
                    mmul(bank[:, 6, :], C["after16"], logd[:, :], start=True, stop=True)
                    for q in range(PAIRS):
                        mm = mmul(bank[:, 7, q * NSEG:(q + 1) * NSEG], logd[:, q * P:(q + 1) * P], C["seg_of_row"],
                                  start=True, stop=True)
                    mm.then_inc(sums, 1)
                    pe.wait_ge(scaled, t + 1)
                    pe.wait_ge(gates, 3 * (t + 1))
                    for i, x in enumerate((at, bt, kt, rt)):
                        for q in range(PAIRS):
                            mm = nc.tensor.transpose(bank[:, i, q * P:(q + 1) * P], x[:, q * P:(q + 1) * P], C["ident"])
                    mm.then_inc(turned, 1)
                    pe.wait_ge(turned_kept, 4 * (t + 1))
                    hd = lambda x, q, g: x[:, (2 * q + g) * HD:(2 * q + g + 1) * HD]

                    def grams(g, which):
                        half = slice(g * HD, (g + 1) * HD)
                        for i in which:
                            x, y = ((atT, btT), (btT, atT), (ktT, atT), (btT, rtT), (ktT, rtT))[i]
                            for q in range(PAIRS):
                                mm = mmul(bank[:, 3 * g + i if i < 3 else 3 + i, q * P:(q + 1) * P], x[half, q, :], y[half, q, :], start=True, stop=True)
                            mm.then_inc(gram[g], 1)

                    def step(s, g):
                        M, MT, M2, M2T, KAT, RBT, RKT, R = solve[g]
                        pe.wait_ge(step_kept[g], 6 * t + 1 + s)
                        if s:
                            pe.wait_ge(pow_kept[g], 5 * t + 2 * s)
                        xT, x = ((MT, M), (M2T, M2), (MT, M))[s]
                        for q in range(PAIRS if s < 2 else 0):
                            mmul(bank[:, 3 * g, q * P:(q + 1) * P], xT[:, q, :], x[:, q, :], start=True, stop=True)
                        for q in range(PAIRS):
                            mmul(bank[:, 3 * g + 1, q * P:(q + 1) * P], x[:, q, :], xT[:, q, :], start=True, stop=True)
                        for q in range(PAIRS):
                            mm = mmul(bank[:, 3 * g + 2, q * P:(q + 1) * P], xT[:, q, :], R[:, q, :], start=True, stop=True)
                        mm.then_inc(step_pe[g], 1)

                    grams(0, (0, 1, 2))
                    grams(1, (0, 1, 2))
                    grams(0, (3, 4))
                    for g in range(2):
                        KAT = solve[g][4]
                        pe.wait_ge(gram_kept[g], 6 * t + 4)
                        for q in range(PAIRS):
                            mm = mmul(bank[:, 3 * g + 2, q * HD:(q + 1) * HD], KAT[:, q, :], hd(v, q, g), start=True, stop=True)
                        mm.then_inc(step_pe[g], 1)
                    for s in range(3):
                        for g in range(2):
                            step(s, g)
                        if s == 0:
                            pe.wait_ge(gram_kept[0], 6 * t + 6)
                            grams(1, (3, 4))
                    for g in range(2):
                        M2T, R = solve[g][3], solve[g][7]
                        pe.wait_ge(step_kept[g], 6 * t + 4)
                        pe.wait_ge(pow_kept[g], 5 * t + 5)
                        for q in range(PAIRS):
                            mm = mmul(bank[:, 3 * g, q * P:(q + 1) * P], M2T[:, q, :], R[:, q, :], start=True, stop=True)
                        mm.then_inc(step_pe[g], 1)
                    for g in range(2):
                        RBT, RKT = solve[g][5:7]
                        half = slice(g * HD, (g + 1) * HD)
                        pe.wait_ge(step_kept[g], 6 * t + 6)
                        pe.wait_ge(gram_kept[g], 6 * t + 6)
                        for q in range(PAIRS):
                            mmul(bank[half, 3 * g + 1, q * P:(q + 1) * P], Wp[:, q, g, :], RBT[:, q, :], start=True, stop=True)
                        for q in range(PAIRS):
                            mmul(bank[:, 3 * g + 2, q * HD:(q + 1) * HD], RBT[:, q, :], U0[:, q, g, :], start=True, stop=False)
                            mm = mmul(bank[:, 3 * g + 2, q * HD:(q + 1) * HD], RKT[:, q, :], hd(v, q, g), start=False, stop=True)
                        mm.then_inc(yg[g], 1)
                    for g in range(2):
                        pe.wait_ge(yg_kept[g], 2 * (t + 1))
                    for q in range(PAIRS):
                        n = PAIRS * t + q
                        pe.wait_ge(expd, 2 * (n + 1))
                        if q >= 2:
                            pe.wait_ge(p_kept, 2 * (n - 1))
                            pe.wait_ge(q_kept, 2 * (n - 1))
                        wq = Wp[:, q, :, :].rearrange("p a b -> p (a b)")
                        uq = U0[:, q, :, :].rearrange("p a b -> p (a b)")
                        be, ke, at0 = bexp[q % 2], kexp[q % 2], 4 * (q % 2)
                        for i in range(2):
                            mm = mmul(bank[:, at0 + i, :], wq, be[:, 4 * i:4 * i + 4, :].rearrange("p a b -> p (a b)"), start=True, stop=True)
                        for c in range(NSEG):
                            o = bank[:, at0 + 2 + c // 4, (c % 4) * P:(c % 4 + 1) * P]
                            mmul(o, be[:, c, :], uq, start=True, stop=False)
                            mm = mmul(o, ke[:, c, :], v[:, q * P:(q + 1) * P], start=False, stop=True)
                        mm.then_inc(pq, 1)
                    pe.wait_ge(p_kept, 2 * PAIRS * (t + 1))
                    pe.wait_ge(q_kept, 2 * PAIRS * (t + 1))

                    def outputs(c):
                        if c == 0:
                            pe.wait_ge(gexp, PAIRS * (t + 1))
                        for q in range(PAIRS):
                            mm = mmul(bank[:, q, 0:P], qexp[q][:, c, :], S[:, c, q, :], start=c == 0, stop=c == NSEG - 1)
                        return mm

                    for c in range(NSEG):
                        n = NSEG * t + c
                        if n:
                            pe.wait_ge(sc_kept, n)
                        if c == 0 and t < SAMP:
                            pe.wait_ge(s_used, t + 1)
                        elif c == 0:
                            pe.wait_ge(s_in, 16)
                        for q in range(PAIRS):
                            mm = mmul(bank[:, 4 + c % 2, q * P:(q + 1) * P], Pbd[:, q, c, :], S[:, c, q, :], start=True, stop=True)
                        mm.then_inc(sc, 1)
                        if c >= 2:
                            outputs(c - 2)
                    outputs(NSEG - 2)
                    outputs(NSEG - 1).then_inc(y1, 1)

            @block.scalar
            def _(act):
                a_ = nc.scalar.activation
                for t in range(TILES):
                    act.wait_ge(lora_t, t + 1)
                    a_(lwaT[0:64, :], bank[0:64, 0, 0:P], ACT.Tanh).then_inc(lora_in, 1)
                    nc.scalar.copy(lwaT[64:P, :], bank[64:P, 0, 0:P]).then_inc(lora_in, 1)
                    a_(lgT[:, :], bank[:, 0, P:2 * P], ACT.Sigmoid).then_inc(lora_in, 1)
                    act.wait_ge(lora_out, t + 1)
                    if t:
                        act.wait_ge(out_ok, t)
                    nc.scalar.copy(g_s[:, :], bank[:, 3, :]).then_inc(gates, 1)
                    act.wait_ge(gates_z, 2 * (t + 1))
                    a_(z_s[:, :], z_s[:, :], ACT.Sigmoid).then_inc(gates, 1)
                    a_(a_s[:, :], a_s[:, :], ACT.Sigmoid).then_inc(gates, 1)
                    act.wait_ge(sq_sum, t + 1)
                    a_(nrm[:, 1, :], nrm[:, 0, :], ACT.Sqrt).then_inc(root, 1)
                    act.wait_ge(sums, t + 1)
                    a_(e_in[:, :], bank[:, 4, :], ACT.Exp).then_inc(exps, 1)
                    a_(e_neg[:, :], bank[:, 4, :], ACT.Exp, scale=-1.0).then_inc(exps, 1)
                    a_(e_ex[:, :], bank[:, 5, :], ACT.Exp).then_inc(exps, 1)
                    a_(e_rev[:, :], bank[:, 6, :], ACT.Exp).then_inc(exps, 1)
                    a_(e_chunk[:, :], bank[:, 7, 0:PAIRS * NSEG], ACT.Exp).then_inc(exps, 1)
                    act.wait_ge(turned, t + 1)
                    for i, x in enumerate((atT, btT, ktT, rtT)):
                        nc.scalar.copy(x[:, :, :].rearrange("p a b -> p (a b)"), bank[:, i, :]).then_inc(turned_kept, 1)
                    for s in range(3):
                        for g in range(2):
                            M, MT, M2, M2T = solve[g][0:4]
                            act.wait_ge(step_pe[g], 5 * t + 2 + s)
                            for i, x in enumerate(((M2, M2T), (M, MT), (None, M2T))[s]):
                                if x is not None:
                                    nc.scalar.copy(x[:, :, :].rearrange("p a b -> p (a b)"), bank[:, 3 * g + i, :]).then_inc(pow_kept[g], 1)
                    if t == 0:
                        act.wait_ge(zeroed, 2)
                    for q in range(PAIRS):
                        act.wait_ge(pq, PAIRS * t + q + 1)
                        for g in range(2):
                            half = slice(g * HD, (g + 1) * HD)
                            b3 = bank[half, 4 * (q % 2) + 2:4 * (q % 2) + 4, :].rearrange("p a (c x) -> p (a c) x", x=P)
                            nc.scalar.copy(Qbd[half, q, :, half], b3[:, :, half]).then_inc(q_kept, 1)
                    act.wait_ge(var_ok, t + 1)
                    a_(nrm[:, 1, :], nrm[:, 0, :], ACT.Sqrt).then_inc(dev_ok, 1)

            @block.gpsimd
            def _(pool):
                nc.gpsimd.memset(prev[0:1, :], 0.0).then_inc(prev_zero, 1)
                for x in (Pbd, Qbd):
                    nc.gpsimd.memset(x[:, :, :, :], 0.0).then_inc(zeroed, 1)

            @block.vector
            def _(dve):
                V = nc.vector
                ch = Chain(dve, chain)
                tt, stt, tsc = V.tensor_tensor, V.scalar_tensor_tensor, V.tensor_scalar
                flat = lambda x: x[:, :, :].rearrange("p a b -> p (a b)")
                h3 = lambda x: x.rearrange("p (h d) -> p h d", h=H)
                dve.wait_ge(rows_in, 16 * 11)

                def shift_rows(t):
                    rw = proj[:, t, 0:RW]
                    dve.wait_ge(last_in, 16)
                    dve.wait_ge(prev_in, 16 * (2 * t + 1))
                    ch(tt(prev[:, :], prev[:, :], rw, ALU.subtract))
                    ch(tt(prev[:, :], prev[:, :], row["mu"][:, :], ALU.mult))
                    tt(rw, rw, prev[:, :], ALU.add).then_inc(mixed, 1)

                dve.wait_ge(prev_zero, 1)
                shift_rows(0)
                for t in range(TILES):
                    r, k, v = (proj[:, t, i * AW:(i + 1) * AW] for i in range(3))
                    dve.wait_ge(mixed, t + 1)
                    dve.wait_ge(lora_out, t + 1)
                    tt(z_s[:, :], bank[:, 1, :], row["w0"][:, :], ALU.add).then_inc(gates_z, 1)
                    tt(a_s[:, :], bank[:, 2, :], row["a0"][:, :], ALU.add).then_inc(gates_z, 1)
                    ch(tt(kk[:, :], k, row["kk"][:, :], ALU.mult))
                    ch(tt(tmp[:, 0:AW], kk[:, :], kk[:, :], ALU.mult))
                    V.tensor_reduce(nrm[:, 0, :], h3(tmp[:, 0:AW]), AX, ALU.add).then_inc(sq_sum, 1)
                    dve.wait_ge(gates, 3 * (t + 1))
                    real = "negc" if t < SAMP else "negc_real"
                    tsc(logd[:, :], z_s[:, :], C[real], None, ALU.mult).then_inc(logd_ok, 1)
                    dve.wait_ge(root, t + 1)
                    ch(tsc(nrm[:, 2, :], nrm[:, 1, :], 1e-12, None, ALU.max))
                    ch(V.reciprocal(nrm[:, 1, :], nrm[:, 2, :]))
                    if t == SAMP:
                        ch(tsc(nrm[:, 1, :], nrm[:, 1, :], C["real"], None, ALU.mult))
                    ch(tt(h3(kk[:, :]), h3(kk[:, :]), last(nrm[:, 1, :], HD), ALU.mult))
                    ch(stt(tmp[:, 0:AW], a_s[:, :], -1.0, row["ka"][:, :], ALU.add, ALU.mult))
                    ch(stt(kp[:, :], tmp[:, 0:AW], 1.0, k, ALU.add, ALU.mult))
                    if t == SAMP:
                        ch(tsc(kp[:, :], kp[:, :], C["real"], None, ALU.mult))
                    ch(tt(a_s[:, :], a_s[:, :], kk[:, :], ALU.mult))
                    ch(tt(tmp[:, 0:AW], r, kp[:, :], ALU.mult))
                    ch(tt(tmp[:, 0:AW], tmp[:, 0:AW], row["rk"][:, :], ALU.mult))
                    ch(V.tensor_reduce(nrm[:, 3, :], h3(tmp[:, 0:AW]), AX, ALU.add))
                    dve.wait_ge(exps, 5 * (t + 1))
                    stt(at[:, :], e_ex[:, :], -1.0, kk[:, :], ALU.mult, ALU.mult)
                    tt(kt[:, :], e_neg[:, :], kp[:, :], ALU.mult)
                    tt(bt[:, :], e_neg[:, :], a_s[:, :], ALU.mult)
                    ch(tt(rt[:, :], e_in[:, :], r, ALU.mult))
                    tt(kend[:, :], e_rev[:, :], kp[:, :], ALU.mult).then_inc(scaled, 1)
                    dve.wait_ge(scaled, t + 1)
                    ch(tt(bend[:, :], e_rev[:, :], a_s[:, :], ALU.mult))

                    def masked(g, which):
                        M, MT, M2, M2T, KAT, RBT, RKT, R = solve[g]
                        for i in which:
                            x, m = ((M, "after16"), (MT, "before16"), (KAT, "before16"), (RBT, "upto16"), (RKT, "upto16"))[i]
                            dve.wait_ge(gram[g], 5 * t + i + 1)
                            tt(x[:, :, :], bank[:, 3 * g + i if i < 3 else 3 + i, :].rearrange("p (a b) -> p a b", b=P), mid(C[m], PAIRS), ALU.mult).then_inc(gram_kept[g], 1)

                    for g in range(2):
                        R = solve[g][7]
                        masked(g, (0, 1, 2))
                        V.tensor_copy(R[:, :, 0:HD], at[:, :].rearrange("p (q g d) -> p q g d", g=2, d=HD)[:, :, g, :]).then_inc(gram_kept[g], 1)
                    for g in range(2):
                        R = solve[g][7]
                        dve.wait_ge(step_pe[g], 5 * t + 1)
                        V.tensor_copy(R[:, :, HD:P], bank[:, 3 * g + 2, 0:PAIRS * HD].rearrange("p (q d) -> p q d", d=HD)).then_inc(step_kept[g], 1)
                    masked(0, (3, 4))
                    for s in range(3):
                        for g in range(2):
                            R = solve[g][7]
                            dve.wait_ge(step_pe[g], 5 * t + 2 + s)
                            dve.wait_ge(step_kept[g], 6 * t + 1 + s)
                            tt(flat(R), flat(R), bank[:, 3 * g + 2, :], ALU.add).then_inc(step_kept[g], 1)
                        if s == 0:
                            masked(1, (3, 4))
                    for g in range(2):
                        R = solve[g][7]
                        dve.wait_ge(step_pe[g], 5 * t + 5)
                        dve.wait_ge(step_kept[g], 6 * t + 4)
                        b3 = bank[:, 3 * g, :].rearrange("p (q x) -> p q x", x=P)
                        tt(Wp[:, :, g, :], R[:, :, 0:HD], b3[:, :, 0:HD], ALU.add).then_inc(step_kept[g], 1)
                        tt(U0[:, :, g, :], R[:, :, HD:P], b3[:, :, HD:P], ALU.add).then_inc(step_kept[g], 1)
                    for g in range(2):
                        half = slice(g * HD, (g + 1) * HD)
                        dve.wait_ge(yg[g], t + 1)
                        tt(GT[half, :, :], bank[half, 3 * g + 1, :].rearrange("p (q x) -> p q x", x=P), rtT[half, :, :], ALU.add).then_inc(yg_kept[g], 1)
                        V.tensor_copy(y0[:, :, :].rearrange("p (q g) d -> p q g d", g=2)[:, :, g, :],
                                      bank[:, 3 * g + 2, 0:PAIRS * HD].rearrange("p (q d) -> p q d", d=HD)).then_inc(yg_kept[g], 1)

                    def spread_keys(q):
                        for x, y in ((bexp, bend), (kexp, kend)):
                            tt(x[q % 2], mid(y[:, q * P:(q + 1) * P], NSEG), last(C["seg_of_row"], P), ALU.mult).then_inc(expd, 1)

                    def spread_queries(q):
                        tt(qexp[q], mid(GT[:, q, :], NSEG), C["seg_of_col"].rearrange("p (c x) -> p c x", x=P), ALU.mult).then_inc(gexp, 1)

                    spread_keys(0)
                    spread_keys(1)
                    if t == 0:
                        dve.wait_ge(zeroed, 2)
                    for g in range(2):
                        dve.wait_ge(yg_kept[g], 2 * (t + 1))
                    for q in range(PAIRS):
                        if q >= 2:
                            dve.wait_ge(p_kept, 2 * (PAIRS * t + q - 1))
                        d3 = tmp[:, q % 2 * AW:(q % 2 + 1) * AW].rearrange("p (c x) -> p c x", x=HD)
                        ch(tt(d3, mid(C["fold"], NSEG), last(e_chunk[:, q * NSEG:(q + 1) * NSEG], HD), ALU.mult))
                        dve.wait_ge(pq, PAIRS * t + q + 1)
                        for g in range(2):
                            half = slice(g * HD, (g + 1) * HD)
                            b3 = bank[half, 4 * (q % 2):4 * (q % 2) + 2, :].rearrange("p a (c x) -> p (a c) x", x=P)
                            tt(Pbd[half, q, :, half], b3[:, :, half], d3[half, :, :], ALU.add).then_inc(p_kept, 1)
                        if q < 2:
                            spread_keys(q + 2)
                        elif q == 2:
                            spread_queries(0)
                            spread_queries(1)
                    dve.wait_ge(q_kept, 2 * PAIRS * (t + 1))
                    dve.wait_ge(p_kept, 2 * PAIRS * (t + 1))
                    sflat = lambda c: S[:, c, :, :]
                    if t == 0:
                        V.memset(sflat(0), 0.0).then_inc(s_used, 1)
                    elif t < SAMP:
                        V.tensor_copy(sflat(0), sflat(NSEG)).then_inc(s_used, 1)
                    if t < SAMP:
                        dve.wait_ge(s_used, t + 1)
                    for c in range(NSEG):
                        n = NSEG * t + c
                        dve.wait_ge(sc, n + 1)
                        b = bank[:, 4 + c % 2, :].rearrange("p (q x) -> p q x", x=P)
                        o = S[:, c + 1, :, :] if t < SAMP else Pbd[:, :, c, :]
                        tt(o, b, Qbd[:, :, c, :], ALU.add).then_inc(sc_kept, 1)
                        if c < 2:
                            spread_queries(c + 2)
                    dve.wait_ge(y1, t + 1)
                    y = tmp[:, 0:AW]
                    y2 = tmp[:, AW:2 * AW]
                    q3 = lambda x: x.rearrange("p (q x) -> p q x", x=P)
                    ch(tt(q3(y), bank[:, 0:PAIRS, 0:P], q3(y0[:, :, :].rearrange("p h d -> p (h d)")), ALU.add))
                    ch(V.tensor_reduce(nrm[:, 0, :], h3(y), AX, ALU.add))
                    ch(tsc(nrm[:, 0, :], nrm[:, 0, :], 1.0 / HD, None, ALU.mult))
                    ch(tt(h3(y), h3(y), last(nrm[:, 0, :], HD), ALU.subtract))
                    ch(tt(y2, y, y, ALU.mult))
                    ch(V.tensor_reduce(nrm[:, 2, :], h3(y2), AX, ALU.add))
                    tsc(nrm[:, 0, :], nrm[:, 2, :], 1.0 / HD, 64e-5, ALU.mult, ALU.add).then_inc(var_ok, 1)
                    if t < SAMP:
                        shift_rows(t + 1)
                    dve.wait_ge(dev_ok, t + 1)
                    ch(V.reciprocal(nrm[:, 2, :], nrm[:, 1, :]))
                    ch(tt(h3(y), h3(y), last(nrm[:, 2, :], HD), ALU.mult))
                    ch(tt(y, y, row["lnw"][:, :], ALU.mult))
                    ch(tt(y, y, row["lnb"][:, :], ALU.add))
                    ch(tt(h3(y2), h3(v), last(nrm[:, 3, :], HD), ALU.mult))
                    ch(tt(y, y, y2, ALU.add))
                    tt(mix[:, t, 0:AW], y, g_s[:, :], ALU.mult).then_inc(out_ok, 1)
                    dve.wait_ge(out_ok, t + 1)


def mla(nc, C, A, proj, mix, O):
    QH = 64 + RP
    ROWS = H * NS
    GB = P // ROWS
    JP = 4
    JB = NPAGE // JP
    STEPS = JB + 1
    UNITS = 2 * JB * GB
    RING, KRING = 6, 5
    KR = KV + RP
    ORDER = [SAMP] + list(range(SAMP))
    with Stage(nc, "mla") as st:
        sb, sem = st.sb, st.sem
        wuq = sb("wuq", [P, 3, H * QH])
        wuk = sb("wuk", [P, 2, H * 64])
        wuv = sb("wuv", [P, 2, H * 64])
        wukT = sb("wukT", [64, H, KV])
        qnorm, kvnorm = sb("qnorm", [P, QL]), sb("kvnorm", [P, KV])
        pages = sb("pages", [1, NB * NPAGE], mybir.dt.int32)
        cn = sb("cn", [P, TILES, KV])
        kr = sb("kr", [P, TILES, RP])
        kpad = sb("kpad", [P, QH])
        cqn, sq = sb("cqn", [P, QL]), sb("sq", [P, QL])
        ms = sb("ms", [P, 6])
        q_s = sb("q", [P, H * QH])
        rt1, rt2 = sb("rt1", [P, H, RP // 2]), sb("rt2", [P, H, RP // 2])
        cqT, cT = sb("cqT", [P, 3, P]), sb("cT", [P, 2, P])
        Vs = sb("Vs", [P, SAMP, H * 64])
        qT = sb("qT", [QH, H, P])
        mx, neg, tot, inv = (sb(n, [P, H]) for n in ("mx", "neg", "tot", "inv"))
        prob, probT = sb("prob", [P, 2, SEQ]), sb("probT", [P, 2, SEQ])
        qlT = sb("qlT", [QH, 3, NB * ROWS])
        knT = sb("knT", [QH, 3, P])
        keys = sb("keys", [QH, KRING, JP, 3, PAGE])
        vals = sb("vals", [P, RING, JP, KV])
        vnew = sb("vnew", [SEG, NB, KV])
        KT = sb("KT", [QH, H, SEQ])
        pp, ppT = sb("pp", [P, JP * PAGE]), sb("ppT", [P, JP, P])
        top, ntop = sb("top", [P, 2]), sb("ntop", [P, 2])
        part, shrink, total = sb("part", [P, 2]), sb("shrink", [P, 2]), sb("total", [P, 2])
        o_s = sb("o", [P, KV])
        oT = sb("oT", [P, 2, H, NB * SEG])
        bank = st.banks("bank", 8)

        here, pad0 = sem("weights_loaded"), sem("pads_zeroed")
        sq_in, rt_in = sem("mean_squares"), sem("roots")
        norm, flipped, flip_kept = sem("rows_normed"), sem("rows_turned"), sem("turned_kept")
        q_ok, q_kept, roped = sem("queries"), sem("queries_kept"), sem("queries_rotated")
        qt, qt_kept = sem("queries_turned"), sem("turned_queries_kept")
        kv, kv_kept = sem("keys_and_values"), sem("keys_and_values_kept")
        sc, sm, ex = sem("scores"), sem("score_maxima"), sem("exps")
        pt, pt_kept, pv, tile_ok = sem("probs_turned"), sem("turned_probs_kept"), sem("head_outputs"), sem("tile_done")
        chain = sem("vector_chain")
        ql, ql_kept = sem("latent_queries"), sem("latent_queries_kept")
        new_out, new_in, stores = sem("new_rows_stored"), sem("new_rows_loaded"), sem("outputs_stored")
        kin = [sem(f"keys_loaded{i}") for i in range(KRING)]
        vin = [sem(f"values_loaded{i}") for i in range(RING)]
        pin = sem("page_table_loaded")
        ps, gv = sem("page_scores"), sem("page_values")
        s_sc, s_mx, s_ex = sem("step_scores"), sem("step_maximum"), sem("step_exps")
        s_pt, s_ptk, s_pv, s_add = sem("step_turned"), sem("step_turned_kept"), sem("step_values"), sem("step_added")
        masked = sem("new_scores_masked")
        go, gl, gl_kept, fin = sem("group_normed"), sem("group_latents_turned"), sem("group_latents_kept"), sem("sample_outputs")

        def steps_after(t, i):
            if i < 1 or i > 8:
                return []
            c = (t * 8 + i - 1) // 2
            u = c // JB * STEPS + c % JB + 1
            if i % 2 == 1:
                return [("s", u)]
            out = [("v", u)]
            if c % JB == JB - 1:
                out += [("end", c // JB)]
                if c == JB - 1:
                    out += [("s", STEPS), ("v", STEPS)]
            return out

        def four_pages(engine, n):
            g, j, b = n // (JB * GB), n // GB % JB, n % GB
            at = (GB * g + b) * NPAGE + JP * j
            return nc.values_load_multi_w_load_instructions(pages[0:1, at:at + JP], engines=(engine,), min_val=0, max_val=A["keysT"].shape[0] - 1)[1]

        def load_values(eng, engine, n):
            if n >= RING:
                eng.wait_ge(gv, n - RING + 1)
            for i, page in enumerate(four_pages(engine, n)):
                eng.dma_start(vals[:, n % RING, i, :], A["cache_ckv"][bass.ds(page, 1), :, :].rearrange("a p x -> p (a x)")).then_inc(vin[n % RING], 16)

        with nc.Block() as block:
            @block.sync
            def _(sp):
                for dst, src in ((wuq[:, :, :], A["w_uq_e"].rearrange("(k p) n -> p k n", p=P)),
                                 (wuk[:, :, :], A["w_uk_e"].rearrange("(k p) n -> p k n", p=P)),
                                 (wuv[:, :, :], A["w_uv_e"].rearrange("(k p) n -> p k n", p=P)),
                                 (wukT[:, :, :], A["w_ukT_e"]),
                                 (qnorm[:, :], A["q_norm_e"].partition_broadcast(P)),
                                 (kvnorm[:, :], A["kv_norm_e"].partition_broadcast(P))):
                    sp.dma_start(dst, src).then_inc(here, 16)
                sp.dma_start(pages[:, :], A["page_table"]).then_inc(pin, 16)
                sp.wait_ge(pin, 16)
                for n in range(UNITS):
                    if n >= KRING:
                        sp.wait_ge(ps, n - KRING + 1)
                    for i, page in enumerate(four_pages(mybir.EngineType.SP, n)):
                        sp.dma_start(keys[:, n % KRING, i, :, :].rearrange("p a b -> p (a b)"),
                                     A["keysT"][bass.ds(page, 1), :, :].rearrange("a p x -> p (a x)")).then_inc(kin[n % KRING], 16)

            @block.gpsimd
            def _(pool):
                nc.gpsimd.memset(oT[:, :, :, :], 0.0).then_inc(pad0, 1)
                pool.wait_ge(norm, 1)
                pool.dma_start(A["new_rows"], cn[:, SAMP, :]).then_inc(new_out, 16)
                pool.wait_ge(new_out, 16)
                pool.dma_start(vnew[:, :, :], A["new_rows"].rearrange("(b s) c -> s b c", s=SEG)).then_inc(new_in, 16)
                pool.wait_ge(pin, 16)
                for n in range(UNITS):
                    load_values(pool, mybir.EngineType.Pool, n)

            @block.tensor
            def _(pe):
                mmul, turn = nc.tensor.matmul, nc.tensor.transpose
                pe.wait_ge(here, 16 * 6)

                def scores(u):
                    g, j = u // STEPS, u % STEPS - 1
                    for b in range(GB):
                        s = GB * g + b
                        cols = slice(s * ROWS, (s + 1) * ROWS)
                        if j < 0:
                            for k in range(3):
                                mm = mmul(bank[b * ROWS:(b + 1) * ROWS, 6, 0:SEG], qlT[:, k, cols], knT[:, k, s * SEG:(s + 1) * SEG],
                                          start=k == 0, stop=k == 2)
                        else:
                            n = (g * JB + j) * GB + b
                            pe.wait_ge(kin[n % KRING], 16 * JP * (n // KRING + 1))
                            o = bank[b * ROWS:(b + 1) * ROWS, 6, :].rearrange("p (i x) -> p i x", i=JP)
                            for k in range(3):
                                mm = mmul(o, qlT[:, k, cols], keys[:, n % KRING, :, k, :], start=k == 0, stop=k == 2)
                            mm.then_inc(ps, 1)
                    if j < 0:
                        mm.then_inc(s_sc, 1)

                def values(u):
                    g, j = u // STEPS, u % STEPS - 1
                    pe.wait_ge(s_ex, u + 1)
                    w = SEG if j < 0 else PAGE
                    for i in range(1 if j < 0 else JP):
                        mm = turn(bank[0:w, 7, i * P:(i + 1) * P], pp[:, i * w:(i + 1) * w], C["ident"])
                    mm.then_inc(s_pt, 1)
                    pe.wait_ge(s_ptk, u + 1)
                    if u:
                        pe.wait_ge(s_add, u)
                    if u == 0:
                        pe.wait_ge(new_in, 16)
                    for b in range(GB):
                        o = bank[b * ROWS:(b + 1) * ROWS, 0, 0:KV]
                        cols = slice(b * ROWS, (b + 1) * ROWS)
                        if j < 0:
                            mm = mmul(o, ppT[0:SEG, 0, cols], vnew[:, GB * g + b, :], start=True, stop=True)
                            if b == GB - 1:
                                mm.then_inc(s_pv, 1)
                        else:
                            n = (g * JB + j) * GB + b
                            pe.wait_ge(vin[n % RING], 16 * JP * (n // RING + 1))
                            for i in range(JP):
                                mm = mmul(o, ppT[:, i, cols], vals[:, n % RING, i, :], start=i == 0, stop=i == JP - 1)
                            mm.then_inc(gv, 1)

                def group_end(g):
                    pe.wait_ge(go, g + 1)
                    for k in range(2):
                        mm = turn(bank[:, 7, k * P:(k + 1) * P], o_s[:, k * P:(k + 1) * P], C["ident"])
                    mm.then_inc(gl, 1)
                    pe.wait_ge(gl_kept, 2 * (g + 1))

                def take(steps):
                    for what, u in steps:
                        {"s": scores, "v": values, "end": group_end}[what](u)

                for pos, t in enumerate(ORDER):
                    pe.wait_ge(norm, pos + 1)
                    if pos:
                        pe.wait_ge(ql_kept, 7)
                        pe.wait_ge(s_add, 1 + 4 * t + t // 2)
                        if t:
                            pe.wait_ge(tile_ok, t)
                    for i in range(3):
                        turn(bank[:, 0, i * P:(i + 1) * P], cqn[:, i * P:(i + 1) * P], C["ident"])
                    for i in range(2):
                        if t < SAMP:
                            turn(bank[:, 1, i * P:(i + 1) * P], cn[:, t, i * P:(i + 1) * P], C["ident"])
                        else:
                            turn(bank[0:QH, 1, i * P:(i + 1) * P], cn[:, t, i * QH:(i + 1) * QH], C["ident"])
                    turn(bank[0:QH, 3, 0:P], kpad[:, :], C["ident"]).then_inc(flipped, 1)
                    pe.wait_ge(flip_kept, 3 * (pos + 1))
                    for x in range(2):
                        for k in range(3):
                            mm = mmul(bank[:, 2 + x, 0:384], cqT[:, k, :], wuq[:, k, x * 384:(x + 1) * 384], start=k == 0, stop=k == 2)
                    mm.then_inc(q_ok, 1)
                    if t < SAMP:
                        for h in range(H):
                            for k in range(2):
                                mmul(bank[0:64, 6 + h // 4, h % 4 * P:(h % 4 + 1) * P], wuk[:, k, h * 64:(h + 1) * 64], cT[:, k, :],
                                     start=k == 0, stop=k == 1)
                        for k in range(2):
                            mm = mmul(bank[:, 0, :], cT[:, k, :], wuv[:, k, :], start=k == 0, stop=k == 1)
                        mm.then_inc(kv, 1)
                    pe.wait_ge(roped, pos + 1)
                    for h in range(H):
                        mm = turn(bank[0:QH, 4 + h // 4, h % 4 * P:(h % 4 + 1) * P], q_s[:, h * QH:(h + 1) * QH], C["ident"])
                    mm.then_inc(qt, 1)
                    pe.wait_ge(qt_kept, 2 * (pos + 1))
                    if t == SAMP:
                        for k in range(3):
                            m = min(QH, KV - k * QH)
                            for h in range(H):
                                mm = mmul(bank[0:m, 2 + 2 * k + h // 4, h % 4 * P:(h % 4 + 1) * P], wukT[:, h, k * QH:k * QH + m], qT[0:64, h, :],
                                          start=True, stop=True)
                        mm.then_inc(ql, 1)
                        pe.wait_ge(ql_kept, 7)
                        take([("s", 0), ("v", 0)])
                        continue
                    pe.wait_ge(kv_kept, 3 * (t + 1))
                    n_k = (t + 1) * P
                    for i in range(H + 2):
                        if i < H:
                            n = H * t + i
                            if i >= 2:
                                pe.wait_ge(ex, n - 1)
                            mmul(bank[:, 2 + i % 2, 0:n_k], qT[:, i, :], KT[:, i, 0:n_k], start=True, stop=True).then_inc(sc, 1)
                        if 1 <= i <= H:
                            n = H * t + i - 1
                            pe.wait_ge(ex, n + 1)
                            if i >= 3:
                                pe.wait_ge(pt_kept, n - 1)
                            for k in range(t + 1):
                                mm = turn(bank[:, 4 + (i - 1) % 2, k * P:(k + 1) * P], prob[:, (i - 1) % 2, k * P:(k + 1) * P], C["ident"])
                            mm.then_inc(pt, 1)
                        if i >= 2:
                            h, n = i - 2, H * t + i - 2
                            pe.wait_ge(pt_kept, n + 1)
                            for k in range(t + 1):
                                mm = mmul(bank[:, 1, h * 64:(h + 1) * 64], probT[:, h % 2, k * P:(k + 1) * P], Vs[:, k, h * 64:(h + 1) * 64],
                                          start=k == 0, stop=k == t)
                            mm.then_inc(pv, 1)
                        take(steps_after(t, i))
                for h in range(H):
                    for k in range(2):
                        mm = mmul(bank[:, 0, h * 64:(h + 1) * 64], oT[:, k, h, :], wuv[:, k, h * 64:(h + 1) * 64], start=k == 0, stop=k == 1)
                mm.then_inc(fin, 1)

            @block.scalar
            def _(act):
                a_, cp = nc.scalar.activation, nc.scalar.copy

                def exps(u):
                    j = u % STEPS - 1
                    w = SEG if j < 0 else JP * PAGE
                    act.wait_ge(s_mx, u + 1)
                    if u:
                        act.wait_ge(s_pt, u)
                    if j >= 0:
                        a_(shrink[:, u % 2:u % 2 + 1], top[:, 1 - u % 2:2 - u % 2], ACT.Exp, bias=ntop[:, u % 2:u % 2 + 1], scale=SM)
                    a_(pp[:, 0:w], bank[:, 6, 0:w], ACT.Exp, bias=ntop[:, u % 2:u % 2 + 1], scale=SM, accum_out=part[:, u % 2:u % 2 + 1]).then_inc(s_ex, 1)

                def turned(u):
                    act.wait_ge(s_pt, u + 1)
                    if u % STEPS == 0:
                        cp(ppT[0:SEG, 0, :], bank[0:SEG, 7, 0:P]).then_inc(s_ptk, 1)
                    else:
                        cp(ppT[:, :, :].rearrange("p a b -> p (a b)"), bank[:, 7, :]).then_inc(s_ptk, 1)

                def take(steps):
                    for what, u in steps:
                        {"s": exps, "v": turned, "end": lambda g: None}[what](u)

                for pos, t in enumerate(ORDER):
                    act.wait_ge(sq_in, pos + 1)
                    a_(ms[:, 2:4], ms[:, 0:2], ACT.Sqrt).then_inc(rt_in, 1)
                    act.wait_ge(flipped, pos + 1)
                    cp(cqT[:, :, :].rearrange("p a b -> p (a b)"), bank[:, 0, 0:3 * P]).then_inc(flip_kept, 1)
                    if t < SAMP:
                        cp(cT[:, :, :].rearrange("p a b -> p (a b)"), bank[:, 1, 0:2 * P]).then_inc(flip_kept, 1)
                        act.wait_ge(kv, t + 1)
                        for i in range(2):
                            cp(KT[0:64, 4 * i:4 * i + 4, t * P:(t + 1) * P], bank[0:64, 6 + i, :].rearrange("p (h x) -> p h x", h=4)).then_inc(kv_kept, 1)
                        cp(Vs[:, t, :], bank[:, 0, :]).then_inc(kv_kept, 1)
                    else:
                        cp(knT[:, 0:2, :].rearrange("p a b -> p (a b)"), bank[0:QH, 1, 0:2 * P]).then_inc(flip_kept, 1)
                    act.wait_ge(qt, pos + 1)
                    for i in range(2):
                        cp(qT[:, 4 * i:4 * i + 4, :].rearrange("p a b -> p (a b)"), bank[0:QH, 4 + i, :]).then_inc(qt_kept, 1)
                    if t == SAMP:
                        act.wait_ge(ql, 1)
                        for k in range(3):
                            m = min(QH, KV - k * QH)
                            for i in range(2):
                                src = bank[0:m, 2 + 2 * k + i, :].rearrange("p (h b s) -> p h b s", h=4, s=SEG)[:, :, :, 1:1 + NS]
                                dst = qlT[0:m, k, :].rearrange("p (b h q) -> p h b q", h=H, q=NS)[:, 4 * i:4 * i + 4, :, :]
                                cp(dst, src).then_inc(ql_kept, 1)
                        act.wait_ge(qt_kept, 2)
                        cp(qlT[64:QH, 2, :].rearrange("p (b h q) -> p h b q", h=H, q=NS),
                           qT[64:QH, :, :].rearrange("p h (b s) -> p h b s", s=SEG)[:, :, :, 1:1 + NS]).then_inc(ql_kept, 1)
                        take([("s", 0), ("v", 0)])
                        continue
                    n_k = (t + 1) * P
                    for i in range(H + 2):
                        if i < H:
                            n = H * t + i
                            act.wait_ge(sm, n + 1)
                            if i >= 2:
                                act.wait_ge(pt, n - 1)
                            a_(prob[:, i % 2, 0:n_k], bank[:, 2 + i % 2, 0:n_k], ACT.Exp, bias=neg[:, i:i + 1], scale=SM,
                               accum_out=tot[:, i:i + 1]).then_inc(ex, 1)
                        if 1 <= i <= H:
                            n = H * t + i - 1
                            act.wait_ge(pt, n + 1)
                            if i >= 3:
                                act.wait_ge(pv, n - 1)
                            cp(probT[:, (i - 1) % 2, 0:n_k], bank[:, 4 + (i - 1) % 2, 0:n_k]).then_inc(pt_kept, 1)
                        take(steps_after(t, i))
                act.wait_ge(norm, TILES)
                act.dma_start(O["ckv"].rearrange("(t p) c -> p t c", p=P), cn[:, :, :]).then_inc(stores, 16)
                act.dma_start(O["kpe"].rearrange("(t p) c -> p t c", p=P), kr[:, :, :]).then_inc(stores, 16)
                act.wait_ge(stores, 32)

            @block.vector
            def _(dve):
                V = nc.vector
                ch = Chain(dve, chain)
                tt, tsc, st2 = V.tensor_tensor, V.tensor_scalar, V.scalar_tensor_tensor
                dve.wait_ge(here, 16 * 6)
                dve.wait_ge(pad0, 1)

                def maximum(u):
                    g, j = u // STEPS, u % STEPS - 1
                    now, before = slice(u % 2, u % 2 + 1), slice(1 - u % 2, 2 - u % 2)
                    if j < 0:
                        dve.wait_ge(s_sc, g + 1)
                        tt(bank[:, 6, 0:SEG], bank[:, 6, 0:SEG], C["newmask"], ALU.add).then_inc(masked, 1)
                        dve.wait_ge(masked, g + 1)
                        ch(V.tensor_reduce(top[:, now], bank[:, 6, 0:SEG], AX, ALU.max))
                    else:
                        dve.wait_ge(ps, (g * JB + j + 1) * GB)
                        ch(V.tensor_reduce(top[:, now], bank[:, 6, :], AX, ALU.max))
                        ch(tt(top[:, now], top[:, now], top[:, before], ALU.max))
                    tsc(ntop[:, now], top[:, now], -SM, None, ALU.mult).then_inc(s_mx, 1)

                def add(u):
                    g, j = u // STEPS, u % STEPS - 1
                    now, before = slice(u % 2, u % 2 + 1), slice(1 - u % 2, 2 - u % 2)
                    dve.wait_ge(s_ex, u + 1)
                    if j < 0:
                        ch(V.tensor_copy(total[:, now], part[:, now]))
                        dve.wait_ge(s_pv, g + 1)
                        V.tensor_copy(o_s[:, :], bank[:, 0, 0:KV]).then_inc(s_add, 1)
                    else:
                        st2(out=total[:, now], in0=total[:, before], scalar=shrink[:, now], in1=part[:, now], op0=ALU.mult, op1=ALU.add)
                        dve.wait_ge(gv, (g * JB + j + 1) * GB)
                        dve.wait_ge(s_add, u)
                        st2(out=o_s[:, :], in0=o_s[:, :], scalar=shrink[:, now], in1=bank[:, 0, 0:KV], op0=ALU.mult, op1=ALU.add).then_inc(s_add, 1)

                def group_end(g):
                    u = (g + 1) * STEPS - 1
                    now = slice(u % 2, u % 2 + 1)
                    dve.wait_ge(s_add, u + 1)
                    ch(V.reciprocal(total[:, now], total[:, now]))
                    tsc(o_s[:, :], o_s[:, :], total[:, now], None, ALU.mult).then_inc(go, 1)
                    dve.wait_ge(gl, g + 1)
                    for k in range(2):
                        for b in range(GB):
                            s = GB * g + b
                            ins = V.tensor_copy(oT[:, k, :, s * SEG + 1:s * SEG + 1 + NS],
                                                bank[:, 7, k * P + b * ROWS:k * P + (b + 1) * ROWS].rearrange("p (h q) -> p h q", h=H))
                        ins.then_inc(gl_kept, 1)

                def take(steps):
                    for what, u in steps:
                        {"s": maximum, "v": add, "end": group_end}[what](u)

                for pos, t in enumerate(ORDER):
                    cq = proj[:, t, 0:QL]
                    ckv = proj[:, t, QL:QL + KV]
                    kpe = proj[:, t, QL + KV:QL + KV + RP]
                    ch(tt(sq[:, :], cq, cq, ALU.mult))
                    ch(V.tensor_reduce(ms[:, 4:5], sq[:, :], AX, ALU.add))
                    ch(tt(sq[:, 0:KV], ckv, ckv, ALU.mult))
                    ch(V.tensor_reduce(ms[:, 5:6], sq[:, 0:KV], AX, ALU.add))
                    ch(tsc(ms[:, 0:1], ms[:, 4:5], 1.0 / QL, 1e-6, ALU.mult, ALU.add))
                    tsc(ms[:, 1:2], ms[:, 5:6], 1.0 / KV, 1e-6, ALU.mult, ALU.add).then_inc(sq_in, 1)
                    dve.wait_ge(rt_in, pos + 1)
                    ch(V.reciprocal(ms[:, 4:6], ms[:, 2:4]))
                    ch(tsc(cqn[:, :], cq, ms[:, 4:5], None, ALU.mult))
                    tt(cqn[:, :], cqn[:, :], qnorm[:, :], ALU.mult)
                    ch(tsc(cn[:, t, :], ckv, ms[:, 5:6], None, ALU.mult))
                    ch(tt(cn[:, t, :], cn[:, t, :], kvnorm[:, :], ALU.mult))
                    cos, sin = (C[n][:, t * 16:(t + 1) * 16] for n in ("cos", "sin"))

                    def rotate(x1, x2, cs, sn, y1, y2, a, b):
                        tt(a, x1, cs, ALU.mult)
                        ch(tt(b, x2, sn, ALU.mult))
                        ch(tt(b, a, b, ALU.subtract))
                        ch(tt(a, x1, sn, ALU.mult))
                        ch(V.tensor_copy(y1, b))
                        ch(tt(b, x2, cs, ALU.mult))
                        ch(tt(y2, a, b, ALU.add))

                    rotate(kpe[:, 0:16], kpe[:, 16:32], cos, sin, kr[:, t, 0:16], kr[:, t, 16:32], rt1[:, 0, :], rt2[:, 0, :])
                    if t == SAMP:
                        V.tensor_copy(kpad[:, 0:64], cn[:, t, 2 * QH:KV])
                    V.tensor_copy(kpad[:, 64:QH], kr[:, t, :]).then_inc(norm, 1)
                    dve.wait_ge(flipped, pos + 1)
                    if t < SAMP:
                        V.tensor_copy(KT[64:QH, :, t * P:(t + 1) * P], mid(bank[64:QH, 3, 0:P], H)).then_inc(flip_kept, 1)
                    else:
                        V.tensor_copy(knT[:, 2, :], bank[0:QH, 3, 0:P]).then_inc(flip_kept, 1)
                    dve.wait_ge(q_ok, pos + 1)
                    ch(V.tensor_copy(q_s[:, :].rearrange("p (a x) -> p a x", a=2), bank[:, 2:4, 0:384]))
                    q3 = q_s[:, :].rearrange("p (h x) -> p h x", h=H)
                    x1, x2 = q3[:, :, 64:80], q3[:, :, 80:96]
                    rotate(x1, x2, mid(cos, H), mid(sin, H), x1, x2, rt1[:, :, :], rt2[:, :, :])
                    V.tensor_copy(rt1[:, 0, 0:1], rt2[:, 0, 0:1]).then_inc(roped, 1)
                    if t == SAMP:
                        take([("s", 0), ("v", 0)])
                        continue
                    for h in range(H + 2):
                        if h < H:
                            n = H * t + h
                            dve.wait_ge(sc, n + 1)
                            b = bank[:, 2 + h % 2, :]
                            ch(tt(b[:, t * P:(t + 1) * P], b[:, t * P:(t + 1) * P], C["causal"], ALU.add))
                            ch(V.tensor_reduce(mx[:, h:h + 1], b[:, 0:(t + 1) * P], AX, ALU.max))
                            tsc(neg[:, h:h + 1], mx[:, h:h + 1], -SM, None, ALU.mult).then_inc(sm, 1)
                        take(steps_after(t, h))
                    dve.wait_ge(ex, H * (t + 1))
                    ch(V.reciprocal(inv[:, :], tot[:, :]))
                    dve.wait_ge(pv, H * (t + 1))
                    tt(mix[:, t, :].rearrange("p (h d) -> p h d", h=H), bank[:, 1, :].rearrange("p (h d) -> p h d", h=H),
                       last(inv[:, :], 64), ALU.mult).then_inc(tile_ok, 1)
                dve.wait_ge(fin, 1)
                ch(V.tensor_copy(mix[:, SAMP, :], bank[:, 0, :]))


GT = SAMP - 1
DENSE = TOK - P
SAMP_AT = GT * P
START = [t * P for t in range(GT)] + [DENSE, SAMP_AT]
T_ROWS = [P] * SAMP + [NB * NS]


def turn(nc, name, C, x, xT, compact):
    with Stage(nc, name) as st:
        bank = st.banks("bank", 4)
        turned, kept = st.sem("rows_turned"), st.sem("columns_kept")
        with nc.Block() as block:
            @block.tensor
            def _(pe):
                for t in range(TILES):
                    for i in range(2):
                        n = 2 * t + i
                        if n >= 4:
                            pe.wait_ge(kept, n - 3)
                        for k in range(4):
                            mm = nc.tensor.transpose(bank[:, n % 4, k * P:(k + 1) * P], x[:, t, (4 * i + k) * P:(4 * i + k + 1) * P], C["ident"])
                        mm.then_inc(turned, 1)

            @block.vector
            def _(dve):
                for t in range(TILES):
                    for i in range(2):
                        n = 2 * t + i
                        dve.wait_ge(turned, n + 1)
                        src = bank[:, n % 4, :].rearrange("p (k x) -> p k x", k=4)
                        dst = xT[:, 4 * i:4 * i + 4, :]
                        if t < SAMP or not compact:
                            at = START[t] if compact else t * P
                            nc.vector.tensor_copy(dst[:, :, at:at + P], src).then_inc(kept, 1)
                        else:
                            nc.vector.tensor_copy(dst[:, :, SAMP_AT:DENSE].rearrange("p k (b s) -> p k b s", s=NS),
                                                  src.rearrange("p k (b s) -> p k b s", s=SEG)[:, :, :, 1:1 + NS]).then_inc(kept, 1)


def layer_norm_vector(nc, dve, ch, x, t, sem_sum, sem_root, sem_norm, stats, mv, gain, shift):
    V = nc.vector
    V.bn_stats(stats[:, 0, :], x[:, t, 0:512])
    ch(V.bn_stats(stats[:, 1, :], x[:, t, 512:D]))
    ch(V.bn_aggr(mv[:, 0:2], stats[:, :, :]))
    V.tensor_scalar(mv[:, 2:3], mv[:, 1:2], 1e-5, None, ALU.add).then_inc(sem_sum, 1)
    dve.wait_ge(sem_root, t + 1)
    ch(V.reciprocal(mv[:, 4:5], mv[:, 3:4]))
    V.scalar_tensor_tensor(out=mv[:, 5:6], in0=mv[:, 0:1], scalar=-1.0, in1=mv[:, 4:5], op0=ALU.mult, op1=ALU.mult).then_inc(sem_sum, 1)
    dve.wait_ge(sem_norm, t + 1)
    ch(V.tensor_tensor(x[:, t, :], x[:, t, :], gain, ALU.mult))
    ch(V.tensor_tensor(x[:, t, :], x[:, t, :], shift, ALU.add))


def layer_norm_scalar(nc, act, x, t, sem_sum, sem_root, sem_norm, mv):
    act.wait_ge(sem_sum, 2 * t + 1)
    nc.scalar.activation(mv[:, 3:4], mv[:, 2:3], ACT.Sqrt).then_inc(sem_root, 1)
    act.wait_ge(sem_sum, 2 * t + 2)
    nc.scalar.activation(x[:, t, :], x[:, t, :], ACT.Identity, bias=mv[:, 5:6], scale=mv[:, 4:5]).then_inc(sem_norm, 1)


def out_project(nc, name, C, mixed, w_dram, gain_dram, shift_dram, x):
    with Stage(nc, name) as st:
        w = st.sb("w", [P, KD, D])
        gain, shift = st.sb("gain", [P, D]), st.sb("shift", [P, D])
        mT = st.sb("mT", [P, 2, KD, P])
        stats, mv = st.sb("stats", [P, 2, 6]), st.sb("mv", [P, 6])
        bank = st.banks("bank", 8)
        here = st.sem("weights_loaded")
        turned, kept, done, added = st.sem("turned"), st.sem("turned_kept"), st.sem("products"), st.sem("residual_added")
        s_sum, s_root, s_norm, chain = st.sem("statistics"), st.sem("deviation"), st.sem("normed"), st.sem("vector_chain")
        with nc.Block() as block:
            @block.sync
            def _(sp):
                sp.dma_start(w[:, :, :], w_dram.rearrange("(k p) n -> p k n", p=P)).then_inc(here, 16)
                sp.dma_start(gain[:, :], gain_dram.partition_broadcast(P)).then_inc(here, 16)
                sp.dma_start(shift[:, :], shift_dram.partition_broadcast(P)).then_inc(here, 16)

            @block.tensor
            def _(pe):
                def turns(t):
                    for i in range(2):
                        n = 2 * t + i
                        if n >= 4:
                            pe.wait_ge(kept, n - 3)
                        for k in range(4):
                            mm = nc.tensor.transpose(bank[:, n % 4, k * P:(k + 1) * P], mixed(t, 4 * i + k), C["ident"])
                        mm.then_inc(turned, 1)

                turns(0)
                pe.wait_ge(here, 48)
                for t in range(TILES):
                    if t + 1 < TILES:
                        turns(t + 1)
                    pe.wait_ge(kept, 2 * (t + 1))
                    if t >= 2:
                        pe.wait_ge(added, t - 1)
                    for i in range(2):
                        for k in range(KD):
                            mm = nc.tensor.matmul(bank[:, 4 + 2 * (t % 2) + i, :], mT[:, t % 2, k, :], w[:, k, i * 512:(i + 1) * 512],
                                                  start=k == 0, stop=k == KD - 1)
                    mm.then_inc(done, 1)

            @block.scalar
            def _(act):
                def keep(t):
                    if t >= 2:
                        act.wait_ge(done, t - 1)
                    for i in range(2):
                        act.wait_ge(turned, 2 * t + i + 1)
                        nc.scalar.copy(mT[:, t % 2, 4 * i:4 * i + 4, :].rearrange("p a b -> p (a b)"), bank[:, (2 * t + i) % 4, :]).then_inc(kept, 1)

                keep(0)
                for t in range(TILES):
                    if t + 1 < TILES:
                        keep(t + 1)
                    layer_norm_scalar(nc, act, x, t, s_sum, s_root, s_norm, mv)

            @block.vector
            def _(dve):
                ch = Chain(dve, chain)
                dve.wait_ge(here, 48)
                for t in range(TILES):
                    dve.wait_ge(done, t + 1)
                    nc.vector.scalar_tensor_tensor(out=x[:, t, :], in0=x[:, t, :], scalar=ALPHA,
                                                   in1=bank[:, 4 + 2 * (t % 2):6 + 2 * (t % 2), :].rearrange("p a b -> p (a b)"),
                                                   op0=ALU.mult, op1=ALU.add).then_inc(added, 1)
                    dve.wait_ge(added, t + 1)
                    layer_norm_vector(nc, dve, ch, x, t, s_sum, s_root, s_norm, stats, mv, gain[:, :], shift[:, :])


GI = 4
NGRP = NK // GI
QUADS = NGRP // 4
PER = 2 * HK * GI // NK


def peer_select(nc, name, C, xT, wq_dram, k1T_dram, k2T_dram, uT_dram, early, picks, expert, gate):
    T4 = SEQ // P
    rows = T_ROWS
    HALF = TOK // 2
    with Stage(nc, name) as st:
        sb, sem = st.sb, st.sem
        wq = sb("wq", [P, 2, KD, 512])
        kT = sb("kT", [P, 2, NK])
        qT = sb("qT", [P, 2, TOK])
        s = sb("scores", [P, 2, TILES, NK])
        s2 = sb("scores_rest", [P, TILES, NK])
        val = sb("val", [P, TILES, PH, 2, PK])
        idx = sb("idx", [P, TILES, PH, 2, PK], U32)
        idxf = sb("idxf", [P, PH, 2, PK])
        cand, cand2 = sb("cand", [P, PH, PK * PK]), sb("cand_rest", [P, PH, PK * PK])
        top, sel = sb("top", [P, PH, PK]), sb("sel", [P, PH, PK], U32)
        ab, abf = sb("ab", [P, 2, HK], U32), sb("abf", [P, 2, HK])
        out = sb("out", [P, 3, HK])
        eg, zg = sb("eg", [P, PH, PK]), sb("zg", [P, 2, PH])
        bank = st.banks("bank", 8)
        w_in, k_in = [sem("wq_loaded0"), sem("wq_loaded1")], sem("sub_keys_loaded")
        q_ok, q_kept, s_ok, s_kept, s_used = sem("queries"), sem("queries_kept"), sem("scores"), sem("scores_kept"), sem("scores_ranked")
        chain, diff, expd = sem("vector_chain"), sem("gate_logits"), sem("gate_exps")
        out_ok, turned, kept = sem("picks_ready"), sem("picks_turned"), sem("picks_kept")
        NC_ = 2 * PH
        EXP_AT = {4 + 6 * n: n for n in range(TILES)}
        TURN_AT = {7 + 6 * n: n for n in range(TILES - 1)}
        u = wq[:, :, :, :].rearrange("p a k n -> p a (k n)").rearrange("p a (c k x) -> p a c k x", c=GI, k=KD)
        hidden = sb("hidden", [P, 2, GI, DENSE])
        u_in, sent = [sem(f"early_u_loaded{i}") for i in range(2)], [sem(f"early_sent{i}") for i in range(2)]
        e_dots, e_gelus = sem("early_dots"), sem("early_gelus")
        FINAL = [t for t in range(TILES) if t != GT] + [GT]
        with nc.Block() as block:
            @block.sync
            def _(sp):
                sp.dma_start(kT[:, 0, :], k1T_dram).then_inc(k_in, 16)
                sp.dma_start(kT[:, 1, :], k2T_dram).then_inc(k_in, 16)
                wv = wq_dram.rearrange("(k p) n -> p k n", p=P)
                for n in range(4):
                    if n >= 2:
                        sp.wait_ge(q_ok, 4 * (n - 1))
                    sp.dma_start(wq[:, n % 2, :, :], wv[:, :, n * 512:(n + 1) * 512]).then_inc(w_in[n % 2], 16)

                def load_u(e):
                    if e < 2:
                        sp.wait_ge(q_ok, 4 * (e + 3))
                    else:
                        sp.wait_ge(e_dots, GI * (e - 1))
                    sp.dma_start(u[:, e % 2, :, :, :].rearrange("p a b c -> p (a b c)"), uT_dram[4 * e + 3]).then_inc(u_in[e % 2], 16)

                load_u(0)
                load_u(1)
                for e in range(QUADS):
                    if e + 2 < QUADS:
                        load_u(e + 2)
                    sp.wait_ge(e_gelus, GI * (e + 1))
                    sp.dma_start(early[e], hidden[:, e % 2, :, :].rearrange("p a b -> p (a b)")).then_inc(sent[e % 2], 16)
                for i in range(2):
                    sp.wait_ge(sent[i], 16 * (QUADS // 2))

            @block.tensor
            def _(pe):
                pe.wait_ge(k_in, 32)
                for c in range(NC_ + 1):
                    if c < NC_:
                        n = c // 4
                        pe.wait_ge(w_in[n % 2], 16 * (n // 2 + 1))
                        if c >= 2:
                            pe.wait_ge(q_kept, c - 1)
                        for i in range(2):
                            for k in range(KD):
                                mm = nc.tensor.matmul(bank[:, 2 * (c % 2) + i, 0:HALF], wq[:, n % 2, k, c % 4 * P:(c % 4 + 1) * P],
                                                      xT[:, k, i * HALF:(i + 1) * HALF], start=k == 0, stop=k == KD - 1)
                        mm.then_inc(q_ok, 1)
                    if c:
                        d = c - 1
                        pe.wait_ge(q_kept, d + 1)
                        if d >= 2:
                            pe.wait_ge(s_kept, 2 * (d - 1))
                        for t in range(TILES):
                            o = bank[0:rows[t], 4 + 2 * (d % 2) + t // T4, t % T4 * P:(t % T4 + 1) * P]
                            mm = nc.tensor.matmul(o, qT[:, d % 2, START[t]:START[t] + rows[t]], kT[:, d % 2, :], start=True, stop=True)
                        mm.then_inc(s_ok, 1)
                pe.wait_ge(s_kept, 2 * NC_)

                def turn_picks(n):
                    t = FINAL[n]
                    r = rows[t]
                    pe.wait_ge(out_ok, n + 1)
                    if n >= 2:
                        pe.wait_ge(kept, n - 1)
                    for i in range(3):
                        mm = nc.tensor.transpose(bank[:, n % 2, i * P:i * P + r], out[0:r, i, :], C["ident"][0:r, 0:r])
                    mm.then_inc(turned, 1)

                for c in range(QUADS * GI):
                    e, j = c // GI, c % GI
                    if j == 0:
                        pe.wait_ge(u_in[e % 2], 16 * (e // 2 + 1))
                    if c >= 4:
                        pe.wait_ge(e_gelus, c - 3)
                    for k in range(KD):
                        mm = nc.tensor.matmul(bank[:, 4 + j, 0:DENSE], u[:, e % 2, j, k, :], xT[:, k, 0:DENSE], start=k == 0, stop=k == KD - 1)
                    mm.then_inc(e_dots, 1)
                    if c in TURN_AT:
                        turn_picks(TURN_AT[c])

            @block.scalar
            def _(act):
                for c in range(NC_ + 1):
                    if c < NC_:
                        act.wait_ge(q_ok, c + 1)
                        if c >= 2:
                            act.wait_ge(s_ok, c - 1)
                        nc.scalar.copy(qT[:, c % 2, :].rearrange("p (a x) -> p a x", a=2), bank[:, 2 * (c % 2):2 * (c % 2) + 2, 0:HALF]).then_inc(q_kept, 1)
                    if c:
                        d = c - 1
                        act.wait_ge(s_ok, d + 1)
                        if d >= 2:
                            act.wait_ge(s_used, d - 1)
                        nc.scalar.copy(s[:, d % 2, 0:T4, :].rearrange("p a b -> p (a b)"), bank[:, 4 + 2 * (d % 2), :]).then_inc(s_kept, 1)
                        nc.scalar.copy(s[0:rows[T4], d % 2, T4, :], bank[0:rows[T4], 5 + 2 * (d % 2), 0:P]).then_inc(s_kept, 1)
                for c in range(QUADS * GI):
                    e, j = c // GI, c % GI
                    act.wait_ge(e_dots, c + 1)
                    if e >= 2 and j == 0:
                        act.wait_ge(sent[e % 2], 16 * (e // 2))
                    nc.scalar.activation(hidden[:, e % 2, j, :], bank[:, 4 + j, 0:DENSE], ACT.Gelu).then_inc(e_gelus, 1)
                    if c in EXP_AT:
                        n = EXP_AT[c]
                        r = rows[FINAL[n]]
                        act.wait_ge(diff, n + 1)
                        nc.scalar.activation(eg[0:r, :, :], eg[0:r, :, :], ACT.Exp).then_inc(expd, 1)
                    if c in TURN_AT:
                        n = TURN_AT[c]
                        t = FINAL[n]
                        act.wait_ge(turned, n + 1)
                        src = bank[:, n % 2, 0:3 * P].rearrange("p (i x) -> p i x", i=3)[:, :, 0:rows[t]]
                        nc.scalar.copy(picks[:, :, START[t]:START[t] + rows[t]], src).then_inc(kept, 1)

            @block.vector
            def _(dve):
                V = nc.vector
                ch = Chain(dve, chain)
                tt = V.tensor_tensor

                def best16(items):
                    for n, step in enumerate((
                            lambda a, r, v, i: V.max(v[:, 0:8], a),
                            lambda a, r, v, i: V.max_index(i[:, 0:8], v[:, 0:8], a),
                            lambda a, r, v, i: V.match_replace(r, v[:, 0:8], a, NEG),
                            lambda a, r, v, i: V.max(v[:, 8:16], r),
                            lambda a, r, v, i: V.max_index(i[:, 8:16], v[:, 8:16], r))):
                        for item in items:
                            ins = step(*item)
                        ch(ins)

                for c in range(NC_):
                    h, half = c // 2, c % 2
                    dve.wait_ge(s_kept, 2 * (c + 1))
                    best16([(s[0:rows[t], c % 2, t, :], s2[0:rows[t], t, :], val[0:rows[t], t, h, half, :], idx[0:rows[t], t, h, half, :])
                            for t in range(TILES)])
                    V.tensor_copy(zg[0:1, 0, 0:1], val[0:1, 0, h, half, 0:1]).then_inc(s_used, 1)
                for n, t in enumerate(FINAL):
                    r = slice(0, rows[t])
                    c4 = cand[r].rearrange("p h (a b) -> p h a b", b=PK)
                    v1 = val[r, t, :, 0, :].unsqueeze(3).to_broadcast([rows[t], PH, PK, PK])
                    v2 = val[r, t, :, 1, :].unsqueeze(2).to_broadcast([rows[t], PH, PK, PK])
                    V.tensor_copy(idxf[r], idx[r, t])
                    ch(tt(c4, v1, v2, ALU.add))
                    best16([(cand[r, h, :], cand2[r, h, :], top[r, h, :], sel[r, h, :]) for h in range(PH)])
                    flat = sel[r].rearrange("p h k -> p (h k)")
                    V.tensor_scalar(ab[r, 0, :], flat, 4, None, ALU.logical_shift_right)
                    V.tensor_scalar(ab[r, 1, :], flat, PK - 1, None, ALU.bitwise_and)
                    ch(tt(eg[r], top[r], top[r, :, 0:1].to_broadcast([rows[t], PH, PK]), ALU.subtract))
                    V.tensor_copy(abf[r], ab[r]).then_inc(diff, 1)
                    dve.wait_ge(diff, n + 1)
                    if n:
                        dve.wait_ge(turned, n)
                    for i in range(2):
                        e = cand[r].rearrange("p h x -> p (h x)")
                        e3 = e.rearrange("p (n a) -> p n a", a=PK)
                        ch(tt(e3, last(abf[r, i, :], PK), mid(C["iota"][r, 0:PK], HK), ALU.is_equal))
                        e4 = e.rearrange("p (h k a) -> p h k a", h=PH, a=PK)
                        ch(tt(e4, e4, idxf[r, :, i, :].unsqueeze(2).to_broadcast([rows[t], PH, PK, PK]), ALU.mult))
                        ch(V.tensor_reduce(out[r, i, :], e3, AX, ALU.add))
                    dve.wait_ge(expd, n + 1)
                    ch(V.tensor_reduce(zg[r, 0, :], eg[r], AX, ALU.add))
                    ch(V.reciprocal(zg[r, 1, :], zg[r, 0, :]))
                    tt(out[r, 2, :].rearrange("p (h k) -> p h k", h=PH), eg[r], last(zg[r, 1, :], PK), ALU.mult).then_inc(out_ok, 1)
                    dve.wait_ge(out_ok, n + 1)
                ch(V.scalar_tensor_tensor(out=abf[:, 0, :], in0=out[:, 0, :], scalar=float(NK), in1=out[:, 1, :], op0=ALU.mult, op1=ALU.add))
                V.tensor_copy(expert, abf[:, 0, :])
                ch(V.tensor_copy(gate, out[:, 2, :]))


BLK = 32
NBLK = DENSE // BLK


def peer_spread(nc, name, C, picks, grids):
    G4 = BLK // 4
    with Stage(nc, name) as st:
        sb, sem = st.sb, st.sem
        rowhot, colhot = sb("rowhot", [P, 4, 4, NK]), sb("colhot", [P, 4, 4, NK])
        grid = sb("grid", [P, 2, NK, BLK])
        apart = sb("apart", [P, 2, NK])
        own = sb("own", [P, 2, 3, BLK])
        bank = st.banks("bank", 4)
        own_ok, away, marked_s = sem("own_ready"), sem("distances"), sem("picks_marked_by_scalar")
        marked, kept, free = sem("picks_marked"), sem("grids_kept"), sem("marks_used")
        sent = [sem("grid_sent0"), sem("grid_sent1")]
        TWO = NBLK // 2

        def block_steps(work, eng):
            with eng.Fori(0, TWO) as m:
                for u in range(2):
                    work(m * 2 + u, u, m)
            work(NBLK - 1, (NBLK - 1) % 2, TWO)

        with nc.Block() as block:
            @block.vector
            def _(dve):
                def copies(b, u):
                    here = lambda i: picks[:, i, bass.ds(b * BLK, BLK)]
                    nc.vector.tensor_scalar(own[:, u, 0, :], here(0), -1.0, None, ALU.mult)
                    nc.vector.tensor_scalar(own[:, u, 1, :], here(2), -1.0, None, ALU.mult)
                    nc.vector.tensor_copy(own[:, u, 2, :], here(2)).then_inc(own_ok, 1)

                def work(b, u, m):
                    if m is not TWO:
                        dve.wait_ge(marked_s, b * G4 + 1)
                        copies(b + 1, 1 - u)
                    for j in range(G4):
                        dve.wait_ge(free, b * G4 + j + 1)
                        nc.vector.tensor_tensor(colhot[:, j % 4, :, :], mid(C["iota"], 4), last(picks[:, 1, bass.ds(b * BLK + 4 * j, 4)], NK), ALU.is_equal)
                        for i in range(3):
                            tok = b * BLK + (4 * j + i)
                            ins = nc.vector.tensor_scalar(rowhot[:, j % 4, i, :], C["iota"], picks[:, 0, bass.ds(tok, 1)],
                                                          picks[:, 2, bass.ds(tok, 1)], ALU.is_equal, ALU.mult)
                        ins.then_inc(marked, 1)
                copies(0, 0)
                block_steps(work, dve)

            @block.tensor
            def _(pe):
                pe.sem_inc(free, 4)
                def work(b, u, m):
                    for j in range(G4):
                        pe.wait_ge(marked, b * G4 + j + 1)
                        pe.wait_ge(marked_s, b * G4 + j + 2)
                        pe.wait_ge(kept, b * G4 + j + 1)
                        for i in range(4):
                            mm = nc.tensor.matmul(bank[:, j % 4, i * NK:(i + 1) * NK], rowhot[:, j % 4, i, :], colhot[:, j % 4, i, :], start=True, stop=True)
                        mm.then_inc(free, 1)
                block_steps(work, pe)

            @block.scalar
            def _(act):
                act.sem_inc(kept, 4)
                act.sem_inc(marked_s, 1)

                def mark(b, u, j):
                    if j == 0:
                        act.wait_ge(own_ok, b + 1)
                    act.wait_ge(free, b * G4 + j + 1)
                    tok = slice(4 * j + 3, 4 * j + 4)
                    nc.scalar.activation(apart[:, j % 2, :], C["iota"], ACT.Abs, bias=own[:, u, 0, tok]).then_inc(away, 1)
                    act.wait_ge(away, b * G4 + j + 1)
                    nc.scalar.activation(rowhot[:, j % 4, 3, :], apart[:, j % 2, :], ACT.Relu, bias=own[:, u, 2, tok], scale=own[:, u, 1, tok]).then_inc(marked_s, 1)

                mark(0, 0, 0)

                def work(b, u, m):
                    act.wait_ge(sent[u], m * 16 + 16)
                    for j in range(G4):
                        if j < G4 - 1:
                            mark(b, u, j + 1)
                        elif m is not TWO:
                            mark(b + 1, 1 - u, 0)
                        act.wait_ge(free, b * G4 + j + 5)
                        nc.scalar.copy(grid[:, u, :, 4 * j:4 * j + 4], bank[:, j % 4, :].rearrange("p (t x) -> p x t", t=4)).then_inc(kept, 1)
                block_steps(work, act)

            @block.sync
            def _(sp):
                for u in range(2):
                    sp.sem_inc(sent[u], 16)
                def work(b, u, m):
                    sp.wait_ge(kept, b * G4 + G4 + 4)
                    sp.dma_start(grids[bass.ds(b, 1), :, :, :].rearrange("a p c t -> p (a c t)"), grid[:, u, :, :].rearrange("p c t -> p (c t)")).then_inc(sent[u], 16)
                block_steps(work, sp)
                sp.wait_ge(sent[0], 16 * (TWO + 2))
                sp.wait_ge(sent[1], 16 * (TWO + 1))


def peer_experts(nc, name, xT, x_rows, expert, gate, uT_dram, early, v_dram, u_rows, v_rows, grids, yT, y_rows):
    with Stage(nc, name) as st:
        sb, sem = st.sb, st.sem
        u = sb("u", [P, 2, GI, KD, NK])
        v = sb("v", [P, 2, GI, D])
        gates = sb("gates", [P, 2, NBLK, GI * BLK])
        act_s = sb("act", [P, 2, DENSE])
        w = sb("w", [P, 2, GI, DENSE])
        RING = 4
        rows = sb("rows", [P, RING, D])
        idx8 = sb("idx8", [P, 2, PER], U32)
        some = sb("some", [P, 2, PER])
        dot, weight = sb("dot", [P, HK]), sb("weight", [P, HK])
        bank = st.banks("bank", 8)
        u_in, v_in, g_in = ([sem(f"{n}_loaded{i}") for i in range(2)] for n in ("u", "v", "gates"))
        dots, gelus, weighed = sem("dots"), sem("gelus"), sem("weighed")
        sums, added = sem("sums"), sem("sums_added")
        row_in = [sem(f"row_gathered{i}") for i in range(RING)]
        slot_taken = sem("slot_taken")
        row_used, idx_ok, some_ok, dot_ok, weight_ok = sem("row_used"), sem("places_ready"), sem("weights_ready"), sem("row_dots"), sem("row_gelus")
        MID = NGRP // 4
        e_in = sem("early_loaded")

        def halves(eng, first, second, between):
            def four(m, which, more=True):
                for r in range(4):
                    if r < 3 or more:
                        first(m, r + 1)
                    second(m, r, which)
            first(0, 0)
            with eng.Fori(0, QUADS // 2) as m:
                four(m, "u")
            between()
            with eng.Fori(QUADS // 2, QUADS - 1) as m:
                four(m, "v")
            four(QUADS - 1, "v", more=False)

        PLACE = {0: 0, 1: 1, 2: 2, 4: 3}
        SLOT = {0: 0, 1: 1, 2: 0, 4: 0}
        loads_of_u = lambda m, r: m + 1 if r == 1 else m * 2 + (1 + r // 2)
        loads_of_rest = lambda m, r: m * 2 + (r // 2 + 1)

        with nc.Block() as block:
            @block.sync
            def _(sp):
                def load_u(m, r):
                    s = SLOT[r]
                    sp.dma_start(u[:, s, :, :, :].rearrange("p a b c -> p (a b c)"), uT_dram[bass.ds(m * 4 + r, 1), :, :].rearrange("a p x -> p (a x)")).then_inc(u_in[s], 16)

                def load_rest(m, r):
                    g, p = m * 4 + r, r % 2
                    sp.dma_start(gates[:, p, :, :], grids[:, :, bass.ds(g * GI, GI), :].rearrange("b p c t -> p b (c t)")).then_inc(g_in[p], 16)
                    sp.dma_start(v[:, p, :, :].rearrange("p a b -> p (a b)"), v_dram[:, bass.ds(g * GI * D, GI * D)]).then_inc(v_in[p], 16)

                load_u(0, 0)
                load_rest(0, 0)
                load_u(0, 1)
                load_rest(0, 1)

                def four(m, more):
                    sp.wait_ge(dots, m * 12 + 4)
                    load_u(m, 2)
                    if more:
                        sp.wait_ge(dots, m * 12 + 8)
                        load_u(m + 1, 1)
                    sp.wait_ge(sums, (m * 4 + 1) * KD)
                    load_rest(m, 2)
                    if more:
                        sp.wait_ge(dots, m * 12 + 12)
                        load_u(m + 1, 0)
                    sp.wait_ge(sums, (m * 4 + 2) * KD)
                    sp.dma_start(w[:, 1, :, :].rearrange("p a b -> p (a b)"), early[bass.ds(m, 1), :, :].rearrange("a p x -> p (a x)")).then_inc(e_in, 16)
                    load_rest(m, 3)
                    if more:
                        sp.wait_ge(sums, (m * 4 + 3) * KD)
                        load_rest(m, 4)
                        sp.wait_ge(sums, (m * 4 + 4) * KD)
                        load_rest(m, 5)
                with sp.Fori(0, QUADS - 1) as m:
                    four(m, True)
                four(QUADS - 1, False)

            @block.gpsimd
            def _(pool):
                def gather(g, p, table, places):
                    nc.gpsimd.tensor_copy(idx8[:, p, :], expert[:, bass.ds(places * PER, PER)]).then_inc(idx_ok, 1)
                    for c in range(PER):
                        pool.wait_ge(row_used, g * PER + c + 1)
                        if c == 0:
                            pool.wait_ge(idx_ok, g + 1)
                        pool.sem_inc(slot_taken, 1)
                        pool.indirect_dma_start(rows[:, c % RING, :], None, table, bass.IndirectOffsetOnAxis(ap=idx8[:, p, c:c + 1], axis=0)).then_inc(row_in[c % RING], 16)

                with pool.Fori(0, MID) as m:
                    for p in range(2):
                        gather(m * 2 + p, p, u_rows, m * 2 + p)
                with pool.Fori(MID, NGRP // 2) as m:
                    for p in range(2):
                        gather(m * 2 + p, p, v_rows, m * 2 + p - 2 * MID)

            @block.tensor
            def _(pe):
                def first(m, r):
                    if r == 3:
                        return
                    s, base = SLOT[r], m * 12 + 4 * PLACE[r]
                    pe.wait_ge(u_in[s], loads_of_u(m, r) * 16)
                    for j in range(GI):
                        if r:
                            pe.wait_ge(gelus, base + (j - 3))
                        for k in range(KD):
                            mm = nc.tensor.matmul(bank[:, j, 0:DENSE], u[:, s, j, k, :], xT[:, k, 0:DENSE], start=k == 0, stop=k == KD - 1)
                        mm.then_inc(dots, 1)

                def second(m, r, which):
                    g, p = m * 4 + r, r % 2
                    pe.wait_ge(v_in[p], loads_of_rest(m, r) * 16)
                    pe.wait_ge(weighed, g * GI + GI)
                    for c in range(KD):
                        pe.wait_ge(added, g * KD + c + 1)
                        for j in range(GI):
                            mm = nc.tensor.matmul(bank[:, 4 + c % 4, 0:DENSE], v[:, p, j, c * P:(c + 1) * P], w[:, p, j, :], start=j == 0, stop=j == GI - 1)
                        mm.then_inc(sums, 1)
                halves(pe, first, second, lambda: None)

            @block.scalar
            def _(act):
                def first(m, r):
                    if r == 3:
                        return
                    for j in range(GI):
                        act.wait_ge(dots, m * 12 + (4 * PLACE[r] + j + 1))
                        if r or j >= 2:
                            act.wait_ge(weighed, m * 4 * GI + (r * GI + j - 1 - (GI if r == 4 and j < 2 else 0)))
                        nc.scalar.activation(act_s[:, j % 2, :], bank[:, j, 0:DENSE], ACT.Gelu).then_inc(gelus, 1)

                def between():
                    act.wait_ge(dot_ok, 2 * MID)
                    nc.scalar.activation(dot[:, :], dot[:, :], ACT.Gelu).then_inc(weight_ok, 1)
                halves(act, first, lambda m, r, which: None, between)

            @block.vector
            def _(dve):
                V = nc.vector
                for i in range(4):
                    V.memset(yT[:, 2 * i:2 * i + 2, :], 0.0).then_inc(added, 1)
                    V.memset(y_rows[:, i * 256:(i + 1) * 256], 0.0).then_inc(row_used, 1)

                def first(m, r):
                    p = r % 2
                    dve.wait_ge(g_in[p], loads_of_rest(m, r) * 16)
                    if r == 3:
                        dve.wait_ge(e_in, m * 16 + 16)
                    for j in range(GI):
                        if r != 3:
                            dve.wait_ge(gelus, m * 12 + (4 * PLACE[r] + j + 1))
                        src = w[:, p, j, :] if r == 3 else act_s[:, j % 2, :]
                        V.tensor_tensor(w[:, p, j, :].rearrange("p (b t) -> p b t", t=BLK), src.rearrange("p (b t) -> p b t", t=BLK),
                                        gates[:, p, :, j * BLK:(j + 1) * BLK], ALU.mult).then_inc(weighed, 1)

                def second(m, r, which):
                    g, p = m * 4 + r, r % 2
                    if which == "v":
                        V.tensor_copy(some[:, p, :], weight[:, bass.ds((g - 2 * MID) * PER, PER)]).then_inc(some_ok, 1)
                        dve.wait_ge(some_ok, g - 2 * MID + 1)
                    for c in range(KD):
                        dve.wait_ge(sums, g * KD + c + 1)
                        V.tensor_tensor(yT[:, c, :], yT[:, c, :], bank[:, 4 + c % 4, 0:DENSE], ALU.add).then_inc(added, 1)
                        dve.wait_ge(row_in[c % RING], (g * 2 + (c // RING + 1)) * 16)
                        r = rows[:, c % RING, :]
                        if which == "u":
                            V.tensor_tensor_reduce(r, r, x_rows, 1.0, 0.0, ALU.mult, ALU.add, some[:, p, c:c + 1]).then_inc(row_used, 1)
                        else:
                            dve.wait_ge(row_used, g * PER + c + 4)
                            V.scalar_tensor_tensor(out=y_rows, in0=r, scalar=some[:, p, c:c + 1], in1=y_rows, op0=ALU.mult, op1=ALU.add).then_inc(row_used, 1)
                    if which == "u":
                        dve.wait_ge(row_used, g * PER + PER + 4)
                        V.tensor_copy(dot[:, bass.ds(g * PER, PER)], some[:, p, :]).then_inc(dot_ok, 1)

                def between():
                    dve.wait_ge(weight_ok, 1)
                    V.tensor_tensor(weight[:, :], dot[:, :], gate, ALU.mult).then_inc(weight_ok, 1)
                    dve.wait_ge(weight_ok, 2)
                halves(dve, first, second, between)


def peer_norm(nc, name, C, yT, y_rows, gain_dram, shift_dram, x):
    with Stage(nc, name) as st:
        gain, shift = st.sb("gain", [P, D]), st.sb("shift", [P, D])
        pad = st.sb("pad", [P, KD, P])
        stats, mv = st.sb("stats", [P, 2, 6]), st.sb("mv", [P, 6])
        bank = st.banks("bank", 4)
        here, padded = st.sem("rows_loaded"), st.sem("samples_padded")
        turned, added = st.sem("turned"), st.sem("residual_added")
        s_sum, s_root, s_norm, chain = st.sem("statistics"), st.sem("deviation"), st.sem("normed"), st.sem("vector_chain")
        with nc.Block() as block:
            @block.sync
            def _(sp):
                sp.dma_start(gain[:, :], gain_dram.partition_broadcast(P)).then_inc(here, 16)
                sp.dma_start(shift[:, :], shift_dram.partition_broadcast(P)).then_inc(here, 16)

            @block.gpsimd
            def _(pool):
                nc.gpsimd.memset(pad[:, :, :], 0.0).then_inc(padded, 1)
                pool.wait_ge(padded, 1)
                nc.gpsimd.tensor_copy(pad[:, :, :].rearrange("p k (b s) -> p k b s", s=SEG)[:, :, :, 1:1 + NS],
                                      yT[:, :, SAMP_AT:DENSE].rearrange("p k (b s) -> p k b s", s=NS)).then_inc(padded, 1)

            @block.tensor
            def _(pe):
                for t in range(TILES):
                    if t == GT:
                        continue
                    if t == SAMP:
                        pe.wait_ge(padded, 2)
                    if t >= 2:
                        pe.wait_ge(added, t - 1)
                    for k in range(KD):
                        src = yT[:, k, t * P:(t + 1) * P] if t < SAMP else pad[:, k, :]
                        mm = nc.tensor.transpose(bank[:, 2 * (t % 2) + k // 4, k % 4 * P:(k % 4 + 1) * P], src, C["ident"])
                    mm.then_inc(turned, 1)

            @block.scalar
            def _(act):
                for t in range(TILES):
                    layer_norm_scalar(nc, act, x, t, s_sum, s_root, s_norm, mv)

            @block.vector
            def _(dve):
                ch = Chain(dve, chain)
                dve.wait_ge(here, 32)
                for t in range(TILES):
                    if t != GT:
                        dve.wait_ge(turned, t + 1 - (t > GT))
                    nc.vector.scalar_tensor_tensor(out=x[:, t, :], in0=x[:, t, :], scalar=ALPHA,
                                                   in1=y_rows if t == GT else bank[:, 2 * (t % 2):2 + 2 * (t % 2), :].rearrange("p a b -> p (a b)"),
                                                   op0=ALU.mult, op1=ALU.add).then_inc(added, 1)
                    dve.wait_ge(added, t + 1)
                    layer_norm_vector(nc, dve, ch, x, t, s_sum, s_root, s_norm, stats, mv, gain[:, :], shift[:, :])


def mlstm(nc, C, A, proj, mix, O):
    VA = DV + 1
    PB = 3
    with Stage(nc, "mlstm") as st:
        sb, sem = st.sb, st.sem
        bias = sb("bias", [P, 2 * H])
        mh = sb("mh", [P, H * DV])
        g16s, g16b = sb("g16s", [P, TILES, 2 * H]), sb("g16b", [P, TILES, 2 * H])
        lfs = sb("lfs", [P, TILES, H])
        e, m, mu_b = sb("e", [P, H]), sb("m", [P, H]), sb("mu_b", [P, 2 * H])
        mx, ml_bl = sb("mx", [P, H]), sb("ml_bl", [P, 2 * H])
        ex_in, ex = sb("ex_in", [P, 4, H]), sb("ex", [P, 4, H])
        Em = sb("Em", [P, H, P])
        big = sb("big", [P, H, P])
        qT, kT, qpT = (sb(n, [P, PAIRS, P]) for n in ("qT", "kT", "qpT"))
        attT = sb("attT", [P, H, P])
        qp, kw = sb("qp", [P, AW]), sb("kw", [P, AW])
        va = sb("va", [P, H, VA])
        den = sb("den", [P, 3, H])
        ms = sb("ms", [P, 3, H])
        Sp = sb("Sp", [P, PAIRS, VA])
        Ss = sb("Ss", [P, NB, PAIRS, VA])
        dsel, dec = sb("dsel", [P, NB, H]), sb("dec", [P, NB, H])
        bank = st.banks("bank", 8)
        here, init = sem("arrays_loaded"), sem("state_zeroed")
        pre, cap, cap2, em, ln = sem("gate_sums"), sem("gate_tanh"), sem("gates_capped"), sem("forget_exp"), sem("forget_log")
        lf_ok, cum, diag, ebc, mu_ok, lastr = sem("log_forget"), sem("cumulated"), sem("diagonals"), sem("e_spread"), sem("mu_ready"), sem("last_rows")
        emx, exq, exs = sem("score_exponents"), sem("small_exponents"), sem("exps")
        qk_t, qk_tk, qk, att, att_t, att_tk = sem("qk_turned"), sem("qk_turned_kept"), sem("qk_products"), sem("weights_ready"), sem("weights_turned"), sem("weights_turned_kept")
        qp_ok, num, sig, ms_ok, root = sem("scaled_ready"), sem("numerators"), sem("output_gates"), sem("mean_squares"), sem("roots")
        spread, spread_used, stp, tile_ok, dsel_ok = sem("spread_ready"), sem("spread_used"), sem("state_products"), sem("tile_done"), sem("decay_rows")
        num_kept = sem("numerators_kept")
        chain, outs, dcol = sem("vector_chain"), sem("outputs_stored"), sem("decays_spread")
        NUM = ((5, 6), (7, 0))
        hb = lambda h: bank[:, NUM[h % 2][h // 2 // PB], h // 2 % PB * VA:(h // 2 % PB + 1) * VA]

        with nc.Block() as block:
            @block.sync
            def _(sp):
                for dst, src in ((bias[:, 0:H], A["b_i_o"].partition_broadcast(P)), (bias[:, H:2 * H], A["b_f_o"].partition_broadcast(P)),
                                 (mh[:, :], A["mh_norm_o"].partition_broadcast(P)), (Ss[:, :, :, :], A["cn_s"])):
                    sp.dma_start(dst, src).then_inc(here, 16)
                sp.wait_ge(tile_ok, SAMP)
                sp.dma_start(O["cn_p"], Sp[:, :, :]).then_inc(outs, 16)
                sp.dma_start(O["m_p"], m[:, :]).then_inc(outs, 16)
                sp.wait_ge(outs, 32)
                sp.dma_start(m[:, :], A["m_s"]).then_inc(here, 16)
                sp.wait_ge(tile_ok, TILES)
                sp.dma_start(O["cn_s"], Ss[:, :, :, :]).then_inc(outs, 16)
                sp.dma_start(O["m_s"], m[:, :]).then_inc(outs, 16)
                sp.wait_ge(outs, 64)

            @block.tensor
            def _(pe):
                mmul, turn_ = nc.tensor.matmul, nc.tensor.transpose
                for t in range(TILES):
                    one = t < SAMP
                    q, k = proj[:, t, 0:AW], proj[:, t, AW:2 * AW]
                    if t:
                        pe.wait_ge(num_kept, t)
                    for i, x in enumerate((q, k)):
                        for p in range(PAIRS):
                            mm = turn_(bank[:, 3 + i, p * P:(p + 1) * P], x[:, p * P:(p + 1) * P], C["ident"])
                    mm.then_inc(qk_t, 1)
                    pe.wait_ge(lf_ok, 2)
                    mmul(bank[:, 0, 0:H], C["upto" if one else "upto16"], lfs[:, t, :], start=True, stop=True).then_inc(cum, 1)
                    pe.wait_ge(diag, t + 1)
                    for i in range(2):
                        mm = mmul(bank[:, 1 + i, :], C["ones"], big[:, 4 * i:4 * i + 4, :].rearrange("p a b -> p (a b)"), start=True, stop=True)
                    mm.then_inc(ebc, 1)
                    pe.wait_ge(qk_tk, 2 * (t + 1))
                    for g in range(2):
                        for p in range(PAIRS):
                            mm = mmul(bank[:, 5 + g, p * P:(p + 1) * P], qT[g * 64:(g + 1) * 64, p, :], kT[g * 64:(g + 1) * 64, p, :], start=True, stop=True)
                    mm.then_inc(qk, 1)
                    pe.wait_ge(mu_ok, t + 1)
                    mmul(bank[:, 0, 2 * H:4 * H], C["last" if one else "last_s"], mu_b[:, :], start=True, stop=True).then_inc(lastr, 1)
                    pe.wait_ge(qp_ok, t + 1)
                    for p in range(PAIRS):
                        mm = turn_(bank[:, 3, p * P:(p + 1) * P], qp[:, p * P:(p + 1) * P], C["ident"])
                    mm.then_inc(qk_t, 1)
                    pe.wait_ge(att, t + 1)
                    for h in range(H):
                        mm = turn_(bank[:, 1 + h // 4, h % 4 * P:(h % 4 + 1) * P], big[:, h, :], C["ident"])
                    mm.then_inc(att_t, 1)
                    pe.wait_ge(att_tk, 3 * (t + 1))
                    for h in range(H):
                        p, g = h // 2, h % 2
                        half = slice(g * 64, (g + 1) * 64)
                        mm = mmul(hb(h), attT[:, h, :], va[:, h, :], start=True, stop=False)
                        if one:
                            mm = mmul(hb(h), qpT[half, p, :], Sp[half, p, :], start=False, stop=True)
                        else:
                            if g == 0:
                                pe.wait_ge(spread, p + 1)
                            for b in range(NB):
                                mm = mmul(hb(h), big[half, b, :], Ss[half, b, p, :], start=False, stop=b == NB - 1)
                            if g:
                                mm.then_inc(spread_used, 1)
                    mm.then_inc(num, 1) if one else None
                    if one:
                        for h in range(H):
                            p, g = h // 2, h % 2
                            mm = mmul(bank[g * 64:(g + 1) * 64, 1 + p // PB, p % PB * VA:(p % PB + 1) * VA], kw[:, h * 64:(h + 1) * 64], va[:, h, :], start=True, stop=True)
                        mm.then_inc(stp, 1)
                    else:
                        pe.wait_ge(dsel_ok, 1)
                        mmul(bank[:, 3, 0:NB * H], C["ones"], dsel[:, :, :].rearrange("p a b -> p (a b)"), start=True, stop=True).then_inc(dcol, 1)
                        for p in range(PAIRS):
                            pe.wait_ge(spread, PAIRS + p + 1)
                            for g in range(2):
                                for b in range(NB):
                                    mm = mmul(bank[g * 64:(g + 1) * 64, 1 + b // 2, b % 2 * VA:(b % 2 + 1) * VA], big[:, b, g * 64:(g + 1) * 64], va[:, 2 * p + g, :],
                                              start=True, stop=True)
                            mm.then_inc(stp, 1)

            @block.scalar
            def _(act):
                a_, cp = nc.scalar.activation, nc.scalar.copy
                flat = lambda x: x[:, :, :].rearrange("p a b -> p (a b)")
                act.wait_ge(pre, 1)
                a_(flat(g16b), flat(g16s), ACT.Tanh, scale=1.0 / CAP).then_inc(cap, 1)
                act.wait_ge(cap2, 1)
                a_(lfs[:, :, :], g16s[:, :, H:2 * H], ACT.Exp, scale=-1.0).then_inc(em, 1)
                act.wait_ge(em, 2)
                a_(flat(lfs), flat(lfs), ACT.Ln).then_inc(ln, 1)
                for t in range(TILES):
                    act.wait_ge(qk_t, 2 * t + 1)
                    cp(flat(qT), bank[:, 3, :]).then_inc(qk_tk, 1)
                    cp(flat(kT), bank[:, 4, :]).then_inc(qk_tk, 1)
                    act.wait_ge(exq, t + 1)
                    a_(flat(ex), flat(ex_in), ACT.Exp).then_inc(exs, 1)
                    act.wait_ge(emx, t + 1)
                    a_(flat(Em), flat(Em), ACT.Exp).then_inc(exs, 1)
                    act.wait_ge(qk_t, 2 * t + 2)
                    cp(flat(qpT), bank[:, 3, :]).then_inc(att_tk, 1)
                    act.wait_ge(att_t, t + 1)
                    for i in range(2):
                        cp(attT[:, 4 * i:4 * i + 4, :].rearrange("p a b -> p (a b)"), bank[:, 1 + i, :]).then_inc(att_tk, 1)
                    o = proj[:, t, 2 * AW + H * DV:2 * AW + 2 * H * DV]
                    a_(o, o, ACT.Sigmoid).then_inc(sig, 1)
                    act.wait_ge(ms_ok, t + 1)
                    a_(ms[:, 2, :], ms[:, 1, :], ACT.Sqrt).then_inc(root, 1)

            @block.vector
            def _(dve):
                V = nc.vector
                ch = Chain(dve, chain)
                tt, tsc, stt = V.tensor_tensor, V.tensor_scalar, V.scalar_tensor_tensor
                flat = lambda x: x.rearrange("p a b -> p (a b)")
                V.memset(va[:, :, DV:VA], 1.0)
                ch(V.memset(Sp[:, :, :], 0.0))
                ch(V.memset(m[:, :], 0.0))
                dve.wait_ge(here, 64)
                tt(g16s[:, :, :], proj[:, :, INO - 2 * H:INO], mid(bias[:, :], TILES), ALU.add).then_inc(pre, 1)
                dve.wait_ge(cap, 1)
                tsc(flat(g16s[:, :, :]), flat(g16b[:, :, :]), CAP, None, ALU.mult).then_inc(cap2, 1)
                dve.wait_ge(em, 1)
                tsc(flat(lfs[:, :, :]), flat(lfs[:, :, :]), 1.0, None, ALU.add).then_inc(em, 1)
                dve.wait_ge(ln, 1)
                tsc(flat(lfs[:, :, :]), flat(lfs[:, :, :]), -1.0, None, ALU.mult).then_inc(lf_ok, 1)
                dve.wait_ge(lf_ok, 1)
                tsc(lfs[:, SAMP, :], lfs[:, SAMP, :], C["real"], None, ALU.mult).then_inc(lf_ok, 1)

                h3 = lambda x: x.rearrange("p (h d) -> p h d", h=H)

                def begin(t):
                    V.tensor_copy(va[:, :, 0:DV], h3(proj[:, t, 2 * AW:2 * AW + H * DV]))
                    dve.wait_ge(cum, t + 1)
                    ch(V.tensor_copy(mu_b[:, H:2 * H], bank[:, 0, 0:H]))
                    ch(tt(e[:, :], g16s[:, t, 0:H], mu_b[:, H:2 * H], ALU.subtract))
                    tt(big[:, :, :], mid(C["ident"], H), last(e[:, :], P), ALU.mult).then_inc(diag, 1)

                begin(0)
                for t in range(TILES):
                    one = t < SAMP
                    q, k = proj[:, t, 0:AW], proj[:, t, AW:2 * AW]
                    if not one:
                        dve.wait_ge(here, 80)
                    dve.wait_ge(ebc, t + 1)
                    ch(tt(Em[:, :, :], bank[:, 1:3, :].rearrange("p a (h x) -> p (a h) x", x=P), mid(C["causal" if one else "causal_s"], H), ALU.add))
                    ch(V.tensor_reduce(mx[:, :], Em[:, :, :], AX, ALU.max))
                    tt(mu_b[:, 0:H], mx[:, :], m[:, :], ALU.max).then_inc(mu_ok, 1)
                    dve.wait_ge(mu_ok, t + 1)
                    tt(Em[:, :, :], Em[:, :, :], last(mu_b[:, 0:H], P), ALU.subtract).then_inc(emx, 1)
                    tt(ex_in[:, 0, :], m[:, :], mu_b[:, 0:H], ALU.subtract)
                    stt(ex_in[:, 1, :], mu_b[:, 0:H], -1.0, mu_b[:, H:2 * H], ALU.mult, ALU.subtract)
                    dve.wait_ge(lastr, t + 1)
                    ch(V.tensor_copy(ml_bl[:, :], bank[:, 0, 2 * H:4 * H]))
                    tt(ex_in[:, 2, :], e[:, :], ml_bl[:, 0:H], ALU.subtract)
                    tt(ex_in[:, 3, :], m[:, :], ml_bl[:, 0:H], ALU.subtract).then_inc(exq, 1)
                    dve.wait_ge(exq, t + 1)
                    tt(m[:, :], ml_bl[:, 0:H], ml_bl[:, H:2 * H], ALU.add)
                    dve.wait_ge(exs, 2 * (t + 1))
                    stt(h3(qp[:, :]), h3(q), HD ** -0.5, last(ex[:, 0, :], 64), ALU.mult, ALU.mult).then_inc(qp_ok, 1)
                    if not one:
                        ch(tsc(ex[:, 2, :], ex[:, 2, :], C["real"], None, ALU.mult))
                    ch(tt(h3(kw[:, :]), h3(k), last(ex[:, 2, :], 64), ALU.mult))
                    dve.wait_ge(qk, t + 1)
                    b4 = big[:, :, :].rearrange("p (q g) x -> p q g x", g=2)
                    e4 = Em[:, :, :].rearrange("p (q g) x -> p q g x", g=2)
                    for g in range(2):
                        ins = stt(b4[:, :, g, :], bank[:, 5 + g, :].rearrange("p (q x) -> p q x", x=P), HD ** -0.5, e4[:, :, g, :], ALU.mult, ALU.mult)
                    ins.then_inc(att, 1)
                    if not one:
                        dve.wait_ge(att_tk, 3 * (t + 1))
                        for p in range(PAIRS):
                            if p:
                                dve.wait_ge(spread_used, p)
                            tt(big[:, :, :], mid(qpT[:, p, :], NSEG), C["seg_of_col"].rearrange("p (c x) -> p c x", x=P), ALU.mult).then_inc(spread, 1)
                        dve.wait_ge(spread_used, PAIRS)
                        tt(dsel[:, :, :], mid(ex[:, 3, :], NB), last(C["newest"], H), ALU.mult).then_inc(dsel_ok, 1)
                        dve.wait_ge(dcol, 1)
                        ch(V.tensor_copy(flat(dec[:, :, :]), bank[:, 3, 0:NB * H]))
                        for p in range(PAIRS):
                            tt(big[:, :, :], mid(kw[:, p * P:(p + 1) * P], NSEG), last(C["seg_of_row"], P), ALU.mult).then_inc(spread, 1)
                            for g in range(2):
                                half = slice(g * 64, (g + 1) * 64)
                                ins = tt(Ss[half, :, p, :], Ss[half, :, p, :], dec[half, :, 2 * p + g:2 * p + g + 1].to_broadcast([64, NB, VA]), ALU.mult)
                            ch(ins)
                            dve.wait_ge(stp, SAMP + p + 1)
                            s4 = Ss[:, :, p, :].rearrange("p (a c) x -> p a c x", c=2)
                            ch(tt(s4, s4, bank[:, 1:5, 0:2 * VA].rearrange("p a (c x) -> p a c x", x=VA), ALU.add))
                    else:
                        dve.wait_ge(num, t + 1)
                        dve.wait_ge(stp, t + 1)
                        for h in range(H):
                            p, g = h // 2, h % 2
                            half = slice(g * 64, (g + 1) * 64)
                            ins = stt(Sp[half, p, :], Sp[half, p, :], ex[half, 3, h:h + 1], bank[half, 1 + p // PB, p % PB * VA:(p % PB + 1) * VA], ALU.mult, ALU.add)
                        ch(ins)
                    for h in range(H):
                        ins = V.tensor_copy(den[:, 0, h:h + 1], hb(h)[:, DV:VA])
                    ch(ins)
                    ch(tsc(den[:, 1, :], den[:, 0, :], -1.0, None, ALU.mult))
                    ch(tt(den[:, 0, :], den[:, 0, :], den[:, 1, :], ALU.max))
                    ch(tt(den[:, 0, :], den[:, 0, :], ex[:, 1, :], ALU.max))
                    ch(V.reciprocal(den[:, 2, :], den[:, 0, :]))
                    d4 = den[:, 2, :].rearrange("p (q g) -> p q g", g=2)
                    for g in range(2):
                        for i, n in enumerate((PB, PAIRS - PB)):
                            a = slice(i * PB, i * PB + n)
                            ins = tt(e4[:, a, g, :], bank[:, NUM[g][i], 0:n * VA].rearrange("p (q x) -> p q x", x=VA)[:, :, 0:DV], last(d4[:, a, g], DV), ALU.mult)
                    ins.then_inc(num_kept, 1)
                    dve.wait_ge(num_kept, t + 1)
                    if one:
                        begin(t + 1)
                    ch(tt(attT[:, :, :], Em[:, :, :], Em[:, :, :], ALU.mult))
                    ch(V.tensor_reduce(ms[:, 0, :], attT[:, :, :], AX, ALU.add))
                    tsc(ms[:, 1, :], ms[:, 0, :], 1.0 / DV, 1e-6, ALU.mult, ALU.add).then_inc(ms_ok, 1)
                    dve.wait_ge(root, t + 1)
                    ch(V.reciprocal(ms[:, 0, :], ms[:, 2, :]))
                    ch(tt(Em[:, :, :], Em[:, :, :], last(ms[:, 0, :], DV), ALU.mult))
                    ch(tt(flat(Em[:, :, :]), flat(Em[:, :, :]), mh[:, :], ALU.mult))
                    dve.wait_ge(sig, t + 1)
                    tt(mix[:, t, :], flat(Em[:, :, :]), proj[:, t, 2 * AW + H * DV:2 * AW + 2 * H * DV], ALU.mult).then_inc(tile_ok, 1)
                    dve.wait_ge(tile_ok, t + 1)


def build(nc, A, O):
    with ExitStack() as ctx:
        consts = ctx.enter_context(nc.sbuf_tensor("const_tile", [P, CONST_N], F32))
        C = {k: consts[:, CONST_AT[k]:CONST_AT[k] + w] for k, w in CONST_COLS.items()}
        load(nc, [(consts[:, :], A["consts"])])
        with nc.sbuf_tensor("mix_a", [P, TILES, AW], F32) as mix_a, nc.sbuf_tensor("mix_b", [P, TILES, AW], F32) as mix_b:
            for part, (lo, hi), mixer, mix in ((0, (0, RW), rwkv, mix_a), (1, (RW, INE), mla, mix_b)):
                with nc.sbuf_tensor(f"proj_e{part}", [P, TILES, hi - lo], F32) as proj:
                    with nc.sbuf_tensor(f"xT_e{part}", [P, KD, TILES * P], F32) as xT:
                        load(nc, [(xT[:, :, :], A["xT0"].rearrange("(k p) t -> p k t", p=P))])
                        project(nc, f"in_e{part}", A["w_in_e"][:, lo:hi], hi - lo, xT, proj)
                    mixer(nc, C, A, proj, mix, O)
            with nc.sbuf_tensor("x_e", [P, TILES, D], F32) as x:
                load(nc, [(x[:, :, :], A["x0"].rearrange("(t p) d -> p t d", p=P))])
                half = lambda t, k: (mix_a if k < 4 else mix_b)[:, t, k % 4 * P:(k % 4 + 1) * P]
                out_project(nc, "out_e", C, half, A["w_out_e"], A["ln1_g0"], A["ln1_b0"], x)
                store(nc, [(A["x_mid"].rearrange("(t p) d -> p t d", p=P), x[:, :, :])])
        x = ctx.enter_context(nc.sbuf_tensor("x", [P, TILES, D], F32))
        load(nc, [(x[:, :, :], A["x_mid"].rearrange("(t p) d -> p t d", p=P))])
        peer(nc, 0, C, A, x)
        with nc.sbuf_tensor("mix_o", [P, TILES, D], F32) as mix:
            with nc.sbuf_tensor("proj_o", [P, TILES, INO], F32) as proj:
                with nc.sbuf_tensor("xT_o", [P, KD, TILES * P], F32) as xT:
                    turn(nc, "turn_o", C, x, xT, False)
                    project(nc, "in_o", A["w_in_o"], INO, xT, proj)
                mlstm(nc, C, A, proj, mix, O)
            out_project(nc, "out_o", C, lambda t, k: mix[:, t, k * P:(k + 1) * P], A["w_out_o"], A["ln1_g1"], A["ln1_b1"], x)
        peer(nc, 1, C, A, x)
        store(nc, [(O["y"].rearrange("(t p) d -> p t d", p=P), x[:, :, :]),
                   (O["shift"][0:1, :], A["x0"][SEQ - 1:SEQ, :]),
                   (O["shift"][1:1 + NB, :], A["x0"][SEQ:, :].rearrange("(b s) d -> b s d", s=SEG)[:, NS, :])])


def peer(nc, layer, C, A, x):
    n = str(layer)
    with (nc.sbuf_tensor("xT_p" + n, [P, KD, TOK], F32) as xT, nc.sbuf_tensor("expert" + n, [P, HK], U32) as expert,
          nc.sbuf_tensor("gate" + n, [P, HK], F32) as gate):
        turn(nc, "turn_p" + n, C, x, xT, True)
        with nc.sbuf_tensor("picks" + n, [P, 3, DENSE], F32) as picks:
            peer_select(nc, "select" + n, C, xT, A["wq" + n], A["k1T" + n], A["k2T" + n], A["uT" + n], A["early"], picks, expert[:, :], gate[:, :])
            peer_spread(nc, "spread" + n, C, picks, A["grids"])
        with nc.sbuf_tensor("yT" + n, [P, KD, DENSE], F32) as yT, nc.sbuf_tensor("yrows" + n, [P, D], F32) as y_rows:
            peer_experts(nc, "experts" + n, xT, x[:, GT, :], expert, gate[:, :], A["uT" + n], A["early"], A["v" + n],
                         A["u_rows" + n], A["v_rows" + n], A["grids"], yT, y_rows[:, :])
            peer_norm(nc, "norm" + n, C, yT, y_rows[:, :], A["ln2_g" + n], A["ln2_b" + n], x)


def store(nc, pairs):
    with Stage(nc, f"store{nc.next_id()}") as st:
        sent = st.sem("arrays_stored")
        with nc.Block() as block:
            @block.sync
            def _(sp):
                for dst, src in pairs:
                    sp.dma_start(dst, src).then_inc(sent, 16)
                sp.wait_ge(sent, 16 * len(pairs))


def load(nc, pairs):
    with Stage(nc, f"load{nc.next_id()}") as st:
        here = st.sem("arrays_loaded")
        with nc.Block() as block:
            @block.sync
            def _(sp):
                for dst, src in pairs:
                    sp.dma_start(dst, src).then_inc(here, 16)
                sp.wait_ge(here, 16 * len(pairs))


def layouts(i):
    f = lambda a: np.ascontiguousarray(a)
    pad = np.zeros((NB, SEG, D), np.float32)
    pad[:, 0] = i["state_shift"][0]
    pad[:, 1:1 + NS] = i["x_sample"]
    x0 = np.concatenate([i["x_prompt"][0], pad.reshape(P, D)], 0)
    a = {"x0": x0, "xT0": f(x0.T)}
    for n in ("w_in_e", "mu_e", "w0_e", "w2_e", "a0_e", "a2_e", "g2_e", "kk_e", "ka_e", "lnx_w_e", "lnx_b_e"):
        a[n] = i[n][0]
    a["rk_e"] = i["rk_e"][0].reshape(-1)
    w = np.zeros((NB, PAIRS, 2, HD, 2, HD), np.float32)
    s = i["state_wkv"][0].reshape(NB, PAIRS, 2, HD, HD)
    for g in range(2):
        w[:, :, g, :, g, :] = s[:, :, g].transpose(0, 1, 3, 2)
    a["wkv_s"] = w.reshape(NB, PAIRS, P, P)
    a["w_uq_e"], a["q_norm_e"], a["kv_norm_e"] = i["w_uq_e"][0], i["q_norm_e"][0], i["kv_norm_e"][0]
    a["w_uk_e"], a["w_uv_e"] = i["w_uk_e"][0].reshape(KV, -1), i["w_uv_e"][0].reshape(KV, -1)
    a["w_ukT_e"] = f(i["w_uk_e"][0].transpose(2, 1, 0))
    a["page_table"] = i["page_table"].reshape(1, -1)
    c = i["cache_ckv"][0]
    a["cache_ckv"] = c
    keys = np.concatenate([c, i["cache_kpe"][0]], 2)
    a["keysT"] = f(keys.reshape(-1, PAGE, 3, HD + RP).transpose(0, 3, 2, 1)).reshape(-1, HD + RP, 3 * PAGE)
    a["w_out_e"], a["w_in_o"], a["w_out_o"] = i["w_out_e"][0], i["w_in_o"][0], i["w_out_o"][0]
    for l in range(2):
        n = str(l)
        for k in ("ln1_g", "ln1_b", "ln2_g", "ln2_b"):
            a[k + n] = i[k][l]
        a["wq" + n], a["k1T" + n], a["k2T" + n] = i["peer_wq"][l], f(i["peer_k1"][l].T), f(i["peer_k2"][l].T)
        u = i["peer_u"][l].reshape(NK, NGRP, GI, KD, P)
        a["uT" + n] = f(u.transpose(1, 4, 2, 3, 0)).reshape(NGRP, P, GI * KD * NK)
        a["v" + n] = i["peer_v"][l].reshape(NK, NK * D)
        a["u_rows" + n], a["v_rows" + n] = i["peer_u"][l], i["peer_v"][l]
    a["b_i_o"], a["b_f_o"], a["mh_norm_o"] = i["b_i_o"][0], i["b_f_o"][0], i["mh_norm_o"][0]
    cn = np.concatenate([i["state_mlstm_c"][0], i["state_mlstm_n"][0][:, :, None, :]], 2)
    cn = cn.reshape(NB, PAIRS, 2, DV + 1, HD).transpose(2, 4, 0, 1, 3)
    a["cn_s"] = f(cn).reshape(P, NB, PAIRS, DV + 1)
    a["m_s"] = np.repeat(i["state_mlstm_m"][0], SEG, axis=0)
    a["consts"] = np.concatenate(list(constants().values()), 1)
    return a


OUTPUTS = {"cn_p": (P, PAIRS, DV + 1), "cn_s": (P, NB, PAIRS, DV + 1), "m_p": (P, H), "m_s": (P, H), "y": (TILES * P, D), "shift": (1 + NB, D), "ckv": (TILES * P, KV), "kpe": (TILES * P, RP), "wkv_p": (PAIRS, P, P), "wkv_s": (PAIRS, NB, P, P)}
SCRATCH = {"x_mid": (TILES * P, D), "grids": (NBLK, P, NK, BLK), "early": (QUADS, P, GI * DENSE), "new_rows": (P, KV), "last_rows": (1, SAMP, RW)}


def kernel(**inputs):
    from concourse import bacc
    from concourse.bass_utils import run_bass_kernel_spmd

    given = layouts({k: np.asarray(v) for k, v in inputs.items()})
    nc = bacc.Bacc("TRN2", target_bir_lowering=False, num_devices=1)
    A, O, arrays = {}, {}, {}
    for n, v in given.items():
        arrays["in_" + n] = np.ascontiguousarray(v)
        A[n] = nc.dram_tensor("in_" + n, v.shape, mybir.dt.from_np(v.dtype), kind="ExternalInput").ap()
    for n, shape in SCRATCH.items():
        A[n] = nc.dram_tensor("scratch_" + n, shape, F32, kind="Internal").ap()
    for n, shape in OUTPUTS.items():
        O[n] = nc.dram_tensor("out_" + n, shape, F32, kind="ExternalOutput").ap()
    build(nc, A, O)
    r = run_bass_kernel_spmd(nc, [arrays], core_ids=[0]).results[0]
    got = {n: np.asarray(r["out_" + n]) for n in OUTPUTS}

    def rows(a):
        return a[:SEQ][None], a[SEQ:].reshape(NB, SEG, -1)[:, 1:1 + NS]

    def wkv(a):
        a = a.reshape(PAIRS, -1, 2, HD, 2, HD)
        a = np.stack([a[:, :, g, :, g, :] for g in range(2)], 2)
        return a.transpose(1, 0, 2, 4, 3).reshape(-1, H, HD, HD)[None]

    def cell(a):
        a = a.reshape(2, HD, -1, PAIRS, DV + 1).transpose(2, 3, 0, 4, 1).reshape(-1, H, DV + 1, HD)
        return a[None, :, :, :DV], a[None, :, :, DV]

    y_p, y_s = rows(got["y"])
    ckv_p, ckv_s = rows(got["ckv"])
    kpe_p, kpe_s = rows(got["kpe"])
    c_p, n_p = cell(got["cn_p"])
    c_s, n_s = cell(got["cn_s"])
    out = (y_p, y_s, ckv_p[None], kpe_p[None], ckv_s[None], kpe_s[None],
           got["shift"][None, 0:1], got["shift"][None, 1:], wkv(got["wkv_p"][:, None]), wkv(got["wkv_s"]),
           c_p, c_s, n_p, n_s, got["m_p"][None, 0:1], got["m_s"][None, ::SEG])
    return tuple(np.ascontiguousarray(a) for a in out)
```
